# Optimizing a Trainium2 kernel written in Bass

```python
import jax, jax.numpy as jnp
from jax import lax
import numpy as np

D_MODEL = 1024
BATCH = 1
SEQ = 1024
DEPTH = 1
DEC_BATCH = 8
DEC_SEQ = 1
PAST_LEN = 8192
PAGE_SIZE = 128

MIX_W = D_MODEL // 2
CHUNK = 128
A_GROUPS = 4
CONV_B = 3
POOL_WINDOWS = (2, 4, 8, 16)
POOL_CTX = 15
CONV_D = 31
N_BRANCH = 4
N_GROUPS_MOE = 4
EXPERTS_PER_GROUP = 8
N_EXPERTS = N_GROUPS_MOE * EXPERTS_PER_GROUP
TOP_K = 2
D_EXPERT = D_MODEL // 4
MOE_BLOCK = 128
EPS = 1e-6
D_IN = 2 * MIX_W + 3 * MIX_W + MIX_W + 2 * MIX_W + N_BRANCH * D_MODEL
SPLITS = (MIX_W, 2 * MIX_W, 3 * MIX_W, 4 * MIX_W, 5 * MIX_W, 6 * MIX_W, 7 * MIX_W, 8 * MIX_W)

kernel_name = 'hybrid_gmlp_conv_pool_conformer_hmoe_step'

def _rmsnorm(x, g):
    xf = x.astype(jnp.float32)
    y = xf * lax.rsqrt(jnp.mean(xf * xf, axis=-1, keepdims=True) + EPS)
    return (y * g.astype(jnp.float32)).astype(x.dtype)

def _layernorm(x, g, b):
    xf = x.astype(jnp.float32)
    mu = jnp.mean(xf, axis=-1, keepdims=True)
    xc = xf - mu
    y = xc * lax.rsqrt(jnp.mean(xc * xc, axis=-1, keepdims=True) + EPS)
    return (y * g.astype(jnp.float32) + b.astype(jnp.float32)).astype(x.dtype)

def _dwconv(x_ext, w):
    c = x_ext.shape[-1]
    return lax.conv_general_dilated(x_ext, w[:, None, :].astype(x_ext.dtype), window_strides=(1,), padding='VALID',
                                    dimension_numbers=('NWC', 'WIO', 'NWC'), feature_group_count=c)

def _spatial_gate(u, v, w_s, b_s, clen):
    n, l, c = v.shape
    nc = l // clen
    cg = c // A_GROUPS
    w = (w_s[:, :clen, :clen] * jnp.tril(jnp.ones((clen, clen), w_s.dtype))).astype(v.dtype)
    vg = v.reshape(n, nc, clen, A_GROUPS, cg)
    mixed = jnp.einsum('gts,bnsgc->bntgc', w, vg) + jnp.swapaxes(b_s[:, :clen], 0, 1)[:, :, None].astype(v.dtype)
    return (u * mixed.reshape(n, l, c)).astype(v.dtype)

def _pool_mix(p_ext, pos0, w_pg, scale):
    n, le, c = p_ext.shape
    l = le - POOL_CTX
    ef = p_ext.astype(jnp.float32)
    cs0 = jnp.concatenate([jnp.zeros((n, 1, c), jnp.float32), jnp.cumsum(ef, axis=1)], axis=1)
    pos = pos0 + jnp.arange(l)
    cg = c // len(POOL_WINDOWS)
    means = []
    for gi, w in enumerate(POOL_WINDOWS):
        lo, hi = gi * cg, (gi + 1) * cg
        s = cs0[:, POOL_CTX + 1:, lo:hi] - cs0[:, POOL_CTX + 1 - w:POOL_CTX + 1 - w + l, lo:hi]
        cnt = jnp.minimum(pos + 1, w).astype(jnp.float32)
        means.append(s / cnt[None, :, None])
    pooled = jnp.concatenate(means, axis=-1) - ef[:, POOL_CTX:]
    mixed = jnp.einsum('blgc,gcd->blgd', pooled.reshape(n, l, len(POOL_WINDOWS), cg), w_pg.astype(jnp.float32))
    return (mixed.reshape(n, l, c) * scale.astype(jnp.float32)).astype(p_ext.dtype)

def _mixer(h, st_b, st_pool, st_d, pos0, clen, pr, li):
    n, l, _ = h.shape
    proj = h @ pr['w_in'][li]
    u, v, gb, gc, xin, pin, ga, gg, gates = jnp.split(proj, SPLITS, axis=-1)
    u = jax.nn.gelu(u)
    v = _layernorm(jax.nn.gelu(v), pr['a_ln_g'][li], pr['a_ln_b'][li])
    ya = _spatial_gate(u, v, pr['a_ws'][li], pr['a_bs'][li], clen)
    cx = gc * xin
    cx_ext = jnp.concatenate([st_b.astype(cx.dtype), cx], axis=1)
    yb = gb * _dwconv(cx_ext, pr['conv_b_w'][li])
    p_ext = jnp.concatenate([st_pool.astype(pin.dtype), pin], axis=1)
    yc = _pool_mix(p_ext, pos0, pr['pool_w'][li], pr['pool_scale'][li])
    gl = ga * jax.nn.sigmoid(gg)
    gl_ext = jnp.concatenate([st_d.astype(gl.dtype), gl], axis=1)
    dc = _dwconv(gl_ext, pr['conv_d_w'][li]) + pr['conv_d_b'][li]
    yd = jax.nn.silu(_layernorm(dc, pr['d_ln_g'][li], pr['d_ln_b'][li]))
    ys = jnp.stack([ya, yb, yc, yd], axis=2)
    br = jnp.einsum('blic,icd->blid', ys, pr['w_branch'][li])
    m = jnp.sum(jax.nn.sigmoid(gates).reshape(n, l, N_BRANCH, D_MODEL) * br, axis=2)
    out = m @ pr['w_out'][li]
    return out, (cx_ext[:, -(CONV_B - 1):], p_ext[:, -POOL_CTX:], gl_ext[:, -(CONV_D - 1):], v)

def _hier_moe(h, pr, li):
    t = h.shape[0]
    hf = h.astype(jnp.float32)
    g_logits = hf @ pr['w_rg'][li].astype(jnp.float32) + pr['b_rg'][li].astype(jnp.float32)
    g_prob = jax.nn.softmax(g_logits, axis=-1)
    g_sel = jnp.argmax(g_logits, axis=-1)
    p_g = jnp.take_along_axis(g_prob, g_sel[:, None], axis=1)[:, 0]
    e_logits = (hf @ pr['w_re'][li].astype(jnp.float32) + pr['b_re'][li].astype(jnp.float32)).reshape(t, N_GROUPS_MOE, EXPERTS_PER_GROUP)
    e_sel_logits = jnp.take_along_axis(e_logits, g_sel[:, None, None], axis=1)[:, 0]
    top_p, top_i = lax.top_k(jax.nn.softmax(e_sel_logits, axis=-1), TOP_K)
    weights = p_g[:, None] * top_p / jnp.sum(top_p, axis=-1, keepdims=True)
    expert = g_sel[:, None].astype(jnp.int32) * EXPERTS_PER_GROUP + top_i.astype(jnp.int32)
    flat_e = expert.reshape(-1)
    flat_w = weights.reshape(-1)
    flat_tok = jnp.arange(t * TOP_K, dtype=jnp.int32) // TOP_K
    order = jnp.argsort(flat_e)
    se = flat_e[order]
    counts = jax.ops.segment_sum(jnp.ones_like(flat_e), flat_e, num_segments=N_EXPERTS)
    starts = jnp.cumsum(counts) - counts
    padded = (counts + MOE_BLOCK - 1) // MOE_BLOCK * MOE_BLOCK
    ends = jnp.cumsum(padded)
    pstarts = ends - padded
    dest = pstarts[se] + jnp.arange(t * TOP_K, dtype=jnp.int32) - starts[se]
    n_blocks = -(-(t * TOP_K) // MOE_BLOCK) + N_EXPERTS
    cap = n_blocks * MOE_BLOCK
    slot_tok = jnp.full((cap,), t, jnp.int32).at[dest].set(flat_tok[order])
    slot_w = jnp.zeros((cap,), jnp.float32).at[dest].set(flat_w[order])
    block_e = jnp.clip(jnp.searchsorted(ends, jnp.arange(n_blocks) * MOE_BLOCK, side='right'), 0, N_EXPERTS - 1)
    h_pad = jnp.concatenate([h, jnp.zeros((1, D_MODEL), h.dtype)], axis=0)
    xs = h_pad[slot_tok].reshape(n_blocks, MOE_BLOCK, D_MODEL)
    w_eg, w_eu, w_ed = pr['w_eg'][li], pr['w_eu'][li], pr['w_ed'][li]

    def expert_block(args):
        xb, e = args
        return (jax.nn.silu(xb @ w_eg[e]) * (xb @ w_eu[e])) @ w_ed[e]

    ys = lax.map(expert_block, (xs, block_e)).reshape(cap, D_MODEL)
    y = jax.ops.segment_sum(ys * slot_w[:, None].astype(ys.dtype), slot_tok, num_segments=t + 1)[:t]
    return y.astype(h.dtype)

def _trunk(x, c, st_b, st_pool, st_d, pos0, clen, pr):
    nb, npool, nd, nv = [], [], [], []
    for li in range(DEPTH):
        mod = (c @ pr['w_mod'][li] + pr['b_mod'][li])[:, None, :]
        sh1, sc1, g1, sh2, sc2, g2 = jnp.split(mod, 6, axis=-1)
        h = _rmsnorm(x, pr['norm1_g'][li]) * (1 + sc1) + sh1
        mo, (sb, sp, sd, v) = _mixer(h, st_b[li], st_pool[li], st_d[li], pos0, clen, pr, li)
        x = x + g1 * mo
        h2 = _rmsnorm(x, pr['norm2_g'][li]) * (1 + sc2) + sh2
        n, l, _ = x.shape
        x = x + g2 * _hier_moe(h2.reshape(n * l, D_MODEL), pr, li).reshape(n, l, D_MODEL)
        nb.append(sb)
        npool.append(sp)
        nd.append(sd)
        nv.append(v)
    y = _rmsnorm(x, pr['final_g'])
    return y, jnp.stack(nb), jnp.stack(npool), jnp.stack(nd), jnp.stack(nv)

def setup_inputs(seed: int = 0) -> dict:
    key = jax.random.key(seed)
    ks = jax.random.split(key, 40)
    f32 = jnp.float32
    nrm = lambda k, s, sc: jax.random.normal(k, s, f32) * sc
    G = len(POOL_WINDOWS)
    return {
        'x_prompt': nrm(ks[0], (BATCH, SEQ, D_MODEL), 1.0),
        'x_sample': nrm(ks[1], (DEC_BATCH, DEC_SEQ, D_MODEL), 1.0),
        'state_conv_b': nrm(ks[2], (DEPTH, DEC_BATCH, CONV_B - 1, MIX_W), 1.0),
        'state_pool': nrm(ks[3], (DEPTH, DEC_BATCH, POOL_CTX, MIX_W), 1.0),
        'state_conv_d': nrm(ks[4], (DEPTH, DEC_BATCH, CONV_D - 1, MIX_W), 0.5),
        'c_prompt': nrm(ks[5], (BATCH, D_MODEL), 1.0),
        'c_sample': nrm(ks[6], (DEC_BATCH, D_MODEL), 1.0),
        'w_mod': nrm(ks[7], (DEPTH, D_MODEL, 6 * D_MODEL), 0.5 * D_MODEL ** -0.5),
        'b_mod': nrm(ks[8], (DEPTH, 6 * D_MODEL), 0.02),
        'norm1_g': 1.0 + nrm(ks[9], (DEPTH, D_MODEL), 0.1),
        'norm2_g': 1.0 + nrm(ks[10], (DEPTH, D_MODEL), 0.1),
        'w_in': nrm(ks[11], (DEPTH, D_MODEL, D_IN), D_MODEL ** -0.5),
        'a_ln_g': 1.0 + nrm(ks[12], (DEPTH, MIX_W), 0.1),
        'a_ln_b': nrm(ks[13], (DEPTH, MIX_W), 0.02),
        'a_ws': nrm(ks[14], (DEPTH, A_GROUPS, CHUNK, CHUNK), CHUNK ** -0.5),
        'a_bs': 1.0 + nrm(ks[15], (DEPTH, A_GROUPS, CHUNK), 0.1),
        'conv_b_w': nrm(ks[16], (DEPTH, CONV_B, MIX_W), CONV_B ** -0.5),
        'pool_w': nrm(ks[17], (DEPTH, G, MIX_W // G, MIX_W // G), (MIX_W // G) ** -0.5),
        'pool_scale': 1.0 + nrm(ks[18], (DEPTH, MIX_W), 0.1),
        'conv_d_w': nrm(ks[19], (DEPTH, CONV_D, MIX_W), CONV_D ** -0.5),
        'conv_d_b': nrm(ks[20], (DEPTH, MIX_W), 0.02),
        'd_ln_g': 1.0 + nrm(ks[21], (DEPTH, MIX_W), 0.1),
        'd_ln_b': nrm(ks[22], (DEPTH, MIX_W), 0.02),
        'w_branch': nrm(ks[23], (DEPTH, N_BRANCH, MIX_W, D_MODEL), MIX_W ** -0.5),
        'w_out': nrm(ks[24], (DEPTH, D_MODEL, D_MODEL), D_MODEL ** -0.5),
        'w_rg': nrm(ks[25], (DEPTH, D_MODEL, N_GROUPS_MOE), D_MODEL ** -0.5),
        'b_rg': nrm(ks[26], (DEPTH, N_GROUPS_MOE), 0.01),
        'w_re': nrm(ks[27], (DEPTH, D_MODEL, N_EXPERTS), D_MODEL ** -0.5),
        'b_re': nrm(ks[28], (DEPTH, N_EXPERTS), 0.01),
        'w_eg': nrm(ks[29], (DEPTH, N_EXPERTS, D_MODEL, D_EXPERT), D_MODEL ** -0.5),
        'w_eu': nrm(ks[30], (DEPTH, N_EXPERTS, D_MODEL, D_EXPERT), D_MODEL ** -0.5),
        'w_ed': nrm(ks[31], (DEPTH, N_EXPERTS, D_EXPERT, D_MODEL), D_EXPERT ** -0.5),
        'final_g': 1.0 + nrm(ks[32], (D_MODEL,), 0.1),
    }

def reference(x_prompt, x_sample, state_conv_b, state_pool, state_conv_d, c_prompt, c_sample,
              w_mod, b_mod, norm1_g, norm2_g, w_in, a_ln_g, a_ln_b, a_ws, a_bs, conv_b_w,
              pool_w, pool_scale, conv_d_w, conv_d_b, d_ln_g, d_ln_b, w_branch, w_out,
              w_rg, b_rg, w_re, b_re, w_eg, w_eu, w_ed, final_g):
    pr = {'w_mod': w_mod, 'b_mod': b_mod, 'norm1_g': norm1_g, 'norm2_g': norm2_g, 'w_in': w_in,
          'a_ln_g': a_ln_g, 'a_ln_b': a_ln_b, 'a_ws': a_ws, 'a_bs': a_bs, 'conv_b_w': conv_b_w,
          'pool_w': pool_w, 'pool_scale': pool_scale, 'conv_d_w': conv_d_w, 'conv_d_b': conv_d_b,
          'd_ln_g': d_ln_g, 'd_ln_b': d_ln_b, 'w_branch': w_branch, 'w_out': w_out,
          'w_rg': w_rg, 'b_rg': b_rg, 'w_re': w_re, 'b_re': b_re,
          'w_eg': w_eg, 'w_eu': w_eu, 'w_ed': w_ed, 'final_g': final_g}
    dt = x_prompt.dtype
    z_b = jnp.zeros((DEPTH, BATCH, CONV_B - 1, MIX_W), dt)
    z_p = jnp.zeros((DEPTH, BATCH, POOL_CTX, MIX_W), dt)
    z_d = jnp.zeros((DEPTH, BATCH, CONV_D - 1, MIX_W), dt)
    y_prompt, nb_p, np_p, nd_p, _ = _trunk(x_prompt, c_prompt, z_b, z_p, z_d, 0, CHUNK, pr)
    y_sample, nb_s, np_s, nd_s, nv_s = _trunk(x_sample, c_sample, state_conv_b, state_pool, state_conv_d,
                                              PAST_LEN, min(DEC_SEQ, CHUNK), pr)
    return (y_prompt, y_sample, nb_p, np_p, nd_p, nb_s, np_s, nd_s, nv_s)


_drawn_inputs = setup_inputs


def setup_inputs(seed=0):
    import zlib

    import numpy as np

    out = dict(_drawn_inputs(seed))
    spreads = {}
    factors = {'a_ln_b': 2.889, 'conv_d_b': 4.102, 'd_ln_b': 7.86, 'b_rg': 21.929, 'b_re': 15.821}
    for name, (base, spread) in spreads.items():
        noise = np.random.default_rng([zlib.crc32(name.encode()), seed]).standard_normal(out[name].shape)
        drawn = base * np.exp(spread * noise) if base else spread * noise
        out[name] = __import__('jax').numpy.asarray(drawn.astype(out[name].dtype))
    for name, factor in factors.items():
        out[name] = (out[name] * factor).astype(out[name].dtype)
    return out
```

```python
from contextlib import ExitStack

import numpy as np

import concourse.bass as bass
from concourse import mybir

F32 = mybir.dt.float32
F32R = mybir.dt.float32r
I32 = mybir.dt.int32
U32 = mybir.dt.uint32
ALU = mybir.AluOpType
ACT = mybir.ActivationFunctionType
AXX = mybir.AxisListType.X

P = 128
D = 1024
KD = D // P
LP = 1024
NS = 8
T = LP + NS
NT = 3
TT = T // NT
W = 512
KW = W // P
NV = 1 + NS
CD = 31
PC = 15
EPS = 1e-6
TILES = LP // P + 1
NE = 32
NG = 4
FE = 256
BLOCKS = 50
MIN_BLOCKS = 18
NPAIR = 24
GUW = KD * 2 * FE
EW = GUW + 2 * D
GLW = CD - 1 + T
SW = T + 32

MIX_PAIRS = {"D": 4, "A": 2, "B": 6, "C": 2}
N_GROUPS = 2 * (sum(MIX_PAIRS.values()) + 4 * KD)
Q0, q = {}, 0
for name_, pairs_ in (("D", 4), ("A", 2), ("gA", 8), ("B", 6), ("gB", 8), ("C", 2), ("gC", 8), ("gD", 8)):
    Q0[name_] = q
    q += 2 * pairs_


def columns():
    at, where = 0, {}
    for name, n in (("ident", P), ("ones", P), ("cT", KD * NV), ("bmod", 48), ("n1g", KD), ("n2g", KD),
                    ("cbw", 3 * KW), ("cdw", KW * CD), ("cdb", KW), ("dlg", KW), ("dlb", KW), ("pscale", KW),
                    ("ws00", KW), ("bs00", KW), ("st_b", KW * NS * 2), ("poolw", KW * P), ("inv", KW * PC),
                    ("modT", 48 * NV), ("psums", KW * NS), ("dsums", KW * NS), ("stats", 16),
                    ("tail_b", KW * 10), ("tail_p", KW * 23), ("smp", 2 * NS)):
        where[name] = (at, at + n)
        at += n
    return where, at


COLS, SMALL = columns()
LOADED = COLS["modT"][0]


def early_columns():
    at, where = 0, {}
    for name, n in (("wv", KD * W), ("st_d", KW * NS * (CD - 1)), ("st_p", KW * NS * PC), ("alg", W),
                    ("alb", W), ("aws", KW * P), ("abs", KW * P), ("vs", W)):
        where[name] = (at, at + n)
        at += n
    return where, at


ECOLS, EARLY = early_columns()
EARLY_LOADED = ECOLS["vs"][0]
R3 = dict(ident=(0, P), ones=(P, 2 * P), tri=(2 * P, 3 * P), iota=(3 * P, 3 * P + NE),
          thr=(416, 425), biota=(425, 425 + BLOCKS), pair=(475, 499), br=(499, 535), wr=(535, 535 + KD * 36))
R3W = 535 + KD * 36


class Steps:

    def __init__(self, eng, sem):
        self.eng, self.sem, self.n = eng, sem, 0

    def link(self, ins):
        ins.then_inc(self.sem, 1)
        self.n = self.n + 1
        self.eng.wait_ge(self.sem, self.n)

    def loop(self, i, first, per):
        self.base, self.first, self.per = self.n, first, per
        self.n = (i - first) * per + self.base

    def done(self, turns):
        self.n = self.base + turns * self.per


def evacuated(q):
    n = (6 if q % 2 == 0 else 4) + q // 2
    if q >= Q0["C"] + 2:
        n += min(2, (q - Q0["C"]) // 2)
    if q >= Q0["gD"]:
        n += 1
    return n


def build(nc, A, O):
    ctx = ExitStack()
    with ctx:
        def sem(name):
            return ctx.enter_context(nc.semaphore(name))

        sm = ctx.enter_context(nc.sbuf_tensor("sm", [P, SMALL], F32))
        with ExitStack() as ch:
            h_hi = ch.enter_context(nc.sbuf_tensor("h_hi", [P, KD, T], F32R))
            h_lo = ch.enter_context(nc.sbuf_tensor("h_lo", [P, KD, T], F32R))
            with ExitStack() as c1:
                y_hi = c1.enter_context(nc.sbuf_tensor("y_hi", [P, KW * T], F32R))
                y_lo = c1.enter_context(nc.sbuf_tensor("y_lo", [P, KW * T], F32R))
                raw = c1.enter_context(nc.sbuf_tensor("raw", [P, 2, KD * P], F32))
                w_hi = c1.enter_context(nc.sbuf_tensor("w_hi", [P, 2, KD, P], F32R))
                w_lo = c1.enter_context(nc.sbuf_tensor("w_lo", [P, 2, KD, P], F32R))
                G = c1.enter_context(nc.sbuf_tensor("G", [P, KW * GLW + KW * T], F32))
                S = c1.enter_context(nc.sbuf_tensor("S", [P, 3 * SW], F32))
                zeros = c1.enter_context(nc.sbuf_tensor("zeros", [P, 512], F32))
                m = c1.enter_context(nc.sbuf_tensor("m", [P, KD * T], F32))
            with ExitStack() as c2:
                wo_hi = c2.enter_context(nc.sbuf_tensor("wo_hi", [P, KD, D], F32R))
                wo_lo = c2.enter_context(nc.sbuf_tensor("wo_lo", [P, KD, D], F32R))
                wo_raw = c2.enter_context(nc.sbuf_tensor("wo_raw", [P, 2, D], F32))
                xt = c2.enter_context(nc.sbuf_tensor("xt", [P, 2, D], F32))
                h2 = c2.enter_context(nc.sbuf_tensor("h2", [P, 2, D], F32))
                h2T = c2.enter_context(nc.sbuf_tensor("h2T", [P, KD, P], F32))
                sq = c2.enter_context(nc.sbuf_tensor("sq", [P, D], F32))
                rows = c2.enter_context(nc.sbuf_tensor("rows", [P, 3, D], F32))
                rows_s = c2.enter_context(nc.sbuf_tensor("rows_s", [P, 3, D], F32))
                r3 = c2.enter_context(nc.sbuf_tensor("r3", [P, R3W], F32))
                MK = c2.enter_context(nc.sbuf_tensor("MK", [P, 3, TILES * NE], F32))
                rt = c2.enter_context(nc.sbuf_tensor("rt", [P, 160], F32))
                ri = c2.enter_context(nc.sbuf_tensor("ri", [P, 16], U32))
                wts = c2.enter_context(nc.sbuf_tensor("wts", [P, 2, TILES], F32))
                slots = c2.enter_context(nc.sbuf_tensor("slots", [P, 2 * TILES], I32))
                tokid = c2.enter_context(nc.sbuf_tensor("tok_ids", [P, TILES], I32))
                zero_ids = c2.enter_context(nc.sbuf_tensor("zero_ids", [P, BLOCKS], I32))
                table = c2.enter_context(nc.sbuf_tensor("table", [P, BLOCKS], I32))
                block_e = c2.enter_context(nc.sbuf_tensor("block_e", [P, BLOCKS + 2], I32))
                cmp_ = c2.enter_context(nc.sbuf_tensor("cmp", [P, BLOCKS * NE], F32))
        with ExitStack() as c3:
            we = c3.enter_context(nc.sbuf_tensor("we", [P, 2, EW], F32))
            xg = c3.enter_context(nc.sbuf_tensor("xg", [P, 2, D], F32))
            xgT = c3.enter_context(nc.sbuf_tensor("xgT", [P, 2, KD, P], F32))
            idx = c3.enter_context(nc.sbuf_tensor("idx", [P, 2], I32))
            sg = c3.enter_context(nc.sbuf_tensor("sg", [P, FE], F32))
            hm = c3.enter_context(nc.sbuf_tensor("hm", [P, FE], F32))
            hmT = c3.enter_context(nc.sbuf_tensor("hmT", [P, 2, P], F32))
            yb = c3.enter_context(nc.sbuf_tensor("yb", [P, 2, D], F32))
            g2r = c3.enter_context(nc.sbuf_tensor("g2r", [P, 2, D], F32))
            fg = c3.enter_context(nc.sbuf_tensor("fg", [P, D], F32))
            y1 = c3.enter_context(nc.sbuf_tensor("y1", [P, 2, D], F32))
            y2 = c3.enter_context(nc.sbuf_tensor("y2", [P, 2, D], F32))
            x1 = c3.enter_context(nc.sbuf_tensor("x1", [P, 2, D], F32))
            cs = c3.enter_context(nc.sbuf_tensor("cs", [P, 8], F32))
        ps = ctx.enter_context(nc.psum_tensor("ps", [P, 8, 512], F32))

        def c(name):
            a, b = COLS[name]
            return sm[:, a:b]

        def e(name):
            a, b = ECOLS[name]
            return m[:, a:b]

        ident, ones = c("ident"), c("ones")
        cT = c("cT").rearrange("p (k v) -> p k v", k=KD)
        modT = c("modT").rearrange("p (n v) -> p n v", n=48)
        xT = G[:, 0:KD * T].rearrange("p (k t) -> p k t", k=KD)
        gl = G[:, 0:KW * GLW].rearrange("p (c t) -> p c t", c=KW)
        dc = G[:, KW * GLW:].rearrange("p (c t) -> p c t", c=KW)
        vn = G[:, KW * GLW:KW * GLW + 8 * W].rearrange("p (n c) -> p n c", n=8)
        mm = m[:, :].rearrange("p (k t) -> p k t", k=KD)
        yh = y_hi[:, :].rearrange("p (c t) -> p c t", c=KW)
        yl = y_lo[:, :].rearrange("p (c t) -> p c t", c=KW)
        yh3 = y_hi[:, :].rearrange("p (c a t) -> p c a t", c=KW, a=NT)
        yl3 = y_lo[:, :].rearrange("p (c a t) -> p c a t", c=KW, a=NT)
        h3h = h_hi[:, :, :].rearrange("p k (a t) -> p k a t", a=NT)
        h3l = h_lo[:, :, :].rearrange("p k (a t) -> p k a t", a=NT)
        wvh = y_hi[:, 0:KD * W].rearrange("p (k n) -> p k n", k=KD)
        wvl = y_lo[:, 0:KD * W].rearrange("p (k n) -> p k n", k=KD)
        slab = [raw[:, :, :].rearrange("p a (k n) -> p (a k n)", k=KD).rearrange("p (k n) -> p k n", k=KD),
                S[:, SW:SW + 2048].rearrange("p (k n) -> p k n", k=KD)]
        st = c("stats")
        cbw = c("cbw").rearrange("p (l c) -> p l c", l=3)
        cdw = c("cdw").rearrange("p (c l) -> p c l", c=KW)
        st_b = c("st_b").rearrange("p (c b l) -> p c b l", c=KW, b=NS)
        st_d = e("st_d").rearrange("p (c b l) -> p c b l", c=KW, b=NS)
        st_p = e("st_p").rearrange("p (c b l) -> p c b l", c=KW, b=NS)
        psums = c("psums").rearrange("p (c b) -> p c b", c=KW)
        dsums = c("dsums").rearrange("p (c b) -> p c b", c=KW)
        poolw = c("poolw").rearrange("p (c n) -> p c n", c=KW)
        inv = c("inv").rearrange("p (c n) -> p c n", c=KW)
        aws = e("aws").rearrange("p (g t) -> p g t", g=KW)
        abs_ = e("abs").rearrange("p (g t) -> p g t", g=KW)
        tail_b = c("tail_b").rearrange("p (c n) -> p c n", c=KW)
        tail_p = c("tail_p").rearrange("p (c n) -> p c n", c=KW)
        smp = c("smp").rearrange("p (a n) -> p a n", a=2)

        def sbf(n, off=0, width=T):
            return S[:, n * SW + off:n * SW + off + width]

        def three(ap):
            return ap.rearrange("p (a t) -> p a t", a=NT)

        def pset(s):
            return ps[:, 3 * s:3 * s + 3, 0:TT]

        small_in = sem("small_in")
        v_start = sem("v_start")
        idx_in = [sem("idx_in0"), sem("idx_in1")]
        zeros_ready, y_zero = sem("zeros_ready"), sem("y_zero")
        x_in = sem("x_in")
        early_in = sem("early_in")
        slab_in = [sem("slab_in0"), sem("slab_in1")]
        slab_used = sem("slab_used")
        mod_ready = sem("mod_ready")
        sq_ready = sem("sq_ready")
        sq_used = sem("sq_used")
        rstd_in = sem("rstd_in")
        rstd_ready = sem("rstd_ready")
        h_f32 = sem("h_f32")
        h_hi_done = sem("h_hi_done")
        h_lo_done = sem("h_lo_done")
        wv_hi = sem("wv_hi")
        wv_lo = sem("wv_lo")
        v_prod = sem("v_prod")
        v_act = sem("v_act")
        v_dve = sem("v_dve")
        v_done = sem("v_done")
        masked = sem("masked")
        gap_zero = sem("gap_zero")
        raw_in = sem("raw_in")
        hi_done = sem("hi_done")
        lo_done = sem("lo_done")
        grp = sem("grp")
        evac = [sem("evac0"), sem("evac1")]
        gate_prod = sem("gate_prod")
        gate_read = sem("gate_read")
        y_done = sem("y_done")
        y_f32 = sem("y_f32")
        pooled = sem("pooled")
        pool_prod = sem("pool_prod")
        ln_sq = sem("ln_sq")
        ln_prod = sem("ln_prod")
        ln_mean = sem("ln_mean")
        ln_in = sem("ln_in")
        ln_rstd = sem("ln_rstd")
        ln_y = sem("ln_y")
        ln_norm = sem("ln_norm")
        ln_lo = sem("ln_lo")
        dve_step = sem("dve_step")
        stored = sem("stored")
        tails_b = sem("tails_b")
        tails_p = sem("tails_p")
        m_ready = sem("m_ready")
        m_hi_done, m_lo_done = sem("m_hi_done"), sem("m_lo_done")
        wo_in = [sem("wo_in0"), sem("wo_in1")]
        wo_hi_done, wo_lo_done = sem("wo_hi_done"), sem("wo_lo_done")
        r3_in = sem("r3_in")
        row_prod, row_done = sem("row_prod"), sem("row_done")
        xt_in = [sem("xt_in0"), sem("xt_in1")]
        o_prod = sem("o_prod")
        o_read = sem("o_read")
        x1_done = sem("x1_done")
        x1_out = [sem("x1_out0"), sem("x1_out1")]
        x1_sq = sem("x1_sq")
        x1_var = sem("x1_var")
        x1_rstd = sem("x1_rstd")
        h2_done = sem("h2_done")
        h2_out = [sem("h2_out0"), sem("h2_out1")]
        h2_turned = sem("h2_turned")
        h2T_done = sem("h2T_done")
        logit_prod = sem("logit_prod")
        logit_read = sem("logit_read")
        gexp_in, gexp_done = sem("gexp_in"), sem("gexp_done")
        eexp_in, eexp_done = sem("eexp_in"), sem("eexp_done")
        mask_done = sem("mask_done")
        rank_prod = sem("rank_prod")
        slots_done = sem("slots_done")
        table_zero = sem("table_zero")
        ids_done = sem("ids_done")
        table_out = sem("table_out")
        table_in = sem("table_in")
        idx_done = sem("idx_done")
        xg_in = [sem("xg_in0"), sem("xg_in1")]
        wd_in = [sem("wd_in0"), sem("wd_in1")]
        we_in = [sem("we_in0"), sem("we_in1")]
        turned, xgT_done, gu_prod, silu_done, hm_done = (sem(n) for n in ("turned", "xgT_done", "gu_prod", "silu_done", "hm_done"))
        hm_turned, hmT_done, y_prod, y_copied = (sem(n) for n in ("hm_turned", "hmT_done", "y_prod", "y_copied"))
        y_out = [sem("y_out0"), sem("y_out1")]
        gathers = sem("gathers")
        fg_in = sem("fg_in")
        g2_prod, g2_done = sem("g2_prod"), sem("g2_done")
        y1_in = [sem("y1_in0"), sem("y1_in1")]
        y2_in = [sem("y2_in0"), sem("y2_in1")]
        x1_in = [sem("x1_in0"), sem("x1_in1")]
        c_sq_in, c_sq = sem("c_sq_in"), sem("c_sq")
        c_var, c_rstd = sem("c_var"), sem("c_rstd")
        c_done = sem("c_done")
        out_st = [sem("out_st0"), sem("out_st1")]

        x1d = nc.dram_tensor("x1_scratch", (T, D), F32).ap()
        h2d = nc.dram_tensor("h2_scratch", (T, D), F32).ap()
        tabd = nc.dram_tensor("table_scratch", (BLOCKS * P, 1), I32).ap()
        yd = nc.dram_tensor("y_scratch", (BLOCKS * P, D), F32).ap()

        def tile_rows(t):
            return (t * P, P) if t < TILES - 1 else (LP, NS)

        def r(name):
            a, b = R3[name] if name in R3 else None
            return r3[:, a:b]

        def send(sp, t):
            at, n = tile_rows(t)
            sp.wait_ge(c_done, t + 1)
            sp.dma_start(O["y"][at:at + n, :], x1[0:n, t % 2, :]).then_inc(out_st[t % 2], 16)

        def broadcast_rows(pe, j, first):
            if 0 < j < 3:
                pe.wait_ge(row_done, 2 * j)
            for v in range(2):
                for k in range(KD):
                    vec = modT[:, first + k, 0:1].to_broadcast([P, P]) if v == 0 else modT[:, first + k, 1:NV]
                    mmi = pe.matmul(ps[0:(P if v == 0 else NS), 2 * v + k // 4, (k % 4) * P:(k % 4 + 1) * P],
                                    vec, ident, start=True, stop=True)
                mmi.then_inc(g2_prod if j == 3 else row_prod, 1)

        def pooled_in(ch):
            return 2 if ch % 2 == 0 else 1

        block = ctx.enter_context(nc.Block())

        @block.sync
        def _(sp):
            sp.dma_start(sm[:, 0:LOADED], A["small"]).then_inc(small_in, 16)
            sp.dma_start(xT, A["xT"]).then_inc(x_in, 16)
            sp.dma_start(m[:, 0:EARLY_LOADED], A["early"]).then_inc(early_in, 16)

            def load_slab(i, s):
                sp.dma_start(slab[s], A["w_mod"][bass.ds(2 * i + s, 1)].rearrange("o p k n -> (o p) k n")
                             ).then_inc(slab_in[s], 16)

            for s in range(2):
                load_slab(0, s)
            with sp.Fori(1, 12) as i:
                for s in range(2):
                    sp.wait_ge(slab_used, 2 * i + s - 1)
                    load_slab(i, s)
            sp.wait_ge(zeros_ready, 1)
            with sp.Fori(MIN_BLOCKS, BLOCKS) as b:
                for a in range(2):
                    sp.dma_start(yd[bass.ds(b * P, P), a * 512:(a + 1) * 512], zeros[:, :]).then_inc(y_zero, 16)
            sp.dma_start(O["keep_b"], A["state_b"][:, 1:2, :]).then_inc(stored, 16)
            sp.dma_start(O["keep_p"], A["state_p"][:, 1:PC, :]).then_inc(stored, 16)
            sp.dma_start(O["keep_d"], A["state_d"][:, 1:CD - 1, :]).then_inc(stored, 16)

            rawf = raw[:, :, :].rearrange("p a n -> p (a n)")
            pair, gpair = 0, 0
            for name in ("D", "A", "gA", "B", "gB", "C", "gC", "gD"):
                n = MIX_PAIRS.get(name, KD)
                src, at = (A["w_mix"], pair) if name in MIX_PAIRS else (A["w_gate"], gpair)
                q0 = Q0[name]
                width = src.shape[2]
                first = 0
                if name == "D":
                    sp.wait_ge(slab_used, 24)
                    sp.dma_start(rawf, src[0]).then_inc(raw_in, 16)
                    first = 1
                with sp.Fori(first, n) as i:
                    sp.wait_ge(hi_done, q0 + 2 * i)
                    sp.wait_ge(lo_done, q0 + 2 * i)
                    sp.dma_start(rawf[:, 0:width], src[bass.ds(at + i, 1)].rearrange("o p n -> (o p) n")
                                 ).then_inc(raw_in, 16)
                if name in MIX_PAIRS:
                    pair += n
                else:
                    gpair += n
                if name == "D":
                    sp.wait_ge(v_done, TILES)
                    sp.dma_start(O["v_s"], e("vs")[0:NS, :]).then_inc(stored, 16)
                if name == "gA":
                    sp.wait_ge(evac[0], evacuated(8))
                    sp.dma_start(O["tail_d"], gl[:, :, LP:LP + CD - 1 + NS]).then_inc(stored, 16)
            sp.wait_ge(tails_b, 1)
            sp.dma_start(O["tail_b"], tail_b).then_inc(stored, 16)
            sp.wait_ge(tails_p, 1)
            sp.dma_start(O["tail_p"], tail_p).then_inc(stored, 16)

            sp.wait_ge(evac[1], evacuated(N_GROUPS - 1) + 1)
            sp.wait_ge(grp, N_GROUPS)
            sp.wait_ge(stored, 16 * 7)

            def load_wo(i, s):
                sp.dma_start(wo_raw[:, s, :], A["w_out"][:, bass.ds(2 * i + s, 1), :].rearrange("p o n -> p (o n)")
                             ).then_inc(wo_in[s], 16)

            def load_x(t, s):
                at, n = t * P, P
                sp.dma_start(xt[:, s, :], A["x_tok"][bass.ds(at, n), :]).then_inc(xt_in[s], 16)

            for s in range(2):
                load_wo(0, s)
            with sp.Fori(1, KD // 2) as i:
                for s in range(2):
                    sp.wait_ge(wo_hi_done, 2 * i + s - 1)
                    sp.wait_ge(wo_lo_done, 2 * i + s - 1)
                    load_wo(i, s)
            load_x(0, 0)
            load_x(1, 1)
            sp.wait_ge(m_lo_done, KD)
            sp.wait_ge(m_hi_done, KD)
            sp.dma_start(r3[:, :], A["routing"]).then_inc(r3_in, 16)
            sp.dma_start(tokid[:, :], A["tokid"]).then_inc(r3_in, 16)
            sp.wait_ge(table_zero, 1)
            sp.dma_start(tabd.rearrange("(p b) o -> p (b o)", p=P), zero_ids[:, :]).then_inc(table_out, 16)
            for t in range(TILES):
                at, n = tile_rows(t)
                sp.wait_ge(x1_done, t + 1)
                sp.dma_start(x1d[at:at + n, :], xt[0:n, t % 2, :]).then_inc(x1_out[t % 2], 16)
                sp.wait_ge(h2_done, t + 1)
                sp.dma_start(h2d[at:at + n, :], h2[0:n, t % 2, :]).then_inc(h2_out[t % 2], 16)
                if t + 2 < TILES:
                    sp.wait_ge(x1_out[t % 2], 16 * (t // 2 + 1))
                    n2 = tile_rows(t + 2)[1]
                    sp.dma_start(xt[0:n2, t % 2, :], A["x_tok"][(t + 2) * P:(t + 2) * P + n2, :]
                                 ).then_inc(xt_in[t % 2], 16)

            sp.wait_ge(slots_done, 1)
            sp.wait_ge(rank_prod, 1)
            sp.wait_ge(x1_out[0], 16 * 5)
            sp.wait_ge(x1_out[1], 16 * 4)
            sp.wait_ge(h2_out[0], 16 * 5)
            sp.wait_ge(h2_out[1], 16 * 4)
            rest = sp.value_load(block_e[0:1, BLOCKS:BLOCKS + 1], min_val=0, max_val=NPAIR - 1)

            def load_experts(i, s, wait):
                ex = sp.value_load(block_e[0:1, bass.ds(2 * i + s, 1)], min_val=0, max_val=NE - 1)
                if wait:
                    sp.wait_ge(gu_prod, 2 * i + s - 1)
                sp.dma_start(we[:, s, 0:GUW], A["w_exp"][bass.ds(ex, 1), :, 0:GUW].rearrange("o p n -> (o p) n")
                             ).then_inc(we_in[s], 16)
                if wait:
                    sp.wait_ge(y_prod, 2 * i + s - 1)
                sp.dma_start(we[:, s, GUW:], A["w_exp"][bass.ds(ex, 1), :, GUW:].rearrange("o p n -> (o p) n")
                             ).then_inc(wd_in[s], 16)

            for s in range(2):
                load_experts(0, s, False)
            with sp.Fori(1, NPAIR) as i:
                with sp.If(i < rest + 1):
                    for s in range(2):
                        load_experts(i, s, True)
            sp.dma_start(fg[:, :], A["final_g"]).then_inc(fg_in, 16)
            for t in range(TILES):
                at, n = tile_rows(t)
                if t >= 2:
                    sp.wait_ge(out_st[t % 2], 16 * (t // 2))
                sp.dma_start(x1[0:n, t % 2, :], x1d[at:at + n, :]).then_inc(x1_in[t % 2], 16)
                if t >= 1:
                    send(sp, t - 1)
            send(sp, TILES - 1)
            sp.wait_ge(out_st[0], 16 * 5)
            sp.wait_ge(out_st[1], 16 * 4)
            sp.wait_ge(stored, 16 * 7)

        @block.tensor
        def _(pe):
            pe.wait_ge(small_in, 16)
            def mod_slab(i, s):
                pe.wait_ge(slab_in[s], 16 * (i + 1))
                for cc in range(2):
                    for k in range(KD):
                        mmi = pe.matmul(ps[:, 6, bass.ds(((2 * i + s) * 2 + cc) * NV, NV)],
                                        slab[s][:, k, cc * P:(cc + 1) * P], cT[:, k, :],
                                        start=(k == 0), stop=(k == KD - 1))
                mmi.then_inc(slab_used, 1)

            with pe.Fori(0, 12) as i:
                for s in range(2):
                    mod_slab(i, s)
            for k in range(KD):
                pe.wait_ge(sq_ready, k + 1)
                for a in range(NT):
                    mmi = pe.matmul(ps[:, a, 0:TT], ones, sbf(0, a * TT, TT), start=(k == 0), stop=(k == KD - 1))
                mmi.then_inc(sq_used, 1)
            pe.wait_ge(h_lo_done, KD)
            pe.wait_ge(h_hi_done, KD)
            pe.wait_ge(wv_lo, 1)
            for t in range(TILES):
                at, n = tile_rows(t)
                if t == 0:
                    pe.wait_ge(evac[0], 1)
                elif t > 1:
                    pe.wait_ge(evac[t % 2], (1 if t % 2 == 0 else 0) + t // 2)
                for k in range(KD):
                    for x, (l, w) in enumerate(((h_hi, wvh), (h_hi, wvl), (h_lo, wvh))):
                        mmi = pe.matmul(ps[0:n, 3 * (t % 2), :], l[:, k, at:at + n], w[:, k, :],
                                        start=(k == 0 and x == 0), stop=(k == KD - 1 and x == 2))
                mmi.then_inc(v_prod, 1)

            def group(q, s, before, rh, rl, nk):
                pe.wait_ge(hi_done, q + 1)
                pe.wait_ge(lo_done, q + 1)
                pe.wait_ge(evac[s], before)
                for k in range(nk):
                    for x, (w, rr) in enumerate(((w_hi, rh), (w_hi, rl), (w_lo, rh))):
                        for a in range(NT):
                            mmi = pe.matmul(ps[:, 3 * s + a, 0:TT], w[:, s, k, :], rr[:, k, a, :],
                                            start=(k == 0 and x == 0), stop=(k == nk - 1 and x == 2))
                mmi.then_inc(grp, 1)

            def pairs_of(name):
                q0 = Q0[name]
                gates = name[0] == "g"
                if gates:
                    pe.wait_ge(y_done, KW * (1 + "ABCD".index(name[1])))
                with pe.Fori(0, MIX_PAIRS.get(name, KD)) as i:
                    group(q0 + 2 * i, 0, evacuated(q0) + i, h3h, h3l, KD)
                    if gates:
                        group(q0 + 2 * i + 1, 1, evacuated(q0 + 1) + i, yh3, yl3, KW)
                    else:
                        group(q0 + 2 * i + 1, 1, evacuated(q0 + 1) + i, h3h, h3l, KD)

            pairs_of("D")
            pe.wait_ge(masked, 1)
            pe.wait_ge(v_done, TILES)
            for g in range(KW):
                q, s = Q0["A"] + g, g % 2
                if g:
                    pe.wait_ge(gate_read, g)
                for n in range(8):
                    pe.matmul(ps[:, 6 + n // 4, (n % 4) * P:(n % 4 + 1) * P], vn[:, n, g * P:(g + 1) * P],
                              aws[:, g, :], start=True, stop=True)
                pe.wait_ge(evac[s], evacuated(q))
                pe.matmul(ps[:, 3 * s, 400:400 + NS], e("vs")[0:NS, g * P:(g + 1) * P], ident[0:NS, 0:NS],
                          start=True, stop=True).then_inc(gate_prod, 1)
                group(q, s, evacuated(q), h3h, h3l, KD)
            pairs_of("gA")
            pairs_of("B")
            pairs_of("gB")

            def pool_mix(ch):
                s = ch % 2
                pe.wait_ge(pooled, ch + 1)
                for a in range(NT):
                    mmi = pe.matmul(ps[:, 3 * s + a, 0:TT], poolw[:, ch, :],
                                    sbf(pooled_in(ch), PC + a * TT, TT), start=True, stop=True)
                mmi.then_inc(pool_prod, 1)

            for ch in range(KW):
                q = Q0["C"] + ch
                if ch == 2:
                    pool_mix(0)
                if ch == 3:
                    pool_mix(1)
                group(q, ch % 2, evacuated(q), h3h, h3l, KD)
            pool_mix(2)
            pool_mix(3)
            pairs_of("gC")
            for which in range(2):
                pe.wait_ge(evac[which], evacuated(Q0["gD"] + which) - 1)
                for ch in range(KW):
                    if which == 1:
                        pe.wait_ge(ln_sq, ch + 1)
                    for a in range(NT):
                        rhs = dc[:, ch, a * TT:(a + 1) * TT] if which == 0 else sbf(1 + ch % 2, a * TT, TT)
                        if which == 0 and ch == 0:
                            pe.wait_ge(ln_in, 1)
                        mmi = pe.matmul(ps[:, 3 * which + a, 0:TT], ones, rhs,
                                        start=(ch == 0), stop=(ch == KW - 1))
                    mmi.then_inc(ln_prod, 1)
            pairs_of("gD")

            pe.wait_ge(r3_in, 32)
            for j, first in enumerate((16, 32, 24)):
                broadcast_rows(pe, j, first)
            pe.wait_ge(wo_hi_done, KD)
            pe.wait_ge(wo_lo_done, KD)
            pe.wait_ge(m_hi_done, KD)
            pe.wait_ge(m_lo_done, KD)

            def project(t):
                at, n = tile_rows(t)
                b = 2 * (t % 2)
                if t < 2:
                    pe.wait_ge(row_done, 6)
                else:
                    pe.wait_ge(o_read, t - 1)
                for k in range(KD):
                    for x, (l, w) in enumerate(((h_hi, wo_hi), (h_hi, wo_lo), (h_lo, wo_hi))):
                        for a in range(2):
                            mmi = pe.matmul(ps[0:n, b + a, :], l[:, k, at:at + n], w[:, k, a * 512:(a + 1) * 512],
                                            start=(k == 0 and x == 0), stop=(k == KD - 1 and x == 2))
                mmi.then_inc(o_prod, 1)

            def route(t):
                at, n = tile_rows(t)
                pe.wait_ge(h2_done, t + 1)
                if t:
                    pe.wait_ge(h2T_done, t)
                for k in range(KD):
                    mmi = pe.transpose(ps[:, 4 + k // 4, (k % 4) * P:(k % 4) * P + n],
                                       h2[0:n, t % 2, k * P:(k + 1) * P], ident[0:n, 0:n])
                mmi.then_inc(h2_turned, 1)
                pe.wait_ge(h2T_done, t + 1)
                if t:
                    pe.wait_ge(logit_read, t)
                for k in range(KD):
                    mmi = pe.matmul(ps[0:n, 6, 0:36], h2T[:, k, 0:n], r("wr").rearrange("p (k n) -> p k n", k=KD)[:, k, :],
                                    start=(k == 0), stop=(k == KD - 1))
                mmi.then_inc(logit_prod, 1)

            for t in range(TILES + 1):
                if t < TILES:
                    project(t)
                if t:
                    route(t - 1)
            pe.wait_ge(mask_done, TILES)
            MS = MK[:, 2, :].rearrange("p (t e) -> p t e", t=TILES)
            for t in range(TILES + 1):
                for u in range(min(t + 1, TILES)):
                    last = u == min(t, TILES - 1)
                    mmi = pe.matmul(ps[:, 7, t * NE:(t + 1) * NE], r("tri") if u == t else ones, MS[:, u, :],
                                    start=(u == 0), stop=last)
            mmi.then_inc(rank_prod, 1)

            pe.wait_ge(slots_done, 1)
            rest = pe.value_load(block_e[0:1, BLOCKS:BLOCKS + 1], min_val=0, max_val=NPAIR - 1)

            def turn(i, s, first=False):
                b = 2 * i + s
                pe.wait_ge(xg_in[s], 16 * (i + 1))
                if not first:
                    pe.wait_ge(xgT_done, b)
                for k in range(KD):
                    mmi = pe.transpose(ps[:, k // 4, (k % 4) * P:(k % 4 + 1) * P], xg[:, s, k * P:(k + 1) * P], ident)
                mmi.then_inc(turned, 1)

            def turn_hidden(b):
                pe.wait_ge(hm_done, b + 1)
                for f in range(2):
                    mmi = pe.transpose(ps[:, 4, f * P:(f + 1) * P], hm[:, f * P:(f + 1) * P], ident)
                mmi.then_inc(hm_turned, 1)

            def gate_up(i, s):
                b = 2 * i + s
                pe.wait_ge(we_in[s], 16 * (i + 1))
                pe.wait_ge(xgT_done, b + 1)
                wv = we[:, s, 0:KD * 2 * FE].rearrange("p (k n) -> p k n", k=KD)
                for k in range(KD):
                    mmi = pe.matmul(ps[:, 2 + s, :], xgT[:, s, k, :], wv[:, k, :], start=(k == 0), stop=(k == KD - 1))
                mmi.then_inc(gu_prod, 1)

            def down(b, i, s, first=False):
                pe.wait_ge(wd_in[s], 16 * (i + 1))
                pe.wait_ge(hmT_done, b + 1)
                if not first:
                    pe.wait_ge(y_copied, b)
                wv = we[:, s, KD * 2 * FE:].rearrange("p (f n) -> p f n", f=2)
                for a in range(2):
                    for f in range(2):
                        mmi = pe.matmul(ps[:, 5 + a, :], hmT[:, f, :], wv[:, f, a * 512:(a + 1) * 512],
                                        start=(f == 0), stop=(f == 1))
                mmi.then_inc(y_prod, 1)

            turn(0, 0, first=True)
            turn(0, 1)
            gate_up(0, 0)
            turn(1, 0)
            turn_hidden(0)
            gate_up(0, 1)
            down(0, 0, 0, first=True)
            with pe.Fori(1, NPAIR) as i:
                with pe.If(i < rest + 1):
                    for s in range(2):
                        turn(i + s, 1 - s)
                        turn_hidden(2 * i + s - 1)
                        gate_up(i, s)
                        down(2 * i + s - 1, i + s - 1, 1 - s)
            turn_hidden(2 * rest + 1)
            down(2 * rest + 1, rest, 1)
            pe.wait_ge(xgT_done, 2 * rest + 3)
            broadcast_rows(pe, 3, 40)

        @block.scalar
        def _(act):
            act.wait_ge(x_in, 16)
            act.wait_ge(small_in, 16)
            for k in range(KD):
                if k:
                    act.wait_ge(sq_used, k)
                act.activation(sbf(0), xT[:, k, :], ACT.Square).then_inc(sq_ready, 1)
            act.wait_ge(early_in, 16)
            act.activation(y_hi[:, 0:KD * W], e("wv"), ACT.Copy).then_inc(wv_hi, 1)
            act.wait_ge(rstd_in, 1)
            act.activation(sbf(0), sbf(0), ACT.Sqrt).then_inc(rstd_ready, 1)
            for k in range(KD):
                act.wait_ge(h_f32, k + 1)
                act.activation(h_hi[:, k, :], xT[:, k, :], ACT.Copy).then_inc(h_hi_done, 1)
            for t in range(TILES):
                n, s = tile_rows(t)[1], t % 2
                act.wait_ge(v_prod, t + 1)
                if t == 0:
                    act.wait_ge(h_lo_done, KD)
                if t >= 2:
                    act.wait_ge(v_done, t - 1)
                act.activation(sbf(s, 0, W)[0:n], ps[0:n, 3 * s, :], ACT.Gelu_apprx_tanh,
                               accum_out=st[0:n, 4 * s:4 * s + 1]).then_inc(evac[s], 1)
                act.wait_ge(v_dve, 2 * t + 1)
                act.activation(sbf(2, 0, W)[0:n], sbf(s, 0, W)[0:n], ACT.Square,
                               accum_out=st[0:n, 4 * s + 1:4 * s + 2]).then_inc(v_act, 1)
                act.wait_ge(v_dve, 2 * t + 2)
                act.activation(st[0:n, 4 * s + 2:4 * s + 3], st[0:n, 4 * s + 2:4 * s + 3], ACT.Sqrt).then_inc(v_act, 1)

            def split_hi(pr, s, wait=True):
                act.wait_ge(raw_in, 16 * (pr + 1))
                if wait:
                    act.wait_ge(grp, 2 * pr + s - 1)
                act.activation(w_hi[:, s, :, :].rearrange("p k n -> p (k n)"), raw[:, s, :], ACT.Copy
                               ).then_inc(hi_done, 1)

            split_hi(0, 0, False)
            split_hi(0, 1, False)
            act.wait_ge(v_done, TILES)

            with act.Fori(0, 4) as i:
                split_hi(i + 1, 0)
                act.wait_ge(grp, 2 * i + 2)
                act.wait_ge(evac[0], evacuated(0) + i)
                act.activation(three(sbf(0)), pset(1), ACT.Sigmoid).then_inc(evac[1], 1)
                split_hi(i + 1, 1)
            for g in range(KW):
                q, s = Q0["A"] + g, g % 2
                act.wait_ge(grp, q + 1)
                if g < 2:
                    act.wait_ge(evac[0], evacuated(6) + 1)
                else:
                    act.wait_ge(y_done, g - 1)
                act.activation(smp[:, s, :], ps[:, 3 * s, 400:400 + NS], ACT.Identity, bias=c("bs00")[:, g:g + 1],
                               scale=c("ws00")[:, g:g + 1])
                act.activation(three(sbf(s)), pset(s), ACT.Gelu_apprx_tanh).then_inc(evac[s], 1)
                split_hi(q // 2 + 1, s)

            def gates(name):
                q0 = Q0[name]

                def pair(i, more=True):
                    act.wait_ge(grp, q0 + 2 * i + 1)
                    act.wait_ge(evac[1], evacuated(q0 + 1) + i)
                    act.activation(three(sbf(0)), pset(0), ACT.Sigmoid).then_inc(evac[0], 1)
                    if more:
                        split_hi(q0 // 2 + i + 1, 0)
                        act.wait_ge(grp, q0 + 2 * i + 2)
                        split_hi(q0 // 2 + i + 1, 1)

                act.wait_ge(y_done, KW * (1 + "ABCD".index(name[1])))
                with act.Fori(0, KD if name != "gD" else KD - 1) as i:
                    pair(i)
                if name == "gD":
                    pair(KD - 1, False)

            gates("gA")
            for j in range(3 * KW):
                q, s = Q0["B"] + j, j % 2
                act.wait_ge(grp, q + 1)
                if j % 3 == 0:
                    act.wait_ge(evac[(q - 2) % 2] if j else evac[1], evacuated(q - 2) + 1 if j else evacuated(q - 1) + 1)
                    act.activation(three(sbf(0)), pset(s), ACT.Copy).then_inc(evac[s], 1)
                split_hi(q // 2 + 1, s)
            gates("gB")
            for ch in range(KW):
                q, s = Q0["C"] + ch, ch % 2
                act.wait_ge(grp, q + 1)
                if ch:
                    act.wait_ge(y_done, 2 * KW + ch)
                else:
                    act.wait_ge(gap_zero, 1)
                act.activation(three(sbf(0, PC)), pset(s), ACT.Copy).then_inc(evac[s], 1)
                split_hi(q // 2 + 1, s)
            gates("gC")
            for ch in range(KW):
                act.wait_ge(ln_mean, ch + 1)
                if ch >= 2:
                    act.wait_ge(ln_prod, KW + ch - 1)
                act.activation(sbf(1 + ch % 2), dc[:, ch, :], ACT.Square).then_inc(ln_sq, 1)
            act.wait_ge(ln_rstd, 1)
            act.activation(sbf(0), sbf(0), ACT.Sqrt).then_inc(ln_rstd, 1)
            for ch in range(KW):
                act.wait_ge(ln_norm, ch + 1)
                act.activation(dc[:, ch, :], dc[:, ch, :], ACT.Silu, bias=c("dlb")[:, ch:ch + 1],
                               scale=c("dlg")[:, ch:ch + 1]).then_inc(ln_y, 1)
                act.wait_ge(ln_y, 2 * ch + 1)
                act.activation(yh[:, ch, :], dc[:, ch, :], ACT.Copy).then_inc(ln_y, 1)
            gates("gD")
            act.wait_ge(m_ready, 1)
            for k in range(KD):
                act.activation(h_hi[:, k, :], mm[:, k, :], ACT.Copy).then_inc(m_hi_done, 1)

            def split_wo(i, s):
                act.wait_ge(wo_in[s], 16 * (i + 1))
                act.activation(wo_hi[:, bass.ds(2 * i + s, 1), :].rearrange("p o n -> p (o n)"), wo_raw[:, s, :], ACT.Copy
                               ).then_inc(wo_hi_done, 1)

            with act.Fori(0, KD // 2) as i:
                for s in range(2):
                    split_wo(i, s)
            for t in range(TILES):
                n, s = tile_rows(t)[1], t % 2
                act.wait_ge(x1_done, t + 1)
                if t == 0:
                    act.wait_ge(r3_in, 32)
                act.activation(sq[0:n, :], xt[0:n, s, :], ACT.Square, accum_out=rt[0:n, 140:141]).then_inc(x1_sq, 1)
                act.wait_ge(x1_var, t + 1)
                act.activation(rt[0:n, 141:142], rt[0:n, 141:142], ACT.Sqrt).then_inc(x1_rstd, 1)
                act.wait_ge(h2_turned, t + 1)
                if t:
                    act.wait_ge(logit_prod, t)
                act.activation(h2T[:, :, 0:n].rearrange("p (a k) n -> p a k n", a=2),
                               ps[:, 4:6, :].rearrange("p a (k n) -> p a k n", k=4)[:, :, :, 0:n], ACT.Copy
                               ).then_inc(h2T_done, 1)
                act.wait_ge(gexp_in, t + 1)
                act.activation(rt[0:n, 60:64], rt[0:n, 0:4], ACT.Exp, bias=rt[0:n, 142:143],
                               accum_out=rt[0:n, 143:144]).then_inc(gexp_done, 1)
                act.wait_ge(eexp_in, t + 1)
                act.activation(rt[0:n, 145:146], rt[0:n, 144:145], ACT.Exp).then_inc(eexp_done, 1)

            act.wait_ge(slots_done, 1)
            act.wait_ge(y_zero, 16 * 2 * (BLOCKS - MIN_BLOCKS))
            rest = act.value_load(block_e[0:1, BLOCKS:BLOCKS + 1], min_val=0, max_val=NPAIR - 1)

            def columns_out(b, s, used=True):
                act.wait_ge(turned, b + 1)
                if used:
                    act.wait_ge(gu_prod, b - 1)
                act.activation(xgT[:, s, :, :].rearrange("p (a k) n -> p a (k n)", a=2), ps[:, 0:2, :], ACT.Copy
                               ).then_inc(xgT_done, 1)

            def silu(b, s, used=True):
                act.wait_ge(gu_prod, b + 1)
                if used:
                    act.wait_ge(hm_done, b)
                act.activation(sg[:, :], ps[:, 2 + s, 0:FE], ACT.Silu).then_inc(silu_done, 1)

            def store(b, s):
                act.wait_ge(y_copied, b + 1)
                act.dma_start(yd[bass.ds(b * P, P), :], yb[:, s, :]).then_inc(y_out[s], 16)

            columns_out(0, 0, False)
            columns_out(1, 1, False)
            silu(0, 0, False)
            columns_out(2, 0)
            silu(1, 1)
            store(0, 0)
            with act.Fori(1, NPAIR) as i:
                with act.If(i < rest + 1):
                    for s in range(2):
                        columns_out(2 * i + s + 1, 1 - s)
                        silu(2 * i + s, s)
                        store(2 * i + s - 1, 1 - s)
            store(2 * rest + 1, 1)
            act.wait_ge(y_out[0], 16 * rest + 16)
            act.wait_ge(y_out[1], 16 * rest + 16)
            for t in range(TILES):
                n, s = tile_rows(t)[1], t % 2
                act.wait_ge(c_sq_in, t + 1)
                act.activation(y1[0:n, s, :], x1[0:n, s, :], ACT.Square, accum_out=cs[0:n, 0:1]).then_inc(c_sq, 1)
                act.wait_ge(c_var, t + 1)
                act.activation(cs[0:n, 1:2], cs[0:n, 1:2], ACT.Sqrt).then_inc(c_rstd, 1)


        @block.gpsimd
        def _(pool):
            pool.memset(zeros[:, :], 0.0).then_inc(zeros_ready, 1)
            pool.wait_ge(early_in, 16)
            pool.affine_select(out=aws, in_=aws, compare_op=ALU.is_ge, fill=0.0, base=0,
                               pattern=[[0, KW], [1, P]], channel_multiplier=-1).then_inc(masked, 1)
            pool.wait_ge(wv_hi, 1)
            pool.tensor_tensor(y_lo[:, 0:KD * W], e("wv"), y_hi[:, 0:KD * W].bitcast(F32), ALU.subtract
                               ).then_inc(wv_lo, 1)

            def split_lo(pr, s, wait=True):
                pool.wait_ge(raw_in, 16 * (pr + 1))
                pool.wait_ge(hi_done, 2 * pr + s + 1)
                if wait:
                    pool.wait_ge(grp, 2 * pr + s - 1)
                pool.tensor_tensor(w_lo[:, s, :, :].rearrange("p k n -> p (k n)"), raw[:, s, :],
                                   w_hi[:, s, :, :].rearrange("p k n -> p (k n)").bitcast(F32), ALU.subtract
                                   ).then_inc(lo_done, 1)

            split_lo(0, 0, False)
            split_lo(0, 1, False)
            with pool.Fori(1, N_GROUPS // 2) as i:
                for s in range(2):
                    split_lo(i, s)

            def split_wo_lo(i, s):
                pool.wait_ge(wo_in[s], 16 * (i + 1))
                pool.wait_ge(wo_hi_done, 2 * i + s + 1)
                pool.tensor_tensor(wo_lo[:, bass.ds(2 * i + s, 1), :].rearrange("p o n -> p (o n)"), wo_raw[:, s, :],
                                   wo_hi[:, bass.ds(2 * i + s, 1), :].rearrange("p o n -> p (o n)").bitcast(F32),
                                   ALU.subtract).then_inc(wo_lo_done, 1)

            with pool.Fori(0, KD // 2) as i:
                for s in range(2):
                    split_wo_lo(i, s)
            pool.wait_ge(m_hi_done, KD)
            pool.wait_ge(m_lo_done, KD)
            pool.memset(zero_ids[:, :], 0).then_inc(table_zero, 1)

            pool.wait_ge(slots_done, 1)
            pool.wait_ge(table_out, 16)
            pool.wait_ge(h2_out[0], 16 * 5)
            pool.wait_ge(h2_out[1], 16 * 4)
            for ch in range(2):
                for t in range(TILES):
                    n = tile_rows(t)[1]
                    j = ch * TILES + t
                    pool.indirect_dma_start(
                        tabd, bass.IndirectOffsetOnAxis(ap=slots[0:n, j:j + 1].bitcast(U32), axis=0),
                        tokid[0:n, t:t + 1], None).then_inc(ids_done, 16)
            pool.wait_ge(ids_done, 16 * 2 * TILES)
            rest = pool.value_load(block_e[0:1, BLOCKS:BLOCKS + 1], min_val=0, max_val=NPAIR - 1)

            def gather(i, s, used=True):
                b = 2 * i + s
                if used:
                    pool.wait_ge(turned, b - 1)
                pool.dma_start(idx[:, s:s + 1], tabd[bass.ds(b * P, P), :]).then_inc(idx_in[s], 16)
                pool.wait_ge(idx_in[s], 16 * (i + 1))
                pool.sem_inc(gathers, 1)
                pool.indirect_dma_start(
                    xg[:, s, :], None, h2d, bass.IndirectOffsetOnAxis(ap=idx[:, s:s + 1].bitcast(U32), axis=0)
                ).then_inc(xg_in[s], 16)

            gather(0, 0, False)
            gather(0, 1, False)
            gather(1, 0)
            with pool.Fori(1, NPAIR) as i:
                with pool.If(i < rest + 1):
                    gather(i, 1)
                    gather(i + 1, 0)
            pool.wait_ge(y_out[0], 16 * rest + 16)
            pool.wait_ge(y_out[1], 16 * rest + 16)
            pool.sem_inc(gathers, 1)
            for t in range(TILES):
                n, s = tile_rows(t)[1], t % 2
                if t >= 2:
                    pool.wait_ge(c_done, t - 1)
                for ch, (buf, got) in enumerate(((y1, y1_in), (y2, y2_in))):
                    j = ch * TILES + t
                    pool.indirect_dma_start(
                        buf[0:n, s, :], None, yd,
                        bass.IndirectOffsetOnAxis(ap=slots[0:n, j:j + 1].bitcast(U32), axis=0)
                    ).then_inc(got[s], 16)

        @block.vector
        def _(dve):
            steps = Steps(dve, dve_step)
            link = steps.link
            SUB, ADD, MUL = ALU.subtract, ALU.add, ALU.mult
            tt, ts, stt, cp = dve.tensor_tensor, dve.tensor_scalar, dve.scalar_tensor_tensor, dve.tensor_copy
            dve.wait_ge(sq_used, KD)
            ts(three(sbf(0)), pset(0), 1.0 / D, EPS, MUL, ADD).then_inc(evac[0], 1)
            dve.wait_ge(evac[0], 1)
            dve.reciprocal(sbf(0), sbf(0)).then_inc(rstd_in, 1)
            dve.wait_ge(slab_used, 24)
            dve.wait_ge(small_in, 16)
            link(tt(modT, ps[:, 6, 0:48 * NV].rearrange("p (n v) -> p n v", n=48),
                    c("bmod").unsqueeze(2).to_broadcast([P, 48, NV]), ADD))
            link(stt(modT[:, 8:16, :], modT[:, 8:16, :], 1.0, c("n1g").unsqueeze(2).to_broadcast([P, KD, NV]), ADD, MUL))
            link(stt(modT[:, 32:40, :], modT[:, 32:40, :], 1.0, c("n2g").unsqueeze(2).to_broadcast([P, KD, NV]),
                     ADD, MUL))
            dve.wait_ge(rstd_ready, 1)
            for k in range(KD):
                link(tt(xT[:, k, :], xT[:, k, :], sbf(0), MUL))
                link(ts(xT[:, k, 0:LP], xT[:, k, 0:LP], modT[:, 8 + k, 0:1], modT[:, k, 0:1], MUL, ADD))
                link(tt(xT[:, k, LP:T], xT[:, k, LP:T], modT[:, 8 + k, 1:NV], MUL))
                tt(xT[:, k, LP:T], xT[:, k, LP:T], modT[:, k, 1:NV], ADD).then_inc(h_f32, 1)
            dve.wait_ge(h_f32, KD)
            for k in range(KD):
                dve.wait_ge(h_hi_done, k + 1)
                tt(h_lo[:, k, :], xT[:, k, :], h_hi[:, k, :].bitcast(F32), SUB).then_inc(h_lo_done, 1)
            dve.wait_ge(h_lo_done, KD)
            dve.wait_ge(early_in, 16)
            for ch in range(KW):
                scr = sbf(1, 0, NS * (CD - 1)).rearrange("p (b l) -> p b l", b=NS)
                link(tt(scr, st_d[:, ch], cdw[:, ch, 0:CD - 1].unsqueeze(1).to_broadcast([P, NS, CD - 1]), MUL))
                link(dve.tensor_reduce(dsums[:, ch, :], scr, AXX, ADD))
                link(dve.tensor_reduce(psums[:, ch, :], st_p[:, ch, :, PC + 1 - 2 ** (ch + 1):PC], AXX, ADD))
            dve.memset(sbf(1, 0, 2), 0.0).then_inc(v_start, 1)
            for t in range(TILES):
                n, s = tile_rows(t)[1], t % 2
                v, w = sbf(s, 0, W)[0:n], st[0:n, 4 * s:4 * s + 4]
                dve.wait_ge(evac[s], (2 if s == 0 else 1) + t // 2)
                link(ts(w[:, 3:4], w[:, 0:1], -1.0 / W, None, MUL))
                ts(v, v, w[:, 3:4], None, ADD).then_inc(v_dve, 1)
                dve.wait_ge(v_act, 2 * t + 1)
                link(ts(w[:, 2:3], w[:, 1:2], 1.0 / W, EPS, MUL, ADD))
                dve.reciprocal(w[:, 2:3], w[:, 2:3]).then_inc(v_dve, 1)
                dve.wait_ge(v_act, 2 * t + 2)
                link(stt(v, v, w[:, 2:3], e("alg")[0:n], MUL, MUL))
                out = vn[:, t, :] if t < TILES - 1 else e("vs")[0:NS, :]
                tt(out, v, e("alb")[0:n], ADD).then_inc(v_done, 1)
            dve.wait_ge(v_done, TILES)
            link(dve.memset(gl[:, :, 0:CD - 1], 0.0))
            with dve.Fori(0, 4) as i:
                dve.wait_ge(evac[1], evacuated(1) + 1 + i)
                tt(three(gl[:, bass.ds(i, 1), CD - 1:].rearrange("p o t -> p (o t)")), pset(0), three(sbf(0)), MUL
                   ).then_inc(evac[0], 1)
            dve.wait_ge(evac[0], evacuated(8))

            def split_y(ch, src, only_lo=False):
                link(cp(yh[:, ch, :], src))
                tt(yl[:, ch, :], src, yh[:, ch, :].bitcast(F32), SUB).then_inc(y_done, 1)

            for g in range(KW):
                q, s = Q0["A"] + g, g % 2
                dve.wait_ge(gate_prod, g + 1)
                if g:
                    dve.wait_ge(y_done, g)
                tt(sbf(2, 0, LP).rearrange("p (a n t) -> p a n t", a=2, n=4), ps[:, 6:8, :].rearrange("p a (n t) -> p a n t", n=4),
                   abs_[:, g, :].unsqueeze(1).unsqueeze(1).to_broadcast([P, 2, 4, P]), ADD).then_inc(gate_read, 1)
                dve.wait_ge(gate_read, g + 1)
                dve.wait_ge(evac[s], evacuated(q) + 1)
                link(tt(sbf(2, 0, LP), sbf(2, 0, LP), sbf(s, 0, LP), MUL))
                link(tt(sbf(2, LP, NS), smp[:, s, :], sbf(s, LP, NS), MUL))
                split_y(g, sbf(2))
            dve.wait_ge(y_done, KW)

            def tap(ch, l):
                x = gl[:, ch, :]
                link(stt(dc[:, ch, 0:LP], gl[:, ch, bass.ds(l, LP)], cdw[:, ch, bass.ds(l, 1)], dc[:, ch, 0:LP],
                         MUL, ADD))

            def first_tap(ch):
                link(ts(dc[:, ch, 0:LP], gl[:, ch, 0:LP], cdw[:, ch, 0:1], c("cdb")[:, ch:ch + 1], MUL, ADD))
                link(stt(dc[:, ch, LP:T], gl[:, ch, GLW - NS:GLW], cdw[:, ch, CD - 1:CD], dsums[:, ch, :], MUL, ADD))
                link(ts(dc[:, ch, LP:T], dc[:, ch, LP:T], c("cdb")[:, ch:ch + 1], None, ADD))

            def merge(name, i, j):
                q0 = Q0[name]
                dve.wait_ge(grp, q0 + 2 * i + 2)
                dve.wait_ge(evac[0], evacuated(q0) + i + 1)
                mj = mm[:, bass.ds(j, 1), :].rearrange("p o t -> p (o t)")
                if name == "gA":
                    tt(three(mj), pset(1), three(sbf(0)), MUL).then_inc(evac[1], 1)
                else:
                    tt(three(sbf(1)), pset(1), three(sbf(0)), MUL).then_inc(evac[1], 1)
                    dve.wait_ge(evac[1], evacuated(q0 + 1) + i + 1)
                    link(tt(mj, mj, sbf(1), ADD))

            def gates(name, chunks=()):
                for ch in chunks:
                    first_tap(ch)
                adds = 0 if name == "gA" else 1
                with dve.Fori(0, KD - 1) as i:
                    steps.loop(i, 0, adds + 4 * len(chunks))
                    merge(name, i, i)
                    for k in range(4):
                        for ch in chunks:
                            tap(ch, 1 + 4 * i + k)
                steps.done(KD - 1)
                merge(name, KD - 1, KD - 1)
                for l in (CD - 2, CD - 1):
                    for ch in chunks:
                        tap(ch, l)

            gates("gA", (0, 1))
            link(dve.memset(sbf(1, 0, 2), 0.0))
            for ch in range(KW):
                q = Q0["B"] + 3 * ch
                cx, o = sbf(1, 0, T + 2), sbf(2)
                dve.wait_ge(grp, q + 2)
                dve.wait_ge(evac[q % 2], evacuated(q) + 1)
                s = (q + 1) % 2
                tt(three(cx[:, 2:]), pset(s), three(sbf(0)), MUL).then_inc(evac[s], 1)
                dve.wait_ge(evac[s], evacuated(q + 1) + 1)
                if ch:
                    dve.wait_ge(y_done, KW + ch)
                link(ts(o[:, 0:LP], cx[:, 0:LP], cbw[:, 0, ch:ch + 1], None, MUL))
                link(ts(o[:, LP:T], st_b[:, ch, :, 0], cbw[:, 0, ch:ch + 1], None, MUL))
                link(stt(o[:, 0:LP], cx[:, 1:LP + 1], cbw[:, 1, ch:ch + 1], o[:, 0:LP], MUL, ADD))
                link(stt(o[:, LP:T], st_b[:, ch, :, 1], cbw[:, 1, ch:ch + 1], o[:, LP:T], MUL, ADD))
                link(stt(o, cx[:, 2:], cbw[:, 2, ch:ch + 1], o, MUL, ADD))
                link(cp(tail_b[:, ch, :], cx[:, LP:LP + 10]))
                s = (q + 2) % 2
                dve.wait_ge(grp, q + 3)
                tt(three(o), pset(s), three(o), MUL).then_inc(evac[s], 1)
                dve.wait_ge(evac[s], evacuated(q + 2) + 1)
                split_y(ch, o)
            dve.wait_ge(y_done, 2 * KW)
            dve.engine_nop().then_inc(tails_b, 1)
            gates("gB", (2, 3))
            dve.memset(sbf(0, 0, PC), 0.0).then_inc(gap_zero, 1)
            X = PC + LP
            for ch in range(KW):
                q, s = Q0["C"] + ch, ch % 2
                x0 = sbf(0, 0, PC + T)
                dve.wait_ge(evac[s], evacuated(q) + 1)
                if ch:
                    dve.wait_ge(y_done, 2 * KW + ch)
                src, width = x0, 1
                for d in range(ch + 1):
                    dst = sbf(1 + d % 2, 0, PC + T)
                    lo = 2 * width - 1
                    link(tt(dst[:, lo:X], src[:, lo:X], src[:, lo - width:X - width], ADD))
                    src, width = dst, 2 * width
                p = sbf(pooled_in(ch), 0, PC + T)
                link(stt(p[:, PC:X], src[:, PC:X], 1.0 / width, x0[:, PC:X], MUL, SUB))
                link(tt(p[:, PC:2 * PC], src[:, PC:2 * PC], inv[:, ch, :], MUL))
                link(tt(p[:, PC:2 * PC], p[:, PC:2 * PC], x0[:, PC:2 * PC], SUB))
                link(tt(p[:, X:X + NS], psums[:, ch, :], x0[:, X:X + NS], ADD))
                link(cp(tail_p[:, ch, :], x0[:, LP:LP + PC + NS]))
                stt(p[:, X:X + NS], p[:, X:X + NS], 1.0 / width, x0[:, X:X + NS], MUL, SUB).then_inc(pooled, 1)
                dve.wait_ge(pool_prod, ch + 1)
                o = sbf(3 - pooled_in(ch))
                ts(three(o), pset(s), c("pscale")[:, ch:ch + 1], None, MUL).then_inc(evac[s], 1)
                dve.wait_ge(evac[s], evacuated(q) + 2)
                split_y(ch, o)
            dve.wait_ge(y_done, 3 * KW)
            dve.engine_nop().then_inc(tails_p, 1)
            gates("gC")
            dve.engine_nop().then_inc(ln_in, 1)
            dve.wait_ge(ln_prod, KW)
            ts(three(sbf(0)), pset(0), 1.0 / W, None, MUL).then_inc(evac[0], 1)
            dve.wait_ge(evac[0], evacuated(Q0["gD"]))
            for ch in range(KW):
                tt(dc[:, ch, :], dc[:, ch, :], sbf(0), SUB).then_inc(ln_mean, 1)
            dve.wait_ge(ln_mean, KW)
            dve.wait_ge(ln_prod, 2 * KW)
            ts(three(sbf(0)), pset(1), 1.0 / W, EPS, MUL, ADD).then_inc(evac[1], 1)
            dve.wait_ge(evac[1], evacuated(Q0["gD"] + 1))
            dve.reciprocal(sbf(0), sbf(0)).then_inc(ln_rstd, 1)
            dve.wait_ge(ln_rstd, 2)
            for ch in range(KW):
                tt(dc[:, ch, :], dc[:, ch, :], sbf(0), MUL).then_inc(ln_norm, 1)
            for ch in range(KW):
                dve.wait_ge(ln_y, 2 * ch + 2)
                tt(yl[:, ch, :], dc[:, ch, :], yh[:, ch, :].bitcast(F32), SUB).then_inc(y_done, 1)
            gates("gD")
            dve.engine_nop().then_inc(m_ready, 1)
            for k in range(KD):
                dve.wait_ge(m_hi_done, k + 1)
                tt(h_lo[:, k, :], mm[:, k, :], h_hi[:, k, :].bitcast(F32), SUB).then_inc(m_lo_done, 1)

            dve.wait_ge(m_lo_done, KD)
            for j in range(3):
                for v, (dst, n) in enumerate(((rows, P), (rows_s, NS))):
                    dve.wait_ge(row_prod, 2 * j + v + 1)
                    cp(dst[0:n, j, :].rearrange("p (a n) -> p a n", a=2), ps[0:n, 2 * v:2 * v + 2, :]
                       ).then_inc(row_done, 1)
            dve.wait_ge(row_done, 6)
            dve.wait_ge(r3_in, 32)
            M1, M2, MS = (MK[:, j, :].rearrange("p (t e) -> p t e", t=TILES) for j in range(3))
            link(dve.memset(MK[:, :, (TILES - 1) * NE:], 0.0))
            link(dve.memset(slots[:, :], 0))
            link(dve.memset(rt[:, 40:48], -3.0e38))
            two = lambda ap: ap.rearrange("p (a n) -> p a n", a=2)
            for t in range(TILES):
                n, s = tile_rows(t)[1], t % 2
                R = rows if t < TILES - 1 else rows_s
                z = rt[0:n, :]
                zi = ri[0:n, :]
                dve.wait_ge(o_prod, t + 1)
                if t >= 2:
                    dve.wait_ge(h2_out[s], 16 * (t // 2))
                    dve.wait_ge(h2_turned, t - 1)
                tt(two(h2[0:n, s, :]), ps[0:n, 2 * s:2 * s + 2, :], two(R[0:n, 0, :]), MUL).then_inc(o_read, 1)
                dve.wait_ge(o_read, t + 1)
                dve.wait_ge(xt_in[s], 16 * (t // 2 + 1))
                tt(xt[0:n, s, :], h2[0:n, s, :], xt[0:n, s, :], ADD).then_inc(x1_done, 1)
                dve.wait_ge(x1_sq, t + 1)
                dve.wait_ge(x1_done, t + 1)
                link(ts(z[:, 141:142], z[:, 140:141], 1.0 / D, EPS, MUL, ADD))
                dve.reciprocal(z[:, 141:142], z[:, 141:142]).then_inc(x1_var, 1)
                dve.wait_ge(x1_rstd, t + 1)
                link(stt(h2[0:n, s, :], xt[0:n, s, :], z[:, 141:142], R[0:n, 1, :], MUL, MUL))
                tt(h2[0:n, s, :], h2[0:n, s, :], R[0:n, 2, :], ADD).then_inc(h2_done, 1)
                dve.wait_ge(logit_prod, t + 1)
                tt(z[:, 0:36], ps[0:n, 6, 0:36], r("br")[0:n], ADD).then_inc(logit_read, 1)
                dve.wait_ge(logit_read, t + 1)
                link(cp(z[:, 40:44], z[:, 0:4]))
                link(dve.max(z[:, 48:56], z[:, 40:48]))
                link(dve.max_index(zi[:, 0:8], z[:, 48:56], z[:, 40:48]))
                link(cp(z[:, 56:57], zi[:, 0:1]))
                ts(z[:, 142:143], z[:, 48:49], -1.0, None, MUL).then_inc(gexp_in, 1)
                link(ts(z[:, 116:120], r("iota")[0:n, 0:NG], z[:, 56:57], None, ALU.is_equal))
                link(tt(z[:, 64:96].rearrange("p (g e) -> p g e", g=NG), z[:, 4:36].rearrange("p (g e) -> p g e", g=NG),
                        z[:, 116:120].unsqueeze(2).to_broadcast([n, NG, 8]), MUL))
                link(dve.tensor_reduce(z[:, 96:104], z[:, 64:96].rearrange("p (g e) -> p e g", g=NG), AXX, ADD))
                link(dve.max(z[:, 104:112], z[:, 96:104]))
                link(dve.max_index(zi[:, 8:16], z[:, 104:112], z[:, 96:104]))
                tt(z[:, 144:145], z[:, 105:106], z[:, 104:105], SUB).then_inc(eexp_in, 1)
                link(cp(z[:, 112:114], zi[:, 8:10]))
                link(stt(z[:, 114:116], z[:, 56:57].to_broadcast([n, 2]), 8.0, z[:, 112:114], MUL, ADD))
                link(ts(M1[0:n, t, :], r("iota")[0:n], z[:, 114:115], None, ALU.is_equal))
                link(ts(M2[0:n, t, :], r("iota")[0:n], z[:, 115:116], None, ALU.is_equal))
                tt(MS[0:n, t, :], M1[0:n, t, :], M2[0:n, t, :], ADD).then_inc(mask_done, 1)
                dve.wait_ge(gexp_done, t + 1)
                dve.wait_ge(eexp_done, t + 1)
                link(ts(z[:, 146:147], z[:, 145:146], 1.0, z[:, 143:144], ADD, MUL))
                link(dve.reciprocal(wts[0:n, 0, t:t + 1], z[:, 146:147]))
                link(tt(wts[0:n, 1, t:t + 1], wts[0:n, 0, t:t + 1], z[:, 145:146], MUL))
            dve.wait_ge(rank_prod, 1)
            cnt = rt[:, 0:NE]
            nb, end, base = rt[:, 32:64], rt[:, 64:96], rt[:, 96:128]
            big = cmp_[:, 0:NE * 9].rearrange("p (e j) -> p e j", e=NE)
            link(cp(cnt, ps[:, 7, TILES * NE:(TILES + 1) * NE]))
            link(tt(big, cnt.unsqueeze(2).to_broadcast([P, NE, 9]), r("thr").unsqueeze(1).to_broadcast([P, NE, 9]),
                    ALU.is_gt))
            link(dve.tensor_reduce(nb, big, AXX, ADD))
            link(dve.tensor_tensor_scan(end, ones[:, 0:NE], nb, 0.0, MUL, ADD))
            link(tt(base, end, nb, SUB))
            link(ts(base, base, float(P), None, MUL))
            rank = cmp_[:, 0:TILES * NE].rearrange("p (t e) -> p t e", t=TILES)
            link(tt(rank, ps[:, 7, 0:TILES * NE].rearrange("p (t e) -> p t e", t=TILES),
                    base.unsqueeze(1).to_broadcast([P, TILES, NE]), ADD))
            for ch, M in enumerate((M1, M2)):
                link(tt(M, M, rank, MUL))
                link(dve.tensor_reduce(rt[:, 128 + ch * TILES:128 + (ch + 1) * TILES], M, AXX, ADD))
            link(cp(slots[:, :], rt[:, 128:128 + 2 * TILES]))
            blk = cmp_[:, :].rearrange("p (b e) -> p b e", b=BLOCKS)
            link(tt(blk, end.unsqueeze(1).to_broadcast([P, BLOCKS, NE]),
                    r("biota").unsqueeze(2).to_broadcast([P, BLOCKS, NE]), ALU.is_le))
            link(dve.tensor_reduce(rt[:, 0:BLOCKS], blk, AXX, ADD))
            link(ts(rt[:, 0:BLOCKS], rt[:, 0:BLOCKS], float(NE - 1), None, ALU.min))
            link(cp(block_e[:, 0:BLOCKS], rt[:, 0:BLOCKS]))
            link(ts(cmp_[:, 0:NPAIR], r("pair"), end[:, NE - 1:NE], None, ALU.is_lt))
            link(dve.tensor_reduce(rt[:, 0:1], cmp_[:, 0:NPAIR], AXX, ADD))
            ts(block_e[:, BLOCKS:BLOCKS + 1], rt[:, 0:1], -1.0, None, ADD).then_inc(slots_done, 1)

            dve.wait_ge(slots_done, 1)
            rest = dve.value_load(block_e[0:1, BLOCKS:BLOCKS + 1], min_val=0, max_val=NPAIR - 1)

            def hidden(b, s):
                dve.wait_ge(silu_done, b + 1)
                tt(hm[:, :], ps[:, 2 + s, FE:2 * FE], sg[:, :], MUL).then_inc(hm_done, 1)

            def hidden_columns(b):
                dve.wait_ge(hm_turned, b + 1)
                cp(hmT[:, :, :].rearrange("p f n -> p (f n)"), ps[:, 4, 0:2 * P]).then_inc(hmT_done, 1)

            def copy_y(b, i, s, used=True):
                dve.wait_ge(y_prod, b + 1)
                if used:
                    dve.wait_ge(y_out[s], 16 * i)
                cp(two(yb[:, s, :]), ps[:, 5:7, :]).then_inc(y_copied, 1)

            hidden(0, 0)
            hidden_columns(0)
            hidden(1, 1)
            copy_y(0, 0, 0, False)
            hidden_columns(1)
            hidden(2, 0)
            copy_y(1, 0, 1, False)
            hidden_columns(2)
            hidden(3, 1)
            copy_y(2, 1, 0)
            with dve.Fori(2, NPAIR) as i:
                with dve.If(i < rest + 1):
                    hidden_columns(2 * i - 1)
                    hidden(2 * i, 0)
                    copy_y(2 * i - 1, i - 1, 1)
                    hidden_columns(2 * i)
                    hidden(2 * i + 1, 1)
                    copy_y(2 * i, i, 0)
            hidden_columns(2 * rest + 1)
            copy_y(2 * rest + 1, rest, 1)
            for v, n in enumerate((P, NS)):
                dve.wait_ge(g2_prod, v + 1)
                link(cp(two(g2r[0:n, v, :]), ps[0:n, 2 * v:2 * v + 2, :]))
            dve.wait_ge(fg_in, 16)
            for t in range(TILES):
                n, s = tile_rows(t)[1], t % 2
                a, b_, x = y1[0:n, s, :], y2[0:n, s, :], x1[0:n, s, :]
                dve.wait_ge(y1_in[s], 16 * (t // 2 + 1))
                link(ts(a, a, wts[0:n, 0, t:t + 1], None, MUL))
                dve.wait_ge(y2_in[s], 16 * (t // 2 + 1))
                link(stt(b_, b_, wts[0:n, 1, t:t + 1], a, MUL, ADD))
                link(tt(b_, b_, g2r[0:n, 0 if t < TILES - 1 else 1, :], MUL))
                dve.wait_ge(x1_in[s], 16 * (t // 2 + 1))
                tt(x, x, b_, ADD).then_inc(c_sq_in, 1)
                dve.wait_ge(c_sq_in, t + 1)
                dve.wait_ge(c_sq, t + 1)
                link(ts(cs[0:n, 1:2], cs[0:n, 0:1], 1.0 / D, EPS, MUL, ADD))
                dve.reciprocal(cs[0:n, 1:2], cs[0:n, 1:2]).then_inc(c_var, 1)
                dve.wait_ge(c_rstd, t + 1)
                stt(x, x, cs[0:n, 1:2], fg[0:n, :], MUL, MUL).then_inc(c_done, 1)


def kernel(**inputs):
    import concourse.bacc as bacc
    from concourse.bass_utils import run_bass_kernel_spmd

    a = {k: np.asarray(v) for k, v in inputs.items()}
    f = np.float32

    def chan(x, n):
        x = np.moveaxis(x, -1, 0)
        return np.moveaxis(x.reshape((n, P) + x.shape[1:]), 0, 1)

    def kmaj(w):
        return w.reshape(-1, P, w.shape[1]).transpose(1, 0, 2)

    def rep(x):
        return np.broadcast_to(x.reshape(1, -1), (P, x.size))

    def fill(where, width, parts):
        out = np.zeros((P, width), f)
        for name, x in parts.items():
            lo, hi = where[name]
            out[:, lo:hi] = np.asarray(x).reshape(P, hi - lo)
        return out

    x = np.concatenate([a["x_prompt"][0], a["x_sample"][:, 0]], axis=0)
    cc = np.concatenate([a["c_prompt"], a["c_sample"]], axis=0)
    eye = np.eye(P, dtype=f)
    inv = np.stack([1.0 / np.minimum(np.arange(PC) + 1, 2 ** (g + 1)) for g in range(KW)]).astype(f)
    ws = a["a_ws"][0]
    small = fill(COLS, LOADED, dict(
        ident=eye, ones=np.ones((P, P), f), cT=chan(cc, KD), bmod=chan(a["b_mod"][0], 48), n1g=chan(a["norm1_g"][0], KD),
        n2g=chan(a["norm2_g"][0], KD), cbw=np.moveaxis(chan(a["conv_b_w"][0], KW), 2, 1), cdw=chan(a["conv_d_w"][0], KW),
        cdb=chan(a["conv_d_b"][0], KW), dlg=chan(a["d_ln_g"][0], KW), dlb=chan(a["d_ln_b"][0], KW),
        pscale=chan(a["pool_scale"][0], KW), ws00=rep(ws[:, 0, 0]), bs00=rep(a["a_bs"][0, :, 0]),
        st_b=chan(a["state_conv_b"][0], KW), poolw=a["pool_w"][0].transpose(1, 0, 2), inv=rep(inv)))
    early = fill(ECOLS, EARLY_LOADED, dict(
        wv=kmaj(a["w_in"][0][:, W:2 * W]), st_d=chan(a["state_conv_d"][0], KW), st_p=chan(a["state_pool"][0], KW),
        alg=rep(a["a_ln_g"][0]), alb=rep(a["a_ln_b"][0]), aws=ws.transpose(2, 0, 1), abs=rep(a["a_bs"][0])))
    w_in = kmaj(a["w_in"][0])

    def cols(first, n=P):
        return w_in[:, :, first:first + n].reshape(P, -1)

    u, gb, gc, xin, pin, ga, gg = (x_ * W for x_ in (0, 2, 3, 4, 5, 6, 7))
    order = []
    for ch in range(KW):
        order += [ga + ch * P, gg + ch * P]
    order += [u + ch * P for ch in range(KW)]
    for ch in range(KW):
        order += [gc + ch * P, xin + ch * P, gb + ch * P]
    order += [pin + ch * P for ch in range(KW)]
    w_mix = np.stack([cols(o) for o in order]).reshape(-1, 2, P, KD * P).transpose(0, 2, 1, 3).reshape(-1, P, 2 * KD * P)
    w_gate = np.stack([np.concatenate([cols(8 * W + br * D + j * P), kmaj(a["w_branch"][0, br][:, j * P:(j + 1) * P]
                                                                     ).reshape(P, -1)], axis=1)
                       for br in range(4) for j in range(KD)])
    gu = np.concatenate([a["w_eg"][0], a["w_eu"][0]], axis=2).reshape(NE, KD, P, 2 * FE).transpose(0, 2, 1, 3)
    dn = a["w_ed"][0].reshape(NE, 2, P, D).transpose(0, 2, 1, 3)
    routing = np.zeros((P, R3W), f)
    routing[:, 0:P] = eye
    routing[:, P:2 * P] = 1.0
    routing[:, slice(*R3["tri"])] = np.triu(np.ones((P, P), f), 1)
    routing[:, slice(*R3["iota"])] = np.arange(NE)
    routing[:, slice(*R3["thr"])] = P * np.arange(9)
    routing[:, slice(*R3["biota"])] = np.arange(BLOCKS)
    routing[:, slice(*R3["pair"])] = 2 * np.arange(NPAIR)
    routing[:, slice(*R3["br"])] = np.concatenate([a["b_rg"][0], a["b_re"][0]])
    routing[:, slice(*R3["wr"])] = kmaj(np.concatenate([a["w_rg"][0], a["w_re"][0]], axis=1)).reshape(P, -1)
    arrays = dict(
        small=small, xT=chan(x, KD), early=early,
        w_mod=kmaj(a["w_mod"][0]).reshape(P, KD, 24, 256).transpose(2, 0, 1, 3), w_mix=w_mix, w_gate=w_gate,
        w_out=kmaj(a["w_out"][0]), x_tok=x, routing=routing,
        tokid=(np.arange(P)[:, None] + P * np.arange(TILES)[None, :]).astype(np.int32),
        w_exp=np.concatenate([gu.reshape(NE, P, -1), dn.reshape(NE, P, -1)], axis=2), final_g=rep(a["final_g"]),
        state_b=a["state_conv_b"][0], state_p=a["state_pool"][0], state_d=a["state_conv_d"][0])
    arrays = {k: np.ascontiguousarray(v) for k, v in arrays.items()}
    shapes = dict(y=(T, D), v_s=(NS, W), keep_b=(NS, 1, W), keep_p=(NS, PC - 1, W), keep_d=(NS, CD - 2, W),
                  tail_b=(P, KW, 10), tail_p=(P, KW, 23), tail_d=(P, KW, 38))
    nc = bacc.Bacc("TRN2", target_bir_lowering=False, num_devices=1)
    A = {k: nc.dram_tensor(k, v.shape, mybir.dt.from_np(v.dtype), kind="ExternalInput").ap() for k, v in arrays.items()}
    O = {k: nc.dram_tensor("out_" + k, v, F32, kind="ExternalOutput").ap() for k, v in shapes.items()}
    build(nc, A, O)
    r = run_bass_kernel_spmd(nc, [arrays], core_ids=[0]).results[0]
    o = {k: np.asarray(r["out_" + k]) for k in shapes}

    def rows_of(tail):
        return tail.transpose(2, 1, 0).reshape(tail.shape[2], W)

    tb, tp, td = (rows_of(o[k]) for k in ("tail_b", "tail_p", "tail_d"))

    def state(keep, tail):
        return np.concatenate([keep, tail[-NS:, None, :]], axis=1)[None]

    return (o["y"][None, :LP], o["y"][LP:, None], tb[None, None, :2], tp[None, None, :PC], td[None, None, :CD - 1],
            state(o["keep_b"], tb), state(o["keep_p"], tp), state(o["keep_d"], td), o["v_s"][None, :, None])
```

```python
from contextlib import ExitStack

import numpy as np

import concourse.bass as bass
from concourse import mybir

F32 = mybir.dt.float32
F32R = mybir.dt.float32r
I32 = mybir.dt.int32
U32 = mybir.dt.uint32
ALU = mybir.AluOpType
ACT = mybir.ActivationFunctionType
AXX = mybir.AxisListType.X

P = 128
D = 1024
KD = D // P
LP = 1024
NS = 8
T = LP + NS
NT = 3
TT = T // NT
W = 512
KW = W // P
NV = 1 + NS
CD = 31
PC = 15
EPS = 1e-6
SLAB = 2 * D
TILES = LP // P + 1
NE = 32
NG = 4
FE = 256
BLOCKS = 50
MIN_BLOCKS = 18
NPAIR = 24
GUW = KD * 2 * FE
YB = 6
EW = GUW + 2 * D
GLW = CD - 1 + T
SW = T + 32

MIX_PAIRS = {"D": 4, "A": 2, "B": 6, "C": 2}
N_GROUPS = 2 * (sum(MIX_PAIRS.values()) + 4 * KD)
Q0, q = {}, 0
for name_, pairs_ in (("D", 4), ("A", 2), ("gA", 8), ("B", 6), ("gB", 8), ("C", 2), ("gC", 8), ("gD", 8)):
    Q0[name_] = q
    q += 2 * pairs_


def columns():
    at, where = 0, {}
    for name, n in (("ident", P), ("ones", P), ("cT", KD * 32),
                    ("cbw", 3 * KW), ("cdw", KW * CD), ("cdb", KW), ("dlg", KW), ("dlb", KW), ("pscale", KW),
                    ("ws00", KW), ("bs00", KW), ("st_b", KW * NS * 2), ("poolw", KW * P), ("inv", KW * PC),
                    ("modT", 16 * NV), ("psums", KW * NS), ("dsums", KW * NS), ("stats", 16),
                    ("tail_b", KW * 10), ("tail_p", KW * 23), ("smp", 2 * NS)):
        where[name] = (at, at + n)
        at += n
    return where, at


COLS, SMALL = columns()
LOADED = COLS["modT"][0]


def early_columns():
    at, where = 0, {}
    for name, n in (("wv", KD * W), ("st_d", KW * NS * (CD - 1)), ("st_p", KW * NS * PC), ("alg", W),
                    ("alb", W), ("aws", KW * P), ("abs", KW * P), ("vs", W)):
        where[name] = (at, at + n)
        at += n
    return where, at


ECOLS, EARLY = early_columns()
EARLY_LOADED = ECOLS["vs"][0]
R3 = dict(ident=(0, P), ones=(P, 2 * P), tri=(2 * P, 3 * P), iota=(3 * P, 3 * P + NE),
          thr=(416, 425), biota=(425, 425 + BLOCKS), pair=(475, 499), br=(499, 535), wr=(535, 535 + KD * 36))
R3W = 535 + KD * 36


class Steps:

    def __init__(self, eng, sem):
        self.eng, self.sem, self.n = eng, sem, 0

    def link(self, ins):
        ins.then_inc(self.sem, 1)
        self.n = self.n + 1
        self.eng.wait_ge(self.sem, self.n)

    def loop(self, i, first, per):
        self.base, self.first, self.per = self.n, first, per
        self.n = (i - first) * per + self.base

    def done(self, turns):
        self.n = self.base + turns * self.per


def evacuated(q):
    n = (6 if q % 2 == 0 else 4) + q // 2
    if q >= Q0["C"]:
        n += 1 + min(2, (q - Q0["C"]) // 2)
    return n


def build(nc, A, O):
    ctx = ExitStack()
    with ctx:
        def sem(name):
            return ctx.enter_context(nc.semaphore(name))

        sm = ctx.enter_context(nc.sbuf_tensor("sm", [P, SMALL], F32))
        with ExitStack() as c0:
            h_area = c0.enter_context(nc.sbuf_tensor("h_area", [P, 2, KD * T], F32))
            c0.enter_context(nc.sbuf_tensor("below_w_lo", [P, 2 * KW * T + 4 * KD * P], F32))
            mod_const = c0.enter_context(nc.sbuf_tensor("mod_rows_const", [P, 4, 512], F32))
        with ExitStack() as ch:
            h_hi = ch.enter_context(nc.sbuf_tensor("h_hi", [P, KD, T], F32R))
            h_lo = ch.enter_context(nc.sbuf_tensor("h_lo", [P, KD, T], F32R))
            with ExitStack() as c1:
                y_hi = c1.enter_context(nc.sbuf_tensor("y_hi", [P, KW * T], F32R))
                y_lo = c1.enter_context(nc.sbuf_tensor("y_lo", [P, KW * T], F32R))
                raw = c1.enter_context(nc.sbuf_tensor("raw", [P, 2, KD * P], F32))
                w_hi = c1.enter_context(nc.sbuf_tensor("w_hi", [P, 2, KD, P], F32R))
                w_lo = c1.enter_context(nc.sbuf_tensor("w_lo", [P, 2, KD, P], F32R))
                G = c1.enter_context(nc.sbuf_tensor("G", [P, KW * GLW + KW * T], F32))
                S = c1.enter_context(nc.sbuf_tensor("S", [P, 3 * SW], F32))
                zeros = c1.enter_context(nc.sbuf_tensor("zeros", [P, 512], F32))
                m = c1.enter_context(nc.sbuf_tensor("m", [P, KD * T], F32))
            with ExitStack() as c2:
                wo_hi = c2.enter_context(nc.sbuf_tensor("wo_hi", [P, KD, D], F32R))
                wo_lo = c2.enter_context(nc.sbuf_tensor("wo_lo", [P, KD, D], F32R))
                wo_raw = c2.enter_context(nc.sbuf_tensor("wo_raw", [P, 2, D], F32))
                xt = c2.enter_context(nc.sbuf_tensor("xt", [P, 2, D], F32))
                h2 = c2.enter_context(nc.sbuf_tensor("h2", [P, 2, D], F32))
                h2T = c2.enter_context(nc.sbuf_tensor("h2T", [P, KD, P], F32))
                sq = c2.enter_context(nc.sbuf_tensor("sq", [P, D], F32))
                rows = c2.enter_context(nc.sbuf_tensor("rows", [P, 3, D], F32))
                rows_s = c2.enter_context(nc.sbuf_tensor("rows_s", [P, 3, D], F32))
                r3 = c2.enter_context(nc.sbuf_tensor("r3", [P, R3W], F32))
                MK = c2.enter_context(nc.sbuf_tensor("MK", [P, 3, TILES * NE], F32))
                rt = c2.enter_context(nc.sbuf_tensor("rt", [P, 160], F32))
                ri = c2.enter_context(nc.sbuf_tensor("ri", [P, 16], U32))
                wts = c2.enter_context(nc.sbuf_tensor("wts", [P, 2, TILES], F32))
                slots = c2.enter_context(nc.sbuf_tensor("slots", [P, 2 * TILES], I32))
                tokid = c2.enter_context(nc.sbuf_tensor("tok_ids", [P, TILES], I32))
                zero_ids = c2.enter_context(nc.sbuf_tensor("zero_ids", [P, BLOCKS], I32))
                table = c2.enter_context(nc.sbuf_tensor("table", [P, BLOCKS], I32))
                block_e = c2.enter_context(nc.sbuf_tensor("block_e", [P, BLOCKS + 2], I32))
                cmp_ = c2.enter_context(nc.sbuf_tensor("cmp", [P, BLOCKS * NE], F32))
        with ExitStack() as c3:
            we = c3.enter_context(nc.sbuf_tensor("we", [P, 2, EW], F32))
            xg = c3.enter_context(nc.sbuf_tensor("xg", [P, 2, D], F32))
            xgT = c3.enter_context(nc.sbuf_tensor("xgT", [P, 2, KD, P], F32))
            idx = c3.enter_context(nc.sbuf_tensor("idx", [P, 2], I32))
            sg = c3.enter_context(nc.sbuf_tensor("sg", [P, FE], F32))
            hm = c3.enter_context(nc.sbuf_tensor("hm", [P, FE], F32))
            hmT = c3.enter_context(nc.sbuf_tensor("hmT", [P, 2, P], F32))
            yb = c3.enter_context(nc.sbuf_tensor("yb", [P, 2, D], F32))
            g2r = c3.enter_context(nc.sbuf_tensor("g2r", [P, 2, D], F32))
            fg = c3.enter_context(nc.sbuf_tensor("fg", [P, D], F32))
            x1 = c3.enter_context(nc.sbuf_tensor("x1", [P, YB, D], F32))
            cs = c3.enter_context(nc.sbuf_tensor("cs", [P, 8], F32))
        ps = ctx.enter_context(nc.psum_tensor("ps", [P, 8, 512], F32))

        def c(name):
            a, b = COLS[name]
            return sm[:, a:b]

        def e(name):
            a, b = ECOLS[name]
            return m[:, a:b]

        h_f = h_area[:, 1, :].rearrange("p (k t) -> p k t", k=KD)
        ident, ones = c("ident"), c("ones")
        cT = c("cT").rearrange("p (k v) -> p k v", k=KD)
        modT = c("modT").rearrange("p (n v) -> p n v", n=16)
        mod_rows = [S[:, at:at + 512] for at in (SW, SW + 512, 2 * SW + 512)]
        xT = G[:, 0:KD * T].rearrange("p (k t) -> p k t", k=KD)
        gl = G[:, 0:KW * GLW].rearrange("p (c t) -> p c t", c=KW)
        dc = G[:, KW * GLW:].rearrange("p (c t) -> p c t", c=KW)
        vn = G[:, KW * GLW:KW * GLW + 8 * W].rearrange("p (n c) -> p n c", n=8)
        mm = m[:, :].rearrange("p (k t) -> p k t", k=KD)
        yh = y_hi[:, :].rearrange("p (c t) -> p c t", c=KW)
        yl = y_lo[:, :].rearrange("p (c t) -> p c t", c=KW)
        yh3 = y_hi[:, :].rearrange("p (c a t) -> p c a t", c=KW, a=NT)
        yl3 = y_lo[:, :].rearrange("p (c a t) -> p c a t", c=KW, a=NT)
        h3h = h_hi[:, :, :].rearrange("p k (a t) -> p k a t", a=NT)
        h3l = h_lo[:, :, :].rearrange("p k (a t) -> p k a t", a=NT)
        wvh = y_hi[:, 0:KD * W].rearrange("p (k n) -> p k n", k=KD)
        wvl = y_lo[:, 0:KD * W].rearrange("p (k n) -> p k n", k=KD)
        slab = [mem[:, at:at + SLAB] for mem, at in [(h_area[:, j // 4, :], j % 4 * SLAB) for j in range(8)]
                + [(G, 0), (G, SLAB), (m, 0), (m, SLAB)] * 4]
        st = c("stats")
        cbw = c("cbw").rearrange("p (l c) -> p l c", l=3)
        cdw = c("cdw").rearrange("p (c l) -> p c l", c=KW)
        st_b = c("st_b").rearrange("p (c b l) -> p c b l", c=KW, b=NS)
        st_d = e("st_d").rearrange("p (c b l) -> p c b l", c=KW, b=NS)
        st_p = e("st_p").rearrange("p (c b l) -> p c b l", c=KW, b=NS)
        psums = c("psums").rearrange("p (c b) -> p c b", c=KW)
        dsums = c("dsums").rearrange("p (c b) -> p c b", c=KW)
        poolw = c("poolw").rearrange("p (c n) -> p c n", c=KW)
        inv = c("inv").rearrange("p (c n) -> p c n", c=KW)
        aws = e("aws").rearrange("p (g t) -> p g t", g=KW)
        abs_ = e("abs").rearrange("p (g t) -> p g t", g=KW)
        tail_b = c("tail_b").rearrange("p (c n) -> p c n", c=KW)
        tail_p = c("tail_p").rearrange("p (c n) -> p c n", c=KW)
        smp = c("smp").rearrange("p (a n) -> p a n", a=2)

        def sbf(n, off=0, width=T):
            return S[:, n * SW + off:n * SW + off + width]

        def ln_row(n):
            return G[:, (n % KW) * T:(n % KW + 1) * T]

        def three(ap):
            return ap.rearrange("p (a t) -> p a t", a=NT)

        def pset(s):
            return ps[:, 3 * s:3 * s + 3, 0:TT]

        small_in = sem("small_in")
        idx_in = [sem("idx_in0"), sem("idx_in1")]
        zeros_ready, y_zero = sem("zeros_ready"), sem("y_zero")
        x_in = sem("x_in")
        early_in = sem("early_in")
        wv_in = sem("wv_in")
        slab_in = [sem("slab_in%d" % j) for j in range(8)]
        slab_used = sem("slab_used")
        mod_ready = sem("mod_ready")
        mod_turned = sem("mod_turned")
        mod_stored = sem("mod_stored")
        const_in = sem("const_in")
        scaled = sem("scaled")
        sq_ready = sem("sq_ready")
        sq_added = sem("sq_added")
        sq_prod = sem("sq_prod")
        rstd_in = sem("rstd_in")
        rstd_ready = sem("rstd_ready")
        h_f32 = sem("h_f32")
        h_hi_done = sem("h_hi_done")
        h_lo_done = sem("h_lo_done")
        wv_hi = sem("wv_hi")
        wv_lo = sem("wv_lo")
        v_prod = sem("v_prod")
        v_act = sem("v_act")
        v_dve = sem("v_dve")
        v_done = sem("v_done")
        masked = sem("masked")
        gap_zero = sem("gap_zero")
        raw_in = sem("raw_in")
        hi_done = sem("hi_done")
        lo_done = sem("lo_done")
        grp = sem("grp")
        evac = [sem("evac0"), sem("evac1")]
        gate_prod = sem("gate_prod")
        gate_read = sem("gate_read")
        y_done = sem("y_done")
        y_f32 = sem("y_f32")
        pooled = sem("pooled")
        pool_prod = sem("pool_prod")
        ln_sq = sem("ln_sq")
        ln_prod = sem("ln_prod")
        ln_mean = sem("ln_mean")
        ln_in = sem("ln_in")
        ln_rstd = sem("ln_rstd")
        ln_y = sem("ln_y")
        ln_norm = sem("ln_norm")
        ln_lo = sem("ln_lo")
        dve_step = sem("dve_step")
        stored = sem("stored")
        tails_b = sem("tails_b")
        tails_p = sem("tails_p")
        m_ready = sem("m_ready")
        m_hi_done, m_lo_done = sem("m_hi_done"), sem("m_lo_done")
        wo_in = [sem("wo_in0"), sem("wo_in1")]
        wo_hi_done, wo_lo_done = sem("wo_hi_done"), sem("wo_lo_done")
        r3_in = sem("r3_in")
        rows_in = sem("rows_in")
        xt_in = [sem("xt_in0"), sem("xt_in1")]
        o_prod = sem("o_prod")
        o_read = sem("o_read")
        x1_done = sem("x1_done")
        x1_out = [sem("x1_out0"), sem("x1_out1")]
        x1_sq = sem("x1_sq")
        x1_var = sem("x1_var")
        x1_rstd = sem("x1_rstd")
        h2_done = sem("h2_done")
        h2_out = [sem("h2_out0"), sem("h2_out1")]
        h2_turned = sem("h2_turned")
        h2T_done = sem("h2T_done")
        logit_prod = sem("logit_prod")
        logit_read = sem("logit_read")
        gexp_in, gexp_done = sem("gexp_in"), sem("gexp_done")
        eexp_in, eexp_done = sem("eexp_in"), sem("eexp_done")
        mask_done = sem("mask_done")
        rank_prod = sem("rank_prod")
        slots_done = sem("slots_done")
        table_zero = sem("table_zero")
        ids_done = sem("ids_done")
        table_out = sem("table_out")
        table_in = sem("table_in")
        idx_done = sem("idx_done")
        xg_in = [sem("xg_in0"), sem("xg_in1")]
        wd_in = [sem("wd_in0"), sem("wd_in1")]
        we_in = [sem("we_in0"), sem("we_in1")]
        turned, xgT_done, gu_prod, silu_done, hm_done = (sem(n) for n in ("turned", "xgT_done", "gu_prod", "silu_done", "hm_done"))
        hm_turned, hmT_done, y_prod, y_copied = (sem(n) for n in ("hm_turned", "hmT_done", "y_prod", "y_copied"))
        y_out = [sem("y_out0"), sem("y_out1")]
        gathers = sem("gathers")
        fg_in = sem("fg_in")
        g2_in = sem("g2_in")
        y1_in = [sem("y1_in%d" % j) for j in range(YB)]
        y2_in = [sem("y2_in%d" % j) for j in range(YB)]
        x1_in = [sem("x1_in%d" % j) for j in range(YB)]
        y1_scaled = sem("y1_scaled")
        c_sq_in, c_sq = sem("c_sq_in"), sem("c_sq")
        c_var, c_rstd = sem("c_var"), sem("c_rstd")
        c_done = sem("c_done")
        out_st = [sem("out_st%d" % j) for j in range(YB)]
        y12 = we[:, :, :].rearrange("p a n -> p (a n)").rearrange("p (t c n) -> p t c n", t=YB, c=2)

        modd = nc.dram_tensor("mod_scratch", (2, P, 512), F32).ap()
        x1d = nc.dram_tensor("x1_scratch", (T, D), F32).ap()
        h2d = nc.dram_tensor("h2_scratch", (T, D), F32).ap()
        tabd = nc.dram_tensor("table_scratch", (BLOCKS * P, 1), I32).ap()
        yd = nc.dram_tensor("y_scratch", (BLOCKS * P, D), F32).ap()

        def tile_rows(t):
            return (t * P, P) if t < TILES - 1 else (LP, NS)

        def r(name):
            a, b = R3[name] if name in R3 else None
            return r3[:, a:b]

        def send(sp, t):
            at, n = tile_rows(t)
            sp.wait_ge(c_done, t + 1)
            sp.dma_start(O["y"][at:at + n, :], x1[0:n, t % YB, :]).then_inc(out_st[t % YB], 16)

        def load_x1(sp, t):
            at, n = tile_rows(t)
            sp.dma_start(x1[0:n, t % YB, :], x1d[at:at + n, :]).then_inc(x1_in[t % YB], 16)

        def load_rows(sp, dst, dst_s, vec, done):
            by_vector = modd.rearrange("s (j v) n -> s v j n", v=32)
            halves = slice(2 * (vec % 2), 2 * (vec % 2) + 2)
            two_ = lambda ap: ap.rearrange("p (a n) -> p a n", a=2)
            sp.dma_start(two_(dst), by_vector[vec // 2, 0, halves, :].partition_broadcast(P)).then_inc(done, 16)
            sp.dma_start(two_(dst_s), by_vector[vec // 2, 1:NV, halves, :]).then_inc(done, 16)

        def pooled_in(ch):
            return 2 if ch % 2 == 0 else 1

        block = ctx.enter_context(nc.Block())

        @block.sync
        def _(sp):
            sp.dma_start(sm[:, 0:LOADED], A["small"]).then_inc(small_in, 16)

            def load_slab(j):
                sp.dma_start(slab[j], A["w_mod"][j]).then_inc(slab_in[j if j < 8 else j % 4], 16)

            sp.dma_start(xT, A["xT"]).then_inc(x_in, 16)
            for j in range(8):
                load_slab(j)
                if j == 6:
                    sp.dma_start(mod_const[:, :, :], A["mod_const"].rearrange("p (s n) -> p s n", s=4)).then_inc(const_in, 16)
            rawf = raw[:, :, :].rearrange("p a n -> p (a n)")
            sp.dma_start(m[:, 0:KD * W], A["early"][:, 0:KD * W]).then_inc(wv_in, 16)
            sp.dma_start(m[:, KD * W:EARLY_LOADED], A["early"][:, KD * W:]).then_inc(early_in, 16)
            sp.dma_start(rawf, A["w_mix"][0]).then_inc(raw_in, 16)
            for j in range(8, 24):
                if j == 8:
                    sp.wait_ge(h_lo_done, KD)
                elif j == 10:
                    sp.wait_ge(wv_lo, 2)
                elif j >= 12:
                    sp.wait_ge(slab_used, j - 3)
                load_slab(j)
            sp.wait_ge(zeros_ready, 1)
            sp.dma_start(O["keep_b"], A["state_b"][:, 1:2, :]).then_inc(stored, 16)
            sp.dma_start(O["keep_p"], A["state_p"][:, 1:PC, :]).then_inc(stored, 16)
            sp.dma_start(O["keep_d"], A["state_d"][:, 1:CD - 1, :]).then_inc(stored, 16)

            pair, gpair = 0, 0
            for name in ("D", "A", "gA", "B", "gB", "C", "gC", "gD"):
                n = MIX_PAIRS.get(name, KD)
                src, at = (A["w_mix"], pair) if name in MIX_PAIRS else (A["w_gate"], gpair)
                q0 = Q0[name]
                width = src.shape[2]
                with sp.Fori(1 if name == "D" else 0, n) as i:
                    sp.wait_ge(hi_done, q0 + 2 * i)
                    sp.wait_ge(lo_done, q0 + 2 * i)
                    sp.dma_start(rawf[:, 0:width], src[bass.ds(at + i, 1)].rearrange("o p n -> (o p) n")
                                 ).then_inc(raw_in, 16)
                    if name not in MIX_PAIRS:
                        for a in range(2):
                            sp.dma_start(yd[bass.ds((i + (MIN_BLOCKS + gpair)) * P, P), a * 512:(a + 1) * 512],
                                         zeros[:, :]).then_inc(y_zero, 16)
                if name in MIX_PAIRS:
                    pair += n
                else:
                    gpair += n
                if name == "D":
                    for s in range(2):
                        sp.wait_ge(mod_ready, s + 2)
                        sp.dma_start(modd[s], mod_rows[s + 1]).then_inc(mod_stored, 16)
                    sp.wait_ge(v_done, TILES)
                    sp.dma_start(O["v_s"], e("vs")[0:NS, :]).then_inc(stored, 16)
                if name == "gA":
                    sp.wait_ge(evac[0], evacuated(8))
                    sp.dma_start(O["tail_d"], gl[:, :, LP:LP + CD - 1 + NS]).then_inc(stored, 16)
            sp.wait_ge(tails_b, 1)
            sp.dma_start(O["tail_b"], tail_b).then_inc(stored, 16)
            sp.wait_ge(tails_p, 1)
            sp.dma_start(O["tail_p"], tail_p).then_inc(stored, 16)

            sp.wait_ge(evac[1], evacuated(N_GROUPS - 1) + 1)
            sp.wait_ge(grp, N_GROUPS)
            sp.wait_ge(stored, 16 * 7)

            def load_wo(i, s):
                sp.dma_start(wo_raw[:, s, :], A["w_out"][:, bass.ds(2 * i + s, 1), :].rearrange("p o n -> p (o n)")
                             ).then_inc(wo_in[s], 16)

            def load_x(t, s):
                at, n = t * P, P
                sp.dma_start(xt[:, s, :], A["x_tok"][bass.ds(at, n), :]).then_inc(xt_in[s], 16)

            for s in range(2):
                load_wo(0, s)
            with sp.Fori(1, KD // 2) as i:
                for s in range(2):
                    sp.wait_ge(wo_hi_done, 2 * i + s - 1)
                    sp.wait_ge(wo_lo_done, 2 * i + s - 1)
                    load_wo(i, s)
            load_x(0, 0)
            load_x(1, 1)
            sp.wait_ge(m_lo_done, KD)
            sp.wait_ge(m_hi_done, KD)
            sp.wait_ge(y_zero, 16 * 2 * (BLOCKS - MIN_BLOCKS))
            sp.wait_ge(mod_stored, 32)
            for j, vec in enumerate((0, 2, 1)):
                load_rows(sp, rows[:, j, :], rows_s[0:NS, j, :], vec, rows_in)
            sp.dma_start(r3[:, :], A["routing"]).then_inc(r3_in, 16)
            sp.dma_start(tokid[:, :], A["tokid"]).then_inc(r3_in, 16)
            sp.wait_ge(table_zero, 1)
            sp.dma_start(tabd.rearrange("(p b) o -> p (b o)", p=P), zero_ids[:, :]).then_inc(table_out, 16)
            for t in range(TILES):
                at, n = tile_rows(t)
                sp.wait_ge(x1_done, t + 1)
                sp.dma_start(x1d[at:at + n, :], xt[0:n, t % 2, :]).then_inc(x1_out[t % 2], 16)
                sp.wait_ge(h2_done, t + 1)
                sp.dma_start(h2d[at:at + n, :], h2[0:n, t % 2, :]).then_inc(h2_out[t % 2], 16)
                if t + 2 < TILES:
                    sp.wait_ge(x1_out[t % 2], 16 * (t // 2 + 1))
                    n2 = tile_rows(t + 2)[1]
                    sp.dma_start(xt[0:n2, t % 2, :], A["x_tok"][(t + 2) * P:(t + 2) * P + n2, :]
                                 ).then_inc(xt_in[t % 2], 16)

            sp.wait_ge(slots_done, 1)
            sp.wait_ge(rank_prod, 1)
            sp.wait_ge(x1_out[0], 16 * 5)
            sp.wait_ge(x1_out[1], 16 * 4)
            sp.wait_ge(h2_out[0], 16 * 5)
            sp.wait_ge(h2_out[1], 16 * 4)
            rest = sp.value_load(block_e[0:1, BLOCKS:BLOCKS + 1], min_val=0, max_val=NPAIR - 1)

            def load_experts(i, s, wait):
                ex = sp.value_load(block_e[0:1, bass.ds(2 * i + s, 1)], min_val=0, max_val=NE - 1)
                if wait:
                    sp.wait_ge(gu_prod, 2 * i + s - 1)
                sp.dma_start(we[:, s, 0:GUW], A["w_exp"][bass.ds(ex, 1), :, 0:GUW].rearrange("o p n -> (o p) n")
                             ).then_inc(we_in[s], 16)
                if wait:
                    sp.wait_ge(y_prod, 2 * i + s - 1)
                sp.dma_start(we[:, s, GUW:], A["w_exp"][bass.ds(ex, 1), :, GUW:].rearrange("o p n -> (o p) n")
                             ).then_inc(wd_in[s], 16)

            for s in range(2):
                load_experts(0, s, False)
            load_rows(sp, g2r[:, 0, :], g2r[0:NS, 1, :], 3, g2_in)
            sp.dma_start(fg[:, :], A["final_g"]).then_inc(fg_in, 16)
            for t in range(YB):
                load_x1(sp, t)
            with sp.Fori(1, NPAIR) as i:
                with sp.If(i < rest + 1):
                    for s in range(2):
                        load_experts(i, s, True)
            for t in range(TILES):
                send(sp, t)
                if t >= 1 and t + YB - 1 < TILES:
                    sp.wait_ge(out_st[t - 1], 16)
                    load_x1(sp, t + YB - 1)
            for j in range(YB):
                sp.wait_ge(out_st[j], 16 * (2 if j + YB < TILES else 1))
            sp.wait_ge(stored, 16 * 7)

        @block.tensor
        def _(pe):
            pe.wait_ge(small_in, 16)
            def mod_slab(j):
                pe.wait_ge(slab_in[j if j < 8 else j % 4], 16 if j < 8 else 16 * (j // 4))
                k = j % KD
                for q in range(4):
                    mmi = pe.matmul(ps[32 * q:32 * q + 32, 7 if j // KD == 2 else 6, :], cT[:, k, :],
                                    slab[j][:, q * 512:(q + 1) * 512], start=(k == 0), stop=(k == KD - 1))
                mmi.then_inc(slab_used, 1)

            for j in range(8):
                mod_slab(j)
                if j == 3:
                    pe.wait_ge(sq_added, KD - 1)
                    for a in range(NT):
                        mmi = pe.matmul(ps[:, a, 0:TT], ones, sbf(2, a * TT, TT), start=True, stop=True)
                    mmi.then_inc(sq_prod, 1)
            pe.wait_ge(mod_ready, 1)
            for n in range(4):
                mmi = pe.transpose(ps[:, 7, n * P:(n + 1) * P], mod_rows[0][:, n * P:(n + 1) * P], ident)
            mmi.then_inc(mod_turned, 1)
            for t in range(TILES):
                at, n = tile_rows(t)
                if t == 0:
                    pe.wait_ge(evac[0], 1)
                elif t > 1:
                    pe.wait_ge(evac[t % 2], (1 if t % 2 == 0 else 0) + t // 2)
                for k in range(KD):
                    if t == 0:
                        pe.wait_ge(wv_lo, 1 + k // 4)
                        pe.wait_ge(h_lo_done, k + 1)
                    for x, (l, w) in enumerate(((h_hi, wvh), (h_hi, wvl), (h_lo, wvh))):
                        mmi = pe.matmul(ps[0:n, 3 * (t % 2), :], l[:, k, at:at + n], w[:, k, :],
                                        start=(k == 0 and x == 0), stop=(k == KD - 1 and x == 2))
                mmi.then_inc(v_prod, 1)
                if t < 8:
                    mod_slab(8 + 2 * t)
                    mod_slab(9 + 2 * t)

            def group(q, s, before, rh, rl, nk):
                pe.wait_ge(hi_done, q + 1)
                pe.wait_ge(lo_done, q + 1)
                pe.wait_ge(evac[s], before)
                for k in range(nk):
                    for x, (w, rr) in enumerate(((w_hi, rh), (w_hi, rl), (w_lo, rh))):
                        for a in range(NT):
                            mmi = pe.matmul(ps[:, 3 * s + a, 0:TT], w[:, s, k, :], rr[:, k, a, :],
                                            start=(k == 0 and x == 0), stop=(k == nk - 1 and x == 2))
                mmi.then_inc(grp, 1)

            def pairs_of(name, first=0):
                q0 = Q0[name]
                gates = name[0] == "g"
                with pe.Fori(first, MIX_PAIRS.get(name, KD)) as i:
                    group(q0 + 2 * i, 0, evacuated(q0) + i, h3h, h3l, KD)
                    if gates:
                        pe.wait_ge(y_done, KW * (1 + "ABCD".index(name[1])))
                        group(q0 + 2 * i + 1, 1, evacuated(q0 + 1) + i, yh3, yl3, KW)
                    else:
                        group(q0 + 2 * i + 1, 1, evacuated(q0 + 1) + i, h3h, h3l, KD)

            pairs_of("D")
            pe.wait_ge(masked, 1)
            pe.wait_ge(v_done, TILES)
            pe.wait_ge(mod_ready, 3)
            for g in range(KW):
                q, s = Q0["A"] + g, g % 2
                if g:
                    pe.wait_ge(gate_read, g)
                for n in range(8):
                    pe.matmul(ps[:, 6 + n // 4, (n % 4) * P:(n % 4 + 1) * P], vn[:, n, g * P:(g + 1) * P],
                              aws[:, g, :], start=True, stop=True)
                pe.wait_ge(evac[s], evacuated(q))
                pe.matmul(ps[:, 3 * s, 400:400 + NS], e("vs")[0:NS, g * P:(g + 1) * P], ident[0:NS, 0:NS],
                          start=True, stop=True).then_inc(gate_prod, 1)
                group(q, s, evacuated(q), h3h, h3l, KD)
            pairs_of("gA")
            pairs_of("B")
            pairs_of("gB")

            def pool_mix(ch):
                s = ch % 2
                pe.wait_ge(pooled, ch + 1)
                for a in range(NT):
                    mmi = pe.matmul(ps[:, 3 * s + a, 0:TT], poolw[:, ch, :],
                                    sbf(pooled_in(ch), PC + a * TT, TT), start=True, stop=True)
                mmi.then_inc(pool_prod, 1)

            def ln_sums(which):
                pe.wait_ge(evac[which], evacuated(Q0["C"] + which) - 1)
                for ch in range(KW):
                    if which == 1:
                        pe.wait_ge(ln_sq, ch + 1)
                    elif ch == 0:
                        pe.wait_ge(ln_in, 1)
                    for a in range(NT):
                        rhs = dc[:, ch, a * TT:(a + 1) * TT] if which == 0 else ln_row(ch + 1)[:, a * TT:(a + 1) * TT]
                        mmi = pe.matmul(ps[:, 3 * which + a, 0:TT], ones, rhs, start=(ch == 0), stop=(ch == KW - 1))
                    mmi.then_inc(ln_prod, 1)

            for ch in range(KW):
                q = Q0["C"] + ch
                if ch < 2:
                    ln_sums(ch)
                if ch == 2:
                    pool_mix(0)
                if ch == 3:
                    pool_mix(1)
                group(q, ch % 2, evacuated(q), h3h, h3l, KD)
            pool_mix(2)
            group(Q0["gC"], 0, evacuated(Q0["gC"]), h3h, h3l, KD)
            pool_mix(3)
            pe.wait_ge(y_done, 3 * KW)
            group(Q0["gC"] + 1, 1, evacuated(Q0["gC"] + 1), yh3, yl3, KW)
            pairs_of("gC", 1)
            pairs_of("gD")

            pe.wait_ge(r3_in, 32)
            pe.wait_ge(wo_hi_done, KD)
            pe.wait_ge(wo_lo_done, KD)
            pe.wait_ge(m_hi_done, KD)
            pe.wait_ge(m_lo_done, KD)

            def project(t):
                at, n = tile_rows(t)
                b = 2 * (t % 2)
                if t < 2:
                    pe.wait_ge(evac[t], evacuated(N_GROUPS - 2 + t) + 1)
                else:
                    pe.wait_ge(o_read, t - 1)
                for k in range(KD):
                    for x, (l, w) in enumerate(((h_hi, wo_hi), (h_hi, wo_lo), (h_lo, wo_hi))):
                        for a in range(2):
                            mmi = pe.matmul(ps[0:n, b + a, :], l[:, k, at:at + n], w[:, k, a * 512:(a + 1) * 512],
                                            start=(k == 0 and x == 0), stop=(k == KD - 1 and x == 2))
                mmi.then_inc(o_prod, 1)

            def turn_h2(t):
                at, n = tile_rows(t)
                pe.wait_ge(h2_done, t + 1)
                if t:
                    pe.wait_ge(h2T_done, t)
                for k in range(KD):
                    mmi = pe.transpose(ps[:, 4 + k // 4, (k % 4) * P:(k % 4) * P + n],
                                       h2[0:n, t % 2, k * P:(k + 1) * P], ident[0:n, 0:n])
                mmi.then_inc(h2_turned, 1)

            def logits(t):
                at, n = tile_rows(t)
                pe.wait_ge(h2T_done, t + 1)
                if t:
                    pe.wait_ge(logit_read, t)
                for k in range(KD):
                    mmi = pe.matmul(ps[0:n, 6, 0:36], h2T[:, k, 0:n], r("wr").rearrange("p (k n) -> p k n", k=KD)[:, k, :],
                                    start=(k == 0), stop=(k == KD - 1))
                mmi.then_inc(logit_prod, 1)

            for t in range(TILES + 2):
                if t < TILES:
                    project(t)
                if t > 1:
                    logits(t - 2)
                if 0 < t <= TILES:
                    turn_h2(t - 1)
            pe.wait_ge(mask_done, TILES)
            MS = MK[:, 2, :].rearrange("p (t e) -> p t e", t=TILES)
            for t in range(TILES + 1):
                for u in range(min(t + 1, TILES)):
                    last = u == min(t, TILES - 1)
                    mmi = pe.matmul(ps[:, 7, t * NE:(t + 1) * NE], r("tri") if u == t else ones, MS[:, u, :],
                                    start=(u == 0), stop=last)
            mmi.then_inc(rank_prod, 1)

            pe.wait_ge(slots_done, 1)
            rest = pe.value_load(block_e[0:1, BLOCKS:BLOCKS + 1], min_val=0, max_val=NPAIR - 1)

            def turn(i, s, first=False):
                b = 2 * i + s
                pe.wait_ge(xg_in[s], 16 * (i + 1))
                if not first:
                    pe.wait_ge(xgT_done, b)
                for k in range(KD):
                    mmi = pe.transpose(ps[:, k // 4, (k % 4) * P:(k % 4 + 1) * P], xg[:, s, k * P:(k + 1) * P], ident)
                mmi.then_inc(turned, 1)

            def turn_hidden(b):
                pe.wait_ge(hm_done, b + 1)
                for f in range(2):
                    mmi = pe.transpose(ps[:, 4, f * P:(f + 1) * P], hm[:, f * P:(f + 1) * P], ident)
                mmi.then_inc(hm_turned, 1)

            def gate_up(i, s):
                b = 2 * i + s
                pe.wait_ge(we_in[s], 16 * (i + 1))
                pe.wait_ge(xgT_done, b + 1)
                wv = we[:, s, 0:KD * 2 * FE].rearrange("p (k n) -> p k n", k=KD)
                for k in range(KD):
                    mmi = pe.matmul(ps[:, 2 + s, :], xgT[:, s, k, :], wv[:, k, :], start=(k == 0), stop=(k == KD - 1))
                mmi.then_inc(gu_prod, 1)

            def down(b, i, s, first=False):
                pe.wait_ge(wd_in[s], 16 * (i + 1))
                pe.wait_ge(hmT_done, b + 1)
                if not first:
                    pe.wait_ge(y_copied, b)
                wv = we[:, s, KD * 2 * FE:].rearrange("p (f n) -> p f n", f=2)
                for a in range(2):
                    for f in range(2):
                        mmi = pe.matmul(ps[:, 5 + a, :], hmT[:, f, :], wv[:, f, a * 512:(a + 1) * 512],
                                        start=(f == 0), stop=(f == 1))
                mmi.then_inc(y_prod, 1)

            turn(0, 0, first=True)
            turn(0, 1)
            gate_up(0, 0)
            turn(1, 0)
            turn_hidden(0)
            gate_up(0, 1)
            down(0, 0, 0, first=True)
            with pe.Fori(1, NPAIR) as i:
                with pe.If(i < rest + 1):
                    for s in range(2):
                        turn(i + s, 1 - s)
                        turn_hidden(2 * i + s - 1)
                        gate_up(i, s)
                        down(2 * i + s - 1, i + s - 1, 1 - s)
            turn_hidden(2 * rest + 1)
            down(2 * rest + 1, rest, 1)

        @block.scalar
        def _(act):
            act.wait_ge(x_in, 16)
            act.wait_ge(small_in, 16)
            for k in range(KD):
                if k >= 2:
                    act.wait_ge(sq_added, max(1, k - 2))
                act.activation(sbf(k % 2), xT[:, k, :], ACT.Square).then_inc(sq_ready, 1)
            act.wait_ge(rstd_in, 1)
            act.activation(sbf(0), sbf(0), ACT.Sqrt).then_inc(rstd_ready, 1)
            act.wait_ge(h_f32, 1)
            act.activation(h_hi[:, :, LP:T], h_f[:, :, LP:T], ACT.Copy).then_inc(h_hi_done, 1)
            for k in range(KD):
                act.activation(h_hi[:, k, 0:LP], xT[:, k, 0:LP], ACT.Identity, bias=modT[:, k, 0:1],
                               scale=modT[:, 8 + k, 0:1]).then_inc(h_hi_done, 1)
                if k in (2, 5):
                    half = slice((k // 3) * KD * W // 2, (k // 3 + 1) * KD * W // 2)
                    act.wait_ge(wv_in, 16)
                    act.activation(y_hi[:, half], e("wv")[:, half], ACT.Copy).then_inc(wv_hi, 1)
            def split_hi(pr, s, wait=True):
                act.wait_ge(raw_in, 16 * (pr + 1))
                if wait:
                    act.wait_ge(grp, 2 * pr + s - 1)
                act.activation(w_hi[:, s, :, :].rearrange("p k n -> p (k n)"), raw[:, s, :], ACT.Copy
                               ).then_inc(hi_done, 1)

            for t in range(TILES):
                n, s = tile_rows(t)[1], t % 2
                act.wait_ge(v_prod, t + 1)
                if t >= 2:
                    act.wait_ge(v_done, t - 1)
                if t == 2:
                    split_hi(0, 0, False)
                    split_hi(0, 1, False)
                act.activation(sbf(s, 0, W)[0:n], ps[0:n, 3 * s, :], ACT.Gelu_apprx_tanh,
                               accum_out=st[0:n, 4 * s:4 * s + 1]).then_inc(evac[s], 1)
                act.wait_ge(v_dve, 2 * t + 1)
                act.activation(sbf(2, 0, W)[0:n], sbf(s, 0, W)[0:n], ACT.Square,
                               accum_out=st[0:n, 4 * s + 1:4 * s + 2]).then_inc(v_act, 1)
                act.wait_ge(v_dve, 2 * t + 2)
                act.activation(st[0:n, 4 * s + 2:4 * s + 3], st[0:n, 4 * s + 2:4 * s + 3], ACT.Sqrt).then_inc(v_act, 1)

            act.wait_ge(v_done, TILES)

            with act.Fori(0, 4) as i:
                split_hi(i + 1, 0)
                act.wait_ge(grp, 2 * i + 2)
                act.wait_ge(evac[0], evacuated(0) + i)
                act.activation(three(sbf(0)), pset(1), ACT.Sigmoid).then_inc(evac[1], 1)
                split_hi(i + 1, 1)
            for g in range(KW):
                q, s = Q0["A"] + g, g % 2
                act.wait_ge(grp, q + 1)
                if g < 2:
                    act.wait_ge(evac[0], evacuated(6) + 1)
                else:
                    act.wait_ge(y_done, g - 1)
                act.activation(smp[:, s, :], ps[:, 3 * s, 400:400 + NS], ACT.Identity, bias=c("bs00")[:, g:g + 1],
                               scale=c("ws00")[:, g:g + 1])
                act.activation(three(sbf(s)), pset(s), ACT.Gelu_apprx_tanh).then_inc(evac[s], 1)
                split_hi(q // 2 + 1, s)

            def gates(name):
                q0 = Q0[name]

                def pair(i, more=True):
                    act.wait_ge(grp, q0 + 2 * i + 1)
                    act.wait_ge(evac[1], evacuated(q0 + 1) + i)
                    act.activation(three(sbf(0)), pset(0), ACT.Sigmoid).then_inc(evac[0], 1)
                    if more:
                        split_hi(q0 // 2 + i + 1, 0)
                        act.wait_ge(grp, q0 + 2 * i + 2)
                        split_hi(q0 // 2 + i + 1, 1)

                act.wait_ge(y_done, KW * (1 + "ABCD".index(name[1])))
                with act.Fori(0, KD if name != "gD" else KD - 1) as i:
                    pair(i)
                if name == "gD":
                    pair(KD - 1, False)

            gates("gA")
            for j in range(3 * KW):
                q, s = Q0["B"] + j, j % 2
                act.wait_ge(grp, q + 1)
                if j % 3 == 0:
                    act.wait_ge(evac[(q - 2) % 2] if j else evac[1], evacuated(q - 2) + 1 if j else evacuated(q - 1) + 1)
                    act.activation(three(sbf(0)), pset(s), ACT.Copy).then_inc(evac[s], 1)
                split_hi(q // 2 + 1, s)
            gates("gB")
            for ch in range(KW):
                act.wait_ge(ln_mean, ch + 1)
                act.activation(ln_row(ch + 1), dc[:, ch, :], ACT.Square).then_inc(ln_sq, 1)
            for ch in range(KW):
                q, s = Q0["C"] + ch, ch % 2
                if ch == 1:
                    act.wait_ge(ln_rstd, 1)
                    act.activation(ln_row(1), ln_row(1), ACT.Sqrt).then_inc(ln_rstd, 1)
                act.wait_ge(grp, q + 1)
                if ch:
                    act.wait_ge(y_done, 2 * KW + ch)
                else:
                    act.wait_ge(gap_zero, 1)
                act.activation(three(sbf(0, PC)), pset(s), ACT.Copy).then_inc(evac[s], 1)
                split_hi(q // 2 + 1, s)
            for ch in range(KW):
                act.wait_ge(ln_norm, ch + 1)
                act.activation(dc[:, ch, :], dc[:, ch, :], ACT.Silu, bias=c("dlb")[:, ch:ch + 1],
                               scale=c("dlg")[:, ch:ch + 1]).then_inc(ln_y, 1)
            gates("gC")
            act.wait_ge(ln_y, KW)
            act.wait_ge(grp, Q0["gD"])
            for ch in range(KW):
                act.activation(yh[:, ch, :], dc[:, ch, :], ACT.Copy).then_inc(ln_y, 1)
            gates("gD")
            act.wait_ge(m_ready, 1)
            for k in range(KD):
                act.activation(h_hi[:, k, :], mm[:, k, :], ACT.Copy).then_inc(m_hi_done, 1)

            def split_wo(i, s):
                act.wait_ge(wo_in[s], 16 * (i + 1))
                act.activation(wo_hi[:, bass.ds(2 * i + s, 1), :].rearrange("p o n -> p (o n)"), wo_raw[:, s, :], ACT.Copy
                               ).then_inc(wo_hi_done, 1)

            with act.Fori(0, KD // 2) as i:
                for s in range(2):
                    split_wo(i, s)
            def normalise(t):
                n, s = tile_rows(t)[1], t % 2
                act.wait_ge(x1_done, t + 1)
                if t == 0:
                    act.wait_ge(r3_in, 32)
                act.activation(sq[0:n, :], xt[0:n, s, :], ACT.Square, accum_out=rt[0:n, 140:141]).then_inc(x1_sq, 1)
                act.wait_ge(x1_var, t + 1)
                act.activation(rt[0:n, 141:142], rt[0:n, 141:142], ACT.Sqrt).then_inc(x1_rstd, 1)

            def h2_columns(t):
                n = tile_rows(t)[1]
                act.wait_ge(h2_turned, t + 1)
                if t:
                    act.wait_ge(logit_prod, t)
                act.activation(h2T[:, :, 0:n].rearrange("p (a k) n -> p a k n", a=2),
                               ps[:, 4:6, :].rearrange("p a (k n) -> p a k n", k=4)[:, :, :, 0:n], ACT.Copy
                               ).then_inc(h2T_done, 1)

            def exponentials(t):
                n = tile_rows(t)[1]
                act.wait_ge(gexp_in, t + 1)
                act.activation(rt[0:n, 60:64], rt[0:n, 0:4], ACT.Exp, bias=rt[0:n, 142:143],
                               accum_out=rt[0:n, 143:144]).then_inc(gexp_done, 1)
                act.wait_ge(eexp_in, t + 1)
                act.activation(rt[0:n, 145:146], rt[0:n, 144:145], ACT.Exp).then_inc(eexp_done, 1)

            for t in range(TILES + 2):
                if t < TILES:
                    normalise(t)
                if 0 < t <= TILES:
                    h2_columns(t - 1)
                if t > 1:
                    exponentials(t - 2)

            act.wait_ge(slots_done, 1)
            act.wait_ge(y_zero, 16 * 2 * (BLOCKS - MIN_BLOCKS))
            rest = act.value_load(block_e[0:1, BLOCKS:BLOCKS + 1], min_val=0, max_val=NPAIR - 1)

            def columns_out(b, s, used=True):
                act.wait_ge(turned, b + 1)
                if used:
                    act.wait_ge(gu_prod, b - 1)
                act.activation(xgT[:, s, :, :].rearrange("p (a k) n -> p a (k n)", a=2), ps[:, 0:2, :], ACT.Copy
                               ).then_inc(xgT_done, 1)

            def silu(b, s, used=True):
                act.wait_ge(gu_prod, b + 1)
                if used:
                    act.wait_ge(hm_done, b)
                act.activation(sg[:, :], ps[:, 2 + s, 0:FE], ACT.Silu).then_inc(silu_done, 1)

            def store(b, s):
                act.wait_ge(y_copied, b + 1)
                act.dma_start(yd[bass.ds(b * P, P), :], yb[:, s, :]).then_inc(y_out[s], 16)

            columns_out(0, 0, False)
            columns_out(1, 1, False)
            silu(0, 0, False)
            columns_out(2, 0)
            silu(1, 1)
            store(0, 0)
            with act.Fori(1, NPAIR) as i:
                with act.If(i < rest + 1):
                    for s in range(2):
                        columns_out(2 * i + s + 1, 1 - s)
                        silu(2 * i + s, s)
                        store(2 * i + s - 1, 1 - s)
            store(2 * rest + 1, 1)
            act.wait_ge(y_out[0], 16 * rest + 16)
            act.wait_ge(y_out[1], 16 * rest + 16)
            def scale_y1(t):
                n, j = tile_rows(t)[1], t % YB
                act.wait_ge(y1_in[j], 16 * (t // YB + 1))
                act.activation(y12[0:n, j, 0, :], y12[0:n, j, 0, :], ACT.Copy, scale=wts[0:n, 0, t:t + 1]
                               ).then_inc(y1_scaled, 1)

            scale_y1(0)
            for t in range(TILES + 1):
                if t + 1 < TILES:
                    scale_y1(t + 1)
                if t < TILES:
                    n, j = tile_rows(t)[1], t % YB
                    act.wait_ge(c_sq_in, t + 1)
                    act.activation(y12[0:n, j, 0, :], x1[0:n, j, :], ACT.Square, accum_out=cs[0:n, 2 * (t % 2):2 * (t % 2) + 1]
                                   ).then_inc(c_sq, 1)
                if t:
                    n, v = tile_rows(t - 1)[1], 2 * ((t - 1) % 2) + 1
                    act.wait_ge(c_var, t)
                    act.activation(cs[0:n, v:v + 1], cs[0:n, v:v + 1], ACT.Sqrt).then_inc(c_rstd, 1)

        @block.gpsimd
        def _(pool):
            pool.memset(zeros[:, :], 0.0).then_inc(zeros_ready, 1)
            pool.wait_ge(early_in, 16)
            pool.affine_select(out=aws, in_=aws, compare_op=ALU.is_ge, fill=0.0, base=0,
                               pattern=[[0, KW], [1, P]], channel_multiplier=-1).then_inc(masked, 1)
            for a in range(2):
                half = slice(a * KD * W // 2, (a + 1) * KD * W // 2)
                pool.wait_ge(wv_hi, a + 1)
                pool.tensor_tensor(y_lo[:, half], e("wv")[:, half], y_hi[:, half].bitcast(F32), ALU.subtract
                                   ).then_inc(wv_lo, 1)

            def split_lo(pr, s, wait=True):
                pool.wait_ge(raw_in, 16 * (pr + 1))
                pool.wait_ge(hi_done, 2 * pr + s + 1)
                if wait:
                    pool.wait_ge(grp, 2 * pr + s - 1)
                pool.tensor_tensor(w_lo[:, s, :, :].rearrange("p k n -> p (k n)"), raw[:, s, :],
                                   w_hi[:, s, :, :].rearrange("p k n -> p (k n)").bitcast(F32), ALU.subtract
                                   ).then_inc(lo_done, 1)

            pool.wait_ge(mod_ready, 3)
            split_lo(0, 0, False)
            split_lo(0, 1, False)
            with pool.Fori(1, N_GROUPS // 2) as i:
                for s in range(2):
                    split_lo(i, s)

            def split_wo_lo(i, s):
                pool.wait_ge(wo_in[s], 16 * (i + 1))
                pool.wait_ge(wo_hi_done, 2 * i + s + 1)
                pool.tensor_tensor(wo_lo[:, bass.ds(2 * i + s, 1), :].rearrange("p o n -> p (o n)"), wo_raw[:, s, :],
                                   wo_hi[:, bass.ds(2 * i + s, 1), :].rearrange("p o n -> p (o n)").bitcast(F32),
                                   ALU.subtract).then_inc(wo_lo_done, 1)

            with pool.Fori(0, KD // 2) as i:
                for s in range(2):
                    split_wo_lo(i, s)
            pool.wait_ge(m_hi_done, KD)
            pool.wait_ge(m_lo_done, KD)
            pool.memset(zero_ids[:, :], 0).then_inc(table_zero, 1)

            pool.wait_ge(slots_done, 1)
            pool.wait_ge(table_out, 16)
            pool.wait_ge(h2_out[0], 16 * 5)
            pool.wait_ge(h2_out[1], 16 * 4)
            for ch in range(2):
                for t in range(TILES):
                    n = tile_rows(t)[1]
                    j = ch * TILES + t
                    pool.indirect_dma_start(
                        tabd, bass.IndirectOffsetOnAxis(ap=slots[0:n, j:j + 1].bitcast(U32), axis=0),
                        tokid[0:n, t:t + 1], None).then_inc(ids_done, 16)
            pool.wait_ge(ids_done, 16 * 2 * TILES)
            rest = pool.value_load(block_e[0:1, BLOCKS:BLOCKS + 1], min_val=0, max_val=NPAIR - 1)

            def gather(i, s, used=True):
                b = 2 * i + s
                if used:
                    pool.wait_ge(turned, b - 1)
                pool.dma_start(idx[:, s:s + 1], tabd[bass.ds(b * P, P), :]).then_inc(idx_in[s], 16)
                pool.wait_ge(idx_in[s], 16 * (i + 1))
                pool.sem_inc(gathers, 1)
                pool.indirect_dma_start(
                    xg[:, s, :], None, h2d, bass.IndirectOffsetOnAxis(ap=idx[:, s:s + 1].bitcast(U32), axis=0)
                ).then_inc(xg_in[s], 16)

            gather(0, 0, False)
            gather(0, 1, False)
            gather(1, 0)
            with pool.Fori(1, NPAIR) as i:
                with pool.If(i < rest + 1):
                    gather(i, 1)
                    gather(i + 1, 0)
            pool.wait_ge(y_out[0], 16 * rest + 16)
            pool.wait_ge(y_out[1], 16 * rest + 16)
            pool.sem_inc(gathers, 1)
            for t in range(TILES):
                n, s = tile_rows(t)[1], t % YB
                if t >= YB:
                    pool.wait_ge(c_done, t - YB + 1)
                for ch, got in enumerate((y1_in, y2_in)):
                    j = ch * TILES + t
                    pool.indirect_dma_start(
                        y12[0:n, s, ch, :], None, yd,
                        bass.IndirectOffsetOnAxis(ap=slots[0:n, j:j + 1].bitcast(U32), axis=0)
                    ).then_inc(got[s], 16)

        @block.vector
        def _(dve):
            steps = Steps(dve, dve_step)
            link = steps.link
            SUB, ADD, MUL = ALU.subtract, ALU.add, ALU.mult
            tt, ts, stt, cp = dve.tensor_tensor, dve.tensor_scalar, dve.scalar_tensor_tensor, dve.tensor_copy
            for k in range(1, KD):
                dve.wait_ge(sq_ready, k + 1)
                if k > 1:
                    dve.wait_ge(sq_added, k - 1)
                tt(sbf(2), sbf(0 if k == 1 else 2), sbf(k % 2), ADD).then_inc(sq_added, 1)
            dve.wait_ge(sq_prod, 1)
            ts(three(sbf(0)), pset(0), 1.0 / D, EPS, MUL, ADD).then_inc(evac[0], 1)
            dve.wait_ge(evac[0], 1)
            dve.reciprocal(sbf(0), sbf(0)).then_inc(rstd_in, 1)
            dve.wait_ge(rstd_ready, 1)
            for k in range(KD):
                tt(xT[:, k, :], xT[:, k, :], sbf(0), MUL).then_inc(scaled, 1)

            def modulation(s, scale):
                R, at = mod_rows[s], slice(scale, scale + 64)
                link(tt(R, ps[:, 7 if s == 2 else 6, :], mod_const[:, s, :], ADD))
                if scale >= 0:
                    link(stt(R[at], R[at], 1.0, mod_const[at, 3, :], ADD, MUL))
                dve.engine_nop().then_inc(mod_ready, 1)

            dve.wait_ge(slab_used, 8)
            dve.wait_ge(small_in, 16)
            dve.wait_ge(const_in, 16)
            modulation(0, 64)
            dve.wait_ge(mod_turned, 1)
            link(cp(modT.rearrange("p (j n) v -> p n j v", j=4),
                    ps[:, 7, :].rearrange("p (n j v) -> p n j v", n=4, v=32)[:, :, :, 0:NV]))
            dve.wait_ge(scaled, KD)
            hs = h_f[:, :, LP:T]
            link(tt(hs, xT[:, :, LP:T], modT[:, 8:16, 1:NV], MUL))
            tt(hs, hs, modT[:, 0:8, 1:NV], ADD).then_inc(h_f32, 1)
            for k in range(KD):
                hk = h_f[:, k, :]
                ts(hk[:, 0:LP], xT[:, k, 0:LP], modT[:, 8 + k, 0:1], modT[:, k, 0:1], MUL, ADD).then_inc(h_f32, 1)
                dve.wait_ge(h_f32, k + 2)
                dve.wait_ge(h_hi_done, k + 2)
                tt(h_lo[:, k, :], hk, h_hi[:, k, :].bitcast(F32), SUB).then_inc(h_lo_done, 1)
            dve.wait_ge(early_in, 16)
            for t in range(TILES):
                n, s = tile_rows(t)[1], t % 2
                v, w = sbf(s, 0, W)[0:n], st[0:n, 4 * s:4 * s + 4]
                dve.wait_ge(evac[s], (2 if s == 0 else 1) + t // 2)
                link(ts(w[:, 3:4], w[:, 0:1], -1.0 / W, None, MUL))
                ts(v, v, w[:, 3:4], None, ADD).then_inc(v_dve, 1)
                dve.wait_ge(v_act, 2 * t + 1)
                link(ts(w[:, 2:3], w[:, 1:2], 1.0 / W, EPS, MUL, ADD))
                dve.reciprocal(w[:, 2:3], w[:, 2:3]).then_inc(v_dve, 1)
                dve.wait_ge(v_act, 2 * t + 2)
                link(stt(v, v, w[:, 2:3], e("alg")[0:n], MUL, MUL))
                out = vn[:, t, :] if t < TILES - 1 else e("vs")[0:NS, :]
                tt(out, v, e("alb")[0:n], ADD).then_inc(v_done, 1)
                if t in (4, 7):
                    s = (t - 1) // 3
                    dve.wait_ge(slab_used, 8 * s + 8)
                    modulation(s, 0 if s == 2 else -1)
            dve.wait_ge(v_done, TILES)
            for ch in range(KW):
                scr = sbf(2, 0, NS * (CD - 1)).rearrange("p (b l) -> p b l", b=NS)
                link(tt(scr, st_d[:, ch], cdw[:, ch, 0:CD - 1].unsqueeze(1).to_broadcast([P, NS, CD - 1]), MUL))
                link(dve.tensor_reduce(dsums[:, ch, :], scr, AXX, ADD))
                link(dve.tensor_reduce(psums[:, ch, :], st_p[:, ch, :, PC + 1 - 2 ** (ch + 1):PC], AXX, ADD))
            link(dve.memset(gl[:, :, 0:CD - 1], 0.0))
            with dve.Fori(0, 4) as i:
                dve.wait_ge(evac[1], evacuated(1) + 1 + i)
                tt(three(gl[:, bass.ds(i, 1), CD - 1:].rearrange("p o t -> p (o t)")), pset(0), three(sbf(0)), MUL
                   ).then_inc(evac[0], 1)
            dve.wait_ge(evac[0], evacuated(8))

            def split_y(ch, src, only_lo=False):
                link(cp(yh[:, ch, :], src))
                tt(yl[:, ch, :], src, yh[:, ch, :].bitcast(F32), SUB).then_inc(y_done, 1)

            for g in range(KW):
                q, s = Q0["A"] + g, g % 2
                dve.wait_ge(gate_prod, g + 1)
                if g:
                    dve.wait_ge(y_done, g)
                tt(sbf(2, 0, LP).rearrange("p (a n t) -> p a n t", a=2, n=4), ps[:, 6:8, :].rearrange("p a (n t) -> p a n t", n=4),
                   abs_[:, g, :].unsqueeze(1).unsqueeze(1).to_broadcast([P, 2, 4, P]), ADD).then_inc(gate_read, 1)
                dve.wait_ge(gate_read, g + 1)
                dve.wait_ge(evac[s], evacuated(q) + 1)
                link(tt(sbf(2, 0, LP), sbf(2, 0, LP), sbf(s, 0, LP), MUL))
                link(tt(sbf(2, LP, NS), smp[:, s, :], sbf(s, LP, NS), MUL))
                split_y(g, sbf(2))
            dve.wait_ge(y_done, KW)

            def tap(ch, l):
                x = gl[:, ch, :]
                link(stt(dc[:, ch, 0:LP], gl[:, ch, bass.ds(l, LP)], cdw[:, ch, bass.ds(l, 1)], dc[:, ch, 0:LP],
                         MUL, ADD))

            def first_tap(ch):
                link(ts(dc[:, ch, 0:LP], gl[:, ch, 0:LP], cdw[:, ch, 0:1], c("cdb")[:, ch:ch + 1], MUL, ADD))
                link(stt(dc[:, ch, LP:T], gl[:, ch, GLW - NS:GLW], cdw[:, ch, CD - 1:CD], dsums[:, ch, :], MUL, ADD))
                link(ts(dc[:, ch, LP:T], dc[:, ch, LP:T], c("cdb")[:, ch:ch + 1], None, ADD))

            def merge(name, i, j):
                q0 = Q0[name]
                dve.wait_ge(grp, q0 + 2 * i + 2)
                dve.wait_ge(evac[0], evacuated(q0) + i + 1)
                mj = mm[:, bass.ds(j, 1), :].rearrange("p o t -> p (o t)")
                if name == "gA":
                    tt(three(mj), pset(1), three(sbf(0)), MUL).then_inc(evac[1], 1)
                else:
                    tt(three(sbf(1)), pset(1), three(sbf(0)), MUL).then_inc(evac[1], 1)
                    dve.wait_ge(evac[1], evacuated(q0 + 1) + i + 1)
                    link(tt(mj, mj, sbf(1), ADD))

            def gates(name, chunks=()):
                for ch in chunks:
                    first_tap(ch)
                adds = 0 if name == "gA" else 1
                with dve.Fori(0, KD - 1) as i:
                    steps.loop(i, 0, adds + 4 * len(chunks))
                    merge(name, i, i)
                    for k in range(4):
                        for ch in chunks:
                            tap(ch, 1 + 4 * i + k)
                steps.done(KD - 1)
                merge(name, KD - 1, KD - 1)
                for l in (CD - 2, CD - 1):
                    for ch in chunks:
                        tap(ch, l)

            gates("gA", (0, 1))
            link(dve.memset(sbf(1, 0, 2), 0.0))
            for ch in range(KW):
                q = Q0["B"] + 3 * ch
                cx, o = sbf(1, 0, T + 2), sbf(2)
                dve.wait_ge(grp, q + 2)
                dve.wait_ge(evac[q % 2], evacuated(q) + 1)
                s = (q + 1) % 2
                tt(three(cx[:, 2:]), pset(s), three(sbf(0)), MUL).then_inc(evac[s], 1)
                dve.wait_ge(evac[s], evacuated(q + 1) + 1)
                if ch:
                    dve.wait_ge(y_done, KW + ch)
                link(ts(o[:, 0:LP], cx[:, 0:LP], cbw[:, 0, ch:ch + 1], None, MUL))
                link(ts(o[:, LP:T], st_b[:, ch, :, 0], cbw[:, 0, ch:ch + 1], None, MUL))
                link(stt(o[:, 0:LP], cx[:, 1:LP + 1], cbw[:, 1, ch:ch + 1], o[:, 0:LP], MUL, ADD))
                link(stt(o[:, LP:T], st_b[:, ch, :, 1], cbw[:, 1, ch:ch + 1], o[:, LP:T], MUL, ADD))
                link(stt(o, cx[:, 2:], cbw[:, 2, ch:ch + 1], o, MUL, ADD))
                link(cp(tail_b[:, ch, :], cx[:, LP:LP + 10]))
                s = (q + 2) % 2
                dve.wait_ge(grp, q + 3)
                tt(three(o), pset(s), three(o), MUL).then_inc(evac[s], 1)
                dve.wait_ge(evac[s], evacuated(q + 2) + 1)
                split_y(ch, o)
            dve.wait_ge(y_done, 2 * KW)
            dve.engine_nop().then_inc(tails_b, 1)
            gates("gB", (2, 3))
            dve.wait_ge(stored, 16 * 5)
            dve.engine_nop().then_inc(ln_in, 1)
            dve.wait_ge(ln_prod, KW)
            ts(three(ln_row(0)), pset(0), 1.0 / W, None, MUL).then_inc(evac[0], 1)
            dve.wait_ge(evac[0], evacuated(Q0["C"]))
            for ch in range(KW):
                tt(dc[:, ch, :], dc[:, ch, :], ln_row(0), SUB).then_inc(ln_mean, 1)
            dve.wait_ge(ln_prod, 2 * KW)
            ts(three(ln_row(1)), pset(1), 1.0 / W, EPS, MUL, ADD).then_inc(evac[1], 1)
            dve.wait_ge(evac[1], evacuated(Q0["C"] + 1))
            dve.reciprocal(ln_row(1), ln_row(1)).then_inc(ln_rstd, 1)
            dve.memset(sbf(0, 0, PC), 0.0).then_inc(gap_zero, 1)
            X = PC + LP
            for ch in range(KW):
                q, s = Q0["C"] + ch, ch % 2
                x0 = sbf(0, 0, PC + T)
                dve.wait_ge(evac[s], evacuated(q) + 1)
                if ch:
                    dve.wait_ge(y_done, 2 * KW + ch)
                src, width = x0, 1
                for d in range(ch + 1):
                    dst = sbf(1 + d % 2, 0, PC + T)
                    lo = 2 * width - 1
                    link(tt(dst[:, lo:X], src[:, lo:X], src[:, lo - width:X - width], ADD))
                    src, width = dst, 2 * width
                p = sbf(pooled_in(ch), 0, PC + T)
                link(stt(p[:, PC:X], src[:, PC:X], 1.0 / width, x0[:, PC:X], MUL, SUB))
                link(tt(p[:, PC:2 * PC], src[:, PC:2 * PC], inv[:, ch, :], MUL))
                link(tt(p[:, PC:2 * PC], p[:, PC:2 * PC], x0[:, PC:2 * PC], SUB))
                link(tt(p[:, X:X + NS], psums[:, ch, :], x0[:, X:X + NS], ADD))
                link(cp(tail_p[:, ch, :], x0[:, LP:LP + PC + NS]))
                stt(p[:, X:X + NS], p[:, X:X + NS], 1.0 / width, x0[:, X:X + NS], MUL, SUB).then_inc(pooled, 1)
                dve.wait_ge(pool_prod, ch + 1)
                o = sbf(3 - pooled_in(ch))
                ts(three(o), pset(s), c("pscale")[:, ch:ch + 1], None, MUL).then_inc(evac[s], 1)
                dve.wait_ge(evac[s], evacuated(q) + 2)
                split_y(ch, o)
            dve.wait_ge(y_done, 3 * KW)
            dve.engine_nop().then_inc(tails_p, 1)
            dve.wait_ge(ln_mean, KW)
            dve.wait_ge(ln_rstd, 2)
            for ch in range(KW):
                tt(dc[:, ch, :], dc[:, ch, :], ln_row(1), MUL).then_inc(ln_norm, 1)
            gates("gC")
            for ch in range(KW):
                dve.wait_ge(ln_y, KW + ch + 1)
                tt(yl[:, ch, :], dc[:, ch, :], yh[:, ch, :].bitcast(F32), SUB).then_inc(y_done, 1)
            gates("gD")
            dve.engine_nop().then_inc(m_ready, 1)
            for k in range(KD):
                dve.wait_ge(m_hi_done, k + 1)
                tt(h_lo[:, k, :], mm[:, k, :], h_hi[:, k, :].bitcast(F32), SUB).then_inc(m_lo_done, 1)

            dve.wait_ge(m_lo_done, KD)
            dve.wait_ge(rows_in, 16 * 6)
            dve.wait_ge(r3_in, 32)
            M1, M2, MS = (MK[:, j, :].rearrange("p (t e) -> p t e", t=TILES) for j in range(3))
            link(dve.memset(MK[:, :, (TILES - 1) * NE:], 0.0))
            link(dve.memset(slots[:, :], 0))
            link(dve.memset(rt[:, 40:48], -3.0e38))
            two = lambda ap: ap.rearrange("p (a n) -> p a n", a=2)

            def residual(t):
                n, s = tile_rows(t)[1], t % 2
                R = rows if t < TILES - 1 else rows_s
                z = rt[0:n, :]
                dve.wait_ge(o_prod, t + 1)
                if t >= 2:
                    dve.wait_ge(h2_out[s], 16 * (t // 2))
                    dve.wait_ge(h2_turned, t - 1)
                tt(two(h2[0:n, s, :]), ps[0:n, 2 * s:2 * s + 2, :], two(R[0:n, 0, :]), MUL).then_inc(o_read, 1)
                dve.wait_ge(o_read, t + 1)
                dve.wait_ge(xt_in[s], 16 * (t // 2 + 1))
                tt(xt[0:n, s, :], h2[0:n, s, :], xt[0:n, s, :], ADD).then_inc(x1_done, 1)
                dve.wait_ge(x1_sq, t + 1)
                dve.wait_ge(x1_done, t + 1)
                link(ts(z[:, 141:142], z[:, 140:141], 1.0 / D, EPS, MUL, ADD))
                dve.reciprocal(z[:, 141:142], z[:, 141:142]).then_inc(x1_var, 1)
                dve.wait_ge(x1_rstd, t + 1)
                link(stt(h2[0:n, s, :], xt[0:n, s, :], z[:, 141:142], R[0:n, 1, :], MUL, MUL))
                tt(h2[0:n, s, :], h2[0:n, s, :], R[0:n, 2, :], ADD).then_inc(h2_done, 1)

            def route(t):
                n = tile_rows(t)[1]
                z = rt[0:n, :]
                zi = ri[0:n, :]
                dve.wait_ge(logit_prod, t + 1)
                tt(z[:, 0:36], ps[0:n, 6, 0:36], r("br")[0:n], ADD).then_inc(logit_read, 1)
                dve.wait_ge(logit_read, t + 1)
                link(cp(z[:, 40:44], z[:, 0:4]))
                link(dve.max(z[:, 48:56], z[:, 40:48]))
                link(dve.max_index(zi[:, 0:8], z[:, 48:56], z[:, 40:48]))
                link(cp(z[:, 56:57], zi[:, 0:1]))
                ts(z[:, 142:143], z[:, 48:49], -1.0, None, MUL).then_inc(gexp_in, 1)
                link(ts(z[:, 116:120], r("iota")[0:n, 0:NG], z[:, 56:57], None, ALU.is_equal))
                link(tt(z[:, 64:96].rearrange("p (g e) -> p g e", g=NG), z[:, 4:36].rearrange("p (g e) -> p g e", g=NG),
                        z[:, 116:120].unsqueeze(2).to_broadcast([n, NG, 8]), MUL))
                link(dve.tensor_reduce(z[:, 96:104], z[:, 64:96].rearrange("p (g e) -> p e g", g=NG), AXX, ADD))
                link(dve.max(z[:, 104:112], z[:, 96:104]))
                link(dve.max_index(zi[:, 8:16], z[:, 104:112], z[:, 96:104]))
                tt(z[:, 144:145], z[:, 105:106], z[:, 104:105], SUB).then_inc(eexp_in, 1)
                link(cp(z[:, 112:114], zi[:, 8:10]))
                link(stt(z[:, 114:116], z[:, 56:57].to_broadcast([n, 2]), 8.0, z[:, 112:114], MUL, ADD))
                link(ts(M1[0:n, t, :], r("iota")[0:n], z[:, 114:115], None, ALU.is_equal))
                link(ts(M2[0:n, t, :], r("iota")[0:n], z[:, 115:116], None, ALU.is_equal))
                tt(MS[0:n, t, :], M1[0:n, t, :], M2[0:n, t, :], ADD).then_inc(mask_done, 1)
                dve.wait_ge(gexp_done, t + 1)
                dve.wait_ge(eexp_done, t + 1)
                link(ts(z[:, 146:147], z[:, 145:146], 1.0, z[:, 143:144], ADD, MUL))
                link(dve.reciprocal(wts[0:n, 0, t:t + 1], z[:, 146:147]))
                link(tt(wts[0:n, 1, t:t + 1], wts[0:n, 0, t:t + 1], z[:, 145:146], MUL))

            for t in range(TILES + 2):
                if t < TILES:
                    residual(t)
                if t > 1:
                    route(t - 2)
            dve.wait_ge(rank_prod, 1)
            cnt = rt[:, 0:NE]
            nb, end, base = rt[:, 32:64], rt[:, 64:96], rt[:, 96:128]
            big = cmp_[:, 0:NE * 9].rearrange("p (e j) -> p e j", e=NE)
            link(cp(cnt, ps[:, 7, TILES * NE:(TILES + 1) * NE]))
            link(tt(big, cnt.unsqueeze(2).to_broadcast([P, NE, 9]), r("thr").unsqueeze(1).to_broadcast([P, NE, 9]),
                    ALU.is_gt))
            link(dve.tensor_reduce(nb, big, AXX, ADD))
            link(dve.tensor_tensor_scan(end, ones[:, 0:NE], nb, 0.0, MUL, ADD))
            link(tt(base, end, nb, SUB))
            link(ts(base, base, float(P), None, MUL))
            rank = cmp_[:, 0:TILES * NE].rearrange("p (t e) -> p t e", t=TILES)
            link(tt(rank, ps[:, 7, 0:TILES * NE].rearrange("p (t e) -> p t e", t=TILES),
                    base.unsqueeze(1).to_broadcast([P, TILES, NE]), ADD))
            for ch, M in enumerate((M1, M2)):
                link(tt(M, M, rank, MUL))
                link(dve.tensor_reduce(rt[:, 128 + ch * TILES:128 + (ch + 1) * TILES], M, AXX, ADD))
            link(cp(slots[:, :], rt[:, 128:128 + 2 * TILES]))
            blk = cmp_[:, :].rearrange("p (b e) -> p b e", b=BLOCKS)
            link(tt(blk, end.unsqueeze(1).to_broadcast([P, BLOCKS, NE]),
                    r("biota").unsqueeze(2).to_broadcast([P, BLOCKS, NE]), ALU.is_le))
            link(dve.tensor_reduce(rt[:, 0:BLOCKS], blk, AXX, ADD))
            link(ts(rt[:, 0:BLOCKS], rt[:, 0:BLOCKS], float(NE - 1), None, ALU.min))
            link(cp(block_e[:, 0:BLOCKS], rt[:, 0:BLOCKS]))
            link(ts(cmp_[:, 0:NPAIR], r("pair"), end[:, NE - 1:NE], None, ALU.is_lt))
            link(dve.tensor_reduce(rt[:, 0:1], cmp_[:, 0:NPAIR], AXX, ADD))
            ts(block_e[:, BLOCKS:BLOCKS + 1], rt[:, 0:1], -1.0, None, ADD).then_inc(slots_done, 1)

            dve.wait_ge(slots_done, 1)
            rest = dve.value_load(block_e[0:1, BLOCKS:BLOCKS + 1], min_val=0, max_val=NPAIR - 1)

            def hidden(b, s):
                dve.wait_ge(silu_done, b + 1)
                tt(hm[:, :], ps[:, 2 + s, FE:2 * FE], sg[:, :], MUL).then_inc(hm_done, 1)

            def hidden_columns(b):
                dve.wait_ge(hm_turned, b + 1)
                cp(hmT[:, :, :].rearrange("p f n -> p (f n)"), ps[:, 4, 0:2 * P]).then_inc(hmT_done, 1)

            def copy_y(b, i, s, used=True):
                dve.wait_ge(y_prod, b + 1)
                if used:
                    dve.wait_ge(y_out[s], 16 * i)
                cp(two(yb[:, s, :]), ps[:, 5:7, :]).then_inc(y_copied, 1)

            hidden(0, 0)
            hidden_columns(0)
            hidden(1, 1)
            copy_y(0, 0, 0, False)
            hidden_columns(1)
            hidden(2, 0)
            copy_y(1, 0, 1, False)
            hidden_columns(2)
            hidden(3, 1)
            copy_y(2, 1, 0)
            with dve.Fori(2, NPAIR) as i:
                with dve.If(i < rest + 1):
                    hidden_columns(2 * i - 1)
                    hidden(2 * i, 0)
                    copy_y(2 * i - 1, i - 1, 1)
                    hidden_columns(2 * i)
                    hidden(2 * i + 1, 1)
                    copy_y(2 * i, i, 0)
            hidden_columns(2 * rest + 1)
            copy_y(2 * rest + 1, rest, 1)
            dve.wait_ge(g2_in, 32)
            dve.wait_ge(fg_in, 16)

            def combine(t):
                n, j = tile_rows(t)[1], t % YB
                a, b_, x = y12[0:n, j, 0, :], y12[0:n, j, 1, :], x1[0:n, j, :]
                dve.wait_ge(y1_scaled, t + 1)
                dve.wait_ge(y2_in[j], 16 * (t // YB + 1))
                link(stt(b_, b_, wts[0:n, 1, t:t + 1], a, MUL, ADD))
                link(tt(b_, b_, g2r[0:n, 0 if t < TILES - 1 else 1, :], MUL))
                dve.wait_ge(x1_in[j], 16 * (t // YB + 1))
                tt(x, x, b_, ADD).then_inc(c_sq_in, 1)

            def last_norm(t):
                n, x = tile_rows(t)[1], x1[0:tile_rows(t)[1], t % YB, :]
                total, rstd = (cs[0:n, 2 * (t % 2) + a:2 * (t % 2) + a + 1] for a in range(2))
                dve.wait_ge(c_sq_in, t + 1)
                dve.wait_ge(c_sq, t + 1)
                link(ts(rstd, total, 1.0 / D, EPS, MUL, ADD))
                dve.reciprocal(rstd, rstd).then_inc(c_var, 1)
                dve.wait_ge(c_rstd, t + 1)
                stt(x, x, rstd, fg[0:n, :], MUL, MUL).then_inc(c_done, 1)

            for t in range(TILES + 1):
                if t < TILES:
                    combine(t)
                if t:
                    last_norm(t - 1)


def kernel(**inputs):
    import concourse.bacc as bacc
    from concourse.bass_utils import run_bass_kernel_spmd

    a = {k: np.asarray(v) for k, v in inputs.items()}
    f = np.float32

    def chan(x, n):
        x = np.moveaxis(x, -1, 0)
        return np.moveaxis(x.reshape((n, P) + x.shape[1:]), 0, 1)

    def kmaj(w):
        return w.reshape(-1, P, w.shape[1]).transpose(1, 0, 2)

    def rep(x):
        return np.broadcast_to(x.reshape(1, -1), (P, x.size))

    def fill(where, width, parts):
        out = np.zeros((P, width), f)
        for name, x in parts.items():
            lo, hi = where[name]
            out[:, lo:hi] = np.asarray(x).reshape(P, hi - lo)
        return out

    x = np.concatenate([a["x_prompt"][0], a["x_sample"][:, 0]], axis=0)
    cc = np.concatenate([a["c_prompt"], a["c_sample"]], axis=0)
    eye = np.eye(P, dtype=f)
    inv = np.stack([1.0 / np.minimum(np.arange(PC) + 1, 2 ** (g + 1)) for g in range(KW)]).astype(f)
    ws = a["a_ws"][0]
    cT = np.zeros((P, KD, 32), f)
    cT[:, :, 0:NV] = chan(cc, KD)
    mod_const = np.zeros((4, 32, 4, 512), f)
    for s in range(3):
        mod_const[:, 0:NV, s] = a["b_mod"][0].reshape(3, 4, 1, 512)[s]
    mod_const[:, 0:NV, 3] = np.concatenate([a["norm2_g"][0], a["norm1_g"][0]]).reshape(4, 1, 512)
    small = fill(COLS, LOADED, dict(
        ident=eye, ones=np.ones((P, P), f), cT=cT, cbw=np.moveaxis(chan(a["conv_b_w"][0], KW), 2, 1), cdw=chan(a["conv_d_w"][0], KW),
        cdb=chan(a["conv_d_b"][0], KW), dlg=chan(a["d_ln_g"][0], KW), dlb=chan(a["d_ln_b"][0], KW),
        pscale=chan(a["pool_scale"][0], KW), ws00=rep(ws[:, 0, 0]), bs00=rep(a["a_bs"][0, :, 0]),
        st_b=chan(a["state_conv_b"][0], KW), poolw=a["pool_w"][0].transpose(1, 0, 2), inv=rep(inv)))
    early = fill(ECOLS, EARLY_LOADED, dict(
        wv=kmaj(a["w_in"][0][:, W:2 * W]), st_d=chan(a["state_conv_d"][0], KW), st_p=chan(a["state_pool"][0], KW),
        alg=rep(a["a_ln_g"][0]), alb=rep(a["a_ln_b"][0]), aws=ws.transpose(2, 0, 1), abs=rep(a["a_bs"][0])))
    w_in = kmaj(a["w_in"][0])

    def cols(first, n=P):
        return w_in[:, :, first:first + n].reshape(P, -1)

    u, gb, gc, xin, pin, ga, gg = (x_ * W for x_ in (0, 2, 3, 4, 5, 6, 7))
    order = []
    for ch in range(KW):
        order += [ga + ch * P, gg + ch * P]
    order += [u + ch * P for ch in range(KW)]
    for ch in range(KW):
        order += [gc + ch * P, xin + ch * P, gb + ch * P]
    order += [pin + ch * P for ch in range(KW)]
    w_mix = np.stack([cols(o) for o in order]).reshape(-1, 2, P, KD * P).transpose(0, 2, 1, 3).reshape(-1, P, 2 * KD * P)
    w_gate = np.stack([np.concatenate([cols(8 * W + br * D + j * P), kmaj(a["w_branch"][0, br][:, j * P:(j + 1) * P]
                                                                     ).reshape(P, -1)], axis=1)
                       for br in range(4) for j in range(KD)])
    gu = np.concatenate([a["w_eg"][0], a["w_eu"][0]], axis=2).reshape(NE, KD, P, 2 * FE).transpose(0, 2, 1, 3)
    dn = a["w_ed"][0].reshape(NE, 2, P, D).transpose(0, 2, 1, 3)
    routing = np.zeros((P, R3W), f)
    routing[:, 0:P] = eye
    routing[:, P:2 * P] = 1.0
    routing[:, slice(*R3["tri"])] = np.triu(np.ones((P, P), f), 1)
    routing[:, slice(*R3["iota"])] = np.arange(NE)
    routing[:, slice(*R3["thr"])] = P * np.arange(9)
    routing[:, slice(*R3["biota"])] = np.arange(BLOCKS)
    routing[:, slice(*R3["pair"])] = 2 * np.arange(NPAIR)
    routing[:, slice(*R3["br"])] = np.concatenate([a["b_rg"][0], a["b_re"][0]])
    routing[:, slice(*R3["wr"])] = kmaj(np.concatenate([a["w_rg"][0], a["w_re"][0]], axis=1)).reshape(P, -1)
    arrays = dict(
        small=small, xT=chan(x, KD), early=early,
        w_mod=kmaj(a["w_mod"][0]).reshape(P, KD, 3, SLAB).transpose(2, 1, 0, 3).reshape(24, P, SLAB),
        mod_const=mod_const.reshape(P, -1), w_mix=w_mix, w_gate=w_gate,
        w_out=kmaj(a["w_out"][0]), x_tok=x, routing=routing,
        tokid=(np.arange(P)[:, None] + P * np.arange(TILES)[None, :]).astype(np.int32),
        w_exp=np.concatenate([gu.reshape(NE, P, -1), dn.reshape(NE, P, -1)], axis=2), final_g=rep(a["final_g"]),
        state_b=a["state_conv_b"][0], state_p=a["state_pool"][0], state_d=a["state_conv_d"][0])
    arrays = {k: np.ascontiguousarray(v) for k, v in arrays.items()}
    shapes = dict(y=(T, D), v_s=(NS, W), keep_b=(NS, 1, W), keep_p=(NS, PC - 1, W), keep_d=(NS, CD - 2, W),
                  tail_b=(P, KW, 10), tail_p=(P, KW, 23), tail_d=(P, KW, 38))
    nc = bacc.Bacc("TRN2", target_bir_lowering=False, num_devices=1)
    A = {k: nc.dram_tensor(k, v.shape, mybir.dt.from_np(v.dtype), kind="ExternalInput").ap() for k, v in arrays.items()}
    O = {k: nc.dram_tensor("out_" + k, v, F32, kind="ExternalOutput").ap() for k, v in shapes.items()}
    build(nc, A, O)
    r = run_bass_kernel_spmd(nc, [arrays], core_ids=[0]).results[0]
    o = {k: np.asarray(r["out_" + k]) for k in shapes}

    def rows_of(tail):
        return tail.transpose(2, 1, 0).reshape(tail.shape[2], W)

    tb, tp, td = (rows_of(o[k]) for k in ("tail_b", "tail_p", "tail_d"))

    def state(keep, tail):
        return np.concatenate([keep, tail[-NS:, None, :]], axis=1)[None]

    return (o["y"][None, :LP], o["y"][LP:, None], tb[None, None, :2], tp[None, None, :PC], td[None, None, :CD - 1],
            state(o["keep_b"], tb), state(o["keep_p"], tp), state(o["keep_d"], td), o["v_s"][None, :, None])
```

```python
from contextlib import ExitStack

import numpy as np

import concourse.bass as bass
from concourse import mybir

F32 = mybir.dt.float32
F32R = mybir.dt.float32r
I32 = mybir.dt.int32
U32 = mybir.dt.uint32
ALU = mybir.AluOpType
ACT = mybir.ActivationFunctionType
AXX = mybir.AxisListType.X

P = 128
D = 1024
KD = D // P
LP = 1024
NS = 8
T = LP + NS
NT = 3
TT = T // NT
W = 512
KW = W // P
NV = 1 + NS
CD = 31
PC = 15
EPS = 1e-6
SLAB = 2 * D
TILES = LP // P + 1
NE = 32
NG = 4
FE = 256
BLOCKS = 50
MIN_BLOCKS = 18
NPAIR = 24
GUW = KD * 2 * FE
WB = 4
YB = 6
EW = GUW + 2 * D
GLW = CD - 1 + T
SW = T + 32

MIX_PAIRS = {"D": 4, "A": 2, "B": 6, "C": 2}
N_GROUPS = 2 * (sum(MIX_PAIRS.values()) + 4 * KD)
Q0, q = {}, 0
for name_, pairs_ in (("D", 4), ("A", 2), ("gA", 8), ("B", 6), ("gB", 8), ("C", 2), ("gC", 8), ("gD", 8)):
    Q0[name_] = q
    q += 2 * pairs_


def columns():
    at, where = 0, {}
    for name, n in (("ident", P), ("ones", P), ("cT", KD * 32),
                    ("cbw", 3 * KW), ("cdw", KW * CD), ("cdb", KW), ("dlg", KW), ("dlb", KW), ("pscale", KW),
                    ("ws00", KW), ("bs00", KW), ("st_b", KW * NS * 2), ("poolw", KW * P), ("inv", KW * PC),
                    ("modT", 16 * NV), ("psums", KW * NS), ("dsums", KW * NS), ("stats", 16),
                    ("tail_b", KW * 10), ("tail_p", KW * 23), ("smp", 2 * NS)):
        where[name] = (at, at + n)
        at += n
    return where, at


COLS, SMALL = columns()
LOADED = COLS["modT"][0]


def early_columns():
    at, where = 0, {}
    for name, n in (("wv", KD * W), ("st_d", KW * NS * (CD - 1)), ("st_p", KW * NS * PC), ("alg", W),
                    ("alb", W), ("aws", KW * P), ("abs", KW * P), ("vs", W)):
        where[name] = (at, at + n)
        at += n
    return where, at


ECOLS, _ = early_columns()
EARLY_LOADED = ECOLS["vs"][0]


def routing_columns():
    at, where = 0, {}
    for name, n in (("tri", P), ("iota", NE), ("thr", TILES), ("blocks", BLOCKS), ("after", BLOCKS), ("places", P),
                    ("pair", NPAIR), ("sign", NPAIR),
                    ("tokens", TILES), ("br", NG + NE), ("wr", KD * (NG + NE))):
        where[name] = (at, at + n)
        at += n
    return where, at


R3, R3W = routing_columns()
BE = 150


class Steps:

    def __init__(self, eng, sem):
        self.eng, self.sem, self.n = eng, sem, 0

    def link(self, ins):
        ins.then_inc(self.sem, 1)
        self.n = self.n + 1
        self.eng.wait_ge(self.sem, self.n)

    def loop(self, i, first, per):
        self.base, self.first, self.per = self.n, first, per
        self.n = (i - first) * per + self.base

    def done(self, turns):
        self.n = self.base + turns * self.per


def evacuated(q):
    n = (6 if q % 2 == 0 else 4) + q // 2
    if q >= Q0["C"]:
        n += min(2, (q - Q0["C"]) // 2)
        if q % 2:
            n += min(2, (q - Q0["C"] + 1) // 2)
    return n


def build(nc, A, O):
    ctx = ExitStack()
    with ctx:
        def sem(name):
            return ctx.enter_context(nc.semaphore(name))

        def tensor(name, shape, dtype=F32, where=ctx):
            return where.enter_context(nc.sbuf_tensor(name, shape, dtype))

        sm = tensor("sm", [P, SMALL])
        wts = tensor("wts", [P, 2, TILES])
        slots = tensor("slots", [P, 2 * TILES], I32)
        block_e = tensor("block_e", [P, BLOCKS + 2], I32)
        table = tensor("table", [P, BLOCKS], I32)
        with ExitStack() as c3:
            we = tensor("we", [P, WB, EW], F32, c3)
            xg = tensor("xg", [P, 2, D], F32, c3)
            xgT = tensor("xgT", [P, 2, KD, P], F32, c3)
            idx = tensor("idx", [P, 2], I32, c3)
            sg = tensor("sg", [P, FE], F32, c3)
            hm = tensor("hm", [P, FE], F32, c3)
            hmT = tensor("hmT", [P, 2, P], F32, c3)
            yb = tensor("yb", [P, 2, D], F32, c3)
            g2r = tensor("g2r", [P, 2, D], F32, c3)
            fg = tensor("fg", [P, D], F32, c3)
            x1 = tensor("x1", [P, YB, D], F32, c3)
            cs = tensor("cs", [P, 8], F32, c3)

        def area(name, width, *holders):
            out = []
            for tensors in holders:
                with ExitStack() as held:
                    out += [tensor(*t, held) for t in tensors]
            tensor(name, [P, width])
            return out

        h_area, h_hi, h_lo, wo_hi, wo_lo = area(
            "area_h", 2 * KD * T, [("h_f32_area", [P, 2, KD * T], F32)],
            [("h_hi", [P, KD, T], F32R), ("h_lo", [P, KD, T], F32R)],
            [("wo_hi", [P, KD, D], F32R), ("wo_lo", [P, KD, D], F32R)])
        y_hi, y_lo, xt, h2, turn, MK, rt, ri, r3 = area(
            "area_y", 2 * KW * T, [("y_hi", [P, KW * T], F32R), ("y_lo", [P, KW * T], F32R)],
            [("xt", [P, 2, D], F32), ("h2", [P, 2, D], F32), ("turn", [P, 2 * D], F32),
             ("MK", [P, 3, TILES * NE], F32), ("rt", [P, 160], F32), ("ri", [P, 16], U32), ("r3", [P, R3W], F32)])
        raw = tensor("raw", [P, 2, KD * P])
        _, mod_const, w_hi, w_lo, rows = area(
            "area_w", 4 * KD * P, [("below_mod_const", [P, 2 * KD * P], F32), ("mod_rows_const", [P, 4, 512], F32)],
            [("w_hi", [P, 2, KD, P], F32R), ("w_lo", [P, 2, KD, P], F32R)], [("rows", [P, 3, D], F32)])
        G, m_hi, in_place, in_block = area(
            "area_G", KW * GLW + KW * T, [("G", [P, KW * GLW + KW * T], F32)], [("m_hi", [P, KD, T], F32R)],
            [("in_place", [P, 2 * TILES, P], F32R), ("in_block", [P, 2 * TILES, BLOCKS], F32R)])
        S = tensor("S", [P, 3 * SW])
        zeros = tensor("zeros", [P, 512])
        m, m_lo = area("area_m", KD * T, [("m", [P, KD * T], F32)], [("m_lo", [P, KD, T], F32R)])
        ps = ctx.enter_context(nc.psum_tensor("ps", [P, 8, 512], F32))

        def c(name):
            a, b = COLS[name]
            return sm[:, a:b]

        def e(name):
            a, b = ECOLS[name]
            return m[:, a:b]

        h2T = turn[:, 0:D].rearrange("p (k n) -> p k n", k=KD)
        sq = turn[:, D:2 * D]
        cmp_ = turn[:, 0:BLOCKS * NE]
        rows_s = S[:, 0:3 * D].rearrange("p (j n) -> p j n", j=3)
        wo_raw = [raw[:, 0, :], raw[:, 1, :], S[:, 2 * SW:2 * SW + D]]
        h_f = h_area[:, 1, :].rearrange("p (k t) -> p k t", k=KD)
        ident, ones = c("ident"), c("ones")
        cT = c("cT").rearrange("p (k v) -> p k v", k=KD)
        modT = c("modT").rearrange("p (n v) -> p n v", n=16)
        mod_rows = [S[:, at:at + 512] for at in (SW, SW + 512, 2 * SW + 512)]
        xT = G[:, 0:KD * T].rearrange("p (k t) -> p k t", k=KD)
        gl = G[:, 0:KW * GLW].rearrange("p (c t) -> p c t", c=KW)
        dc = G[:, KW * GLW:].rearrange("p (c t) -> p c t", c=KW)
        vn = G[:, KW * GLW:KW * GLW + 8 * W].rearrange("p (n c) -> p n c", n=8)
        mm = m[:, :].rearrange("p (k t) -> p k t", k=KD)
        yh = y_hi[:, :].rearrange("p (c t) -> p c t", c=KW)
        yl = y_lo[:, :].rearrange("p (c t) -> p c t", c=KW)
        yh3 = y_hi[:, :].rearrange("p (c a t) -> p c a t", c=KW, a=NT)
        yl3 = y_lo[:, :].rearrange("p (c a t) -> p c a t", c=KW, a=NT)
        h3h = h_hi[:, :, :].rearrange("p k (a t) -> p k a t", a=NT)
        h3l = h_lo[:, :, :].rearrange("p k (a t) -> p k a t", a=NT)
        wvh = y_hi[:, 0:KD * W].rearrange("p (k n) -> p k n", k=KD)
        wvl = y_lo[:, 0:KD * W].rearrange("p (k n) -> p k n", k=KD)
        slab = [mem[:, at:at + SLAB] for mem, at in [(h_area[:, j // 4, :], j % 4 * SLAB) for j in range(8)]
                + [(m, 0), (m, SLAB), (G, 0), (G, SLAB)] * 4]
        st = c("stats")
        cbw = c("cbw").rearrange("p (l c) -> p l c", l=3)
        cdw = c("cdw").rearrange("p (c l) -> p c l", c=KW)
        st_b = c("st_b").rearrange("p (c b l) -> p c b l", c=KW, b=NS)
        st_d = e("st_d").rearrange("p (c b l) -> p c b l", c=KW, b=NS)
        st_p = e("st_p").rearrange("p (c b l) -> p c b l", c=KW, b=NS)
        psums = c("psums").rearrange("p (c b) -> p c b", c=KW)
        dsums = c("dsums").rearrange("p (c b) -> p c b", c=KW)
        poolw = c("poolw").rearrange("p (c n) -> p c n", c=KW)
        inv = c("inv").rearrange("p (c n) -> p c n", c=KW)
        aws = e("aws").rearrange("p (g t) -> p g t", g=KW)
        abs_ = e("abs").rearrange("p (g t) -> p g t", g=KW)
        tail_b = c("tail_b").rearrange("p (c n) -> p c n", c=KW)
        tail_p = c("tail_p").rearrange("p (c n) -> p c n", c=KW)
        smp = c("smp").rearrange("p (a n) -> p a n", a=2)

        def sbf(n, off=0, width=T):
            return S[:, n * SW + off:n * SW + off + width]

        def ln_row(n):
            return G[:, (n % KW) * T:(n % KW + 1) * T]

        def three(ap):
            return ap.rearrange("p (a t) -> p a t", a=NT)

        def pset(s):
            return ps[:, 3 * s:3 * s + 3, 0:TT]

        small_in = sem("small_in")
        zeros_ready, y_zero = sem("zeros_ready"), sem("y_zero")
        x_in = sem("x_in")
        early_in = sem("early_in")
        wv_in = sem("wv_in")
        slab_in = [sem("slab_in%d" % j) for j in range(8)]
        slab_used = sem("slab_used")
        mod_ready = sem("mod_ready")
        mod_turned = sem("mod_turned")
        mod_stored = sem("mod_stored")
        const_in = sem("const_in")
        scaled = sem("scaled")
        sq_ready = sem("sq_ready")
        sq_added = sem("sq_added")
        sq_prod = sem("sq_prod")
        rstd_in = sem("rstd_in")
        rstd_ready = sem("rstd_ready")
        rstd_row = sem("rstd_row")
        h_f32 = sem("h_f32")
        h_hi_done = sem("h_hi_done")
        h_lo_done = [sem("h_lo_even"), sem("h_lo_odd")]
        wv_hi = sem("wv_hi")
        wv_lo = sem("wv_lo")
        v_prod = sem("v_prod")
        v_act = sem("v_act")
        v_dve = sem("v_dve")
        v_done = sem("v_done")
        masked = sem("masked")
        gap_zero = sem("gap_zero")
        raw_in = sem("raw_in")
        hi_done = sem("hi_done")
        lo_done = sem("lo_done")
        grp = sem("grp")
        evac = [sem("evac0"), sem("evac1")]
        gate_prod = sem("gate_prod")
        gate_read = sem("gate_read")
        y_done = sem("y_done")
        pooled = sem("pooled")
        pool_prod = sem("pool_prod")
        ln_sq = sem("ln_sq")
        ln_prod = sem("ln_prod")
        ln_mean = sem("ln_mean")
        ln_in = sem("ln_in")
        ln_rstd = sem("ln_rstd")
        ln_y = sem("ln_y")
        ln_norm = sem("ln_norm")
        dve_step = sem("dve_step")
        stored = sem("stored")
        tails_b = sem("tails_b")
        tails_p = sem("tails_p")
        m_ready = sem("m_ready")
        m_hi_done, m_lo_done = sem("m_hi_done"), sem("m_lo_done")
        wo_in = [sem("wo_in%d" % j) for j in range(3)]
        wo_hi_done = sem("wo_hi_done")
        wo_lo_done = [sem("wo_lo_even"), sem("wo_lo_odd")]
        rows_s_in = sem("rows_s_in")
        r3_in = sem("r3_in")
        rows_in = sem("rows_in")
        xt_in = [sem("xt_in0"), sem("xt_in1")]
        o_prod = sem("o_prod")
        o_read = sem("o_read")
        x1_done = sem("x1_done")
        x1_out = [sem("x1_out0"), sem("x1_out1")]
        x1_sq = sem("x1_sq")
        x1_var = sem("x1_var")
        x1_rstd = sem("x1_rstd")
        h2_done = sem("h2_done")
        h2_out = [sem("h2_out0"), sem("h2_out1")]
        h2_turned = sem("h2_turned")
        h2T_done = sem("h2T_done")
        logit_prod = sem("logit_prod")
        logit_read = sem("logit_read")
        gexp_in, gexp_done = sem("gexp_in"), sem("gexp_done")
        eexp_in, eexp_done = sem("eexp_in"), sem("eexp_done")
        mask_done = sem("mask_done")
        rank_prod = sem("rank_prod")
        expert_in, expert_prod = sem("expert_in"), sem("expert_prod")
        blocks_done = sem("blocks_done")
        hot_done, table_prod = sem("hot_done"), sem("table_prod")
        table_done = sem("table_done")
        idx_done = sem("idx_done")
        xg_in = [sem("xg_in0"), sem("xg_in1")]
        we_in = [sem("we_in%d" % j) for j in range(WB)]
        wd_in = [sem("wd_in%d" % j) for j in range(WB)]
        turned = sem("turned")
        xgT_done = sem("xgT_done")
        gu_prod = sem("gu_prod")
        silu_done = sem("silu_done")
        hm_done = sem("hm_done")
        hm_turned = sem("hm_turned")
        hmT_done = sem("hmT_done")
        y_prod = sem("y_prod")
        y_copied = sem("y_copied")
        y_out = [sem("y_out0"), sem("y_out1")]
        gathers = sem("gathers")
        fg_in, g2_in = sem("fg_in"), sem("g2_in")
        y12_in = [sem("y12_in%d" % j) for j in range(TILES)]
        x1_in = [sem("x1_in%d" % j) for j in range(YB)]
        y1_scaled = sem("y1_scaled")
        c_sq_in, c_sq = sem("c_sq_in"), sem("c_sq")
        c_var, c_rstd = sem("c_var"), sem("c_rstd")
        c_normed, c_done = sem("c_normed"), sem("c_done")
        out_st = [sem("out_st%d" % j) for j in range(YB)]
        y12 = we[:, :, :].rearrange("p a n -> p (a n)").rearrange("p (t c n) -> p t c n", c=2, n=D)

        modd = nc.dram_tensor("mod_scratch", (2, P, 512), F32).ap()
        x1d = nc.dram_tensor("x1_scratch", (T, D), F32).ap()
        h2d = nc.dram_tensor("h2_scratch", (T, D), F32).ap()
        yd = nc.dram_tensor("y_scratch", (BLOCKS * P, D), F32).ap()

        def tile_rows(t):
            return (t * P, P) if t < TILES - 1 else (LP, NS)

        def r(name):
            a, b = R3[name]
            return r3[:, a:b]

        def send(sp, t):
            at, n = tile_rows(t)
            sp.wait_ge(c_done, t + 1)
            sp.dma_start(O["y"][at:at + n, :], x1[0:n, t % YB, :]).then_inc(out_st[t % YB], 16)

        def load_x1(sp, t):
            at, n = tile_rows(t)
            sp.dma_start(x1[0:n, t % YB, :], x1d[at:at + n, :]).then_inc(x1_in[t % YB], 16)

        def load_rows(sp, dst, dst_s, vec, done):
            by_vector = modd.rearrange("s (j v) n -> s v j n", v=32)
            halves = slice(2 * (vec % 2), 2 * (vec % 2) + 2)
            two_ = lambda ap: ap.rearrange("p (a n) -> p a n", a=2)
            if dst is not None:
                sp.dma_start(two_(dst), by_vector[vec // 2, 0, halves, :].partition_broadcast(P)).then_inc(done, 16)
            if dst_s is not None:
                sp.dma_start(two_(dst_s), by_vector[vec // 2, 1:NV, halves, :]).then_inc(done, 16)

        def pooled_in(ch):
            return 2 if ch % 2 == 0 else 1

        block = ctx.enter_context(nc.Block())

        @block.sync
        def _(sp):
            sp.dma_start(sm[:, 0:LOADED], A["small"]).then_inc(small_in, 16)

            def load_slab(j):
                sp.dma_start(slab[j], A["w_mod"][j]).then_inc(slab_in[j if j < 8 else j % 4], 16)

            sp.dma_start(xT, A["xT"]).then_inc(x_in, 16)
            for j in range(8):
                load_slab(j)
                if j == 4:
                    sp.dma_start(m[:, 0:KD * W], A["early"][:, 0:KD * W]).then_inc(wv_in, 16)
                if j == 6:
                    sp.dma_start(mod_const[:, :, :], A["mod_const"].rearrange("p (s n) -> p s n", s=4)).then_inc(const_in, 16)
            rawf = raw[:, :, :].rearrange("p a n -> p (a n)")
            sp.dma_start(m[:, KD * W:EARLY_LOADED], A["early"][:, KD * W:]).then_inc(early_in, 16)
            sp.dma_start(rawf, A["w_mix"][0]).then_inc(raw_in, 16)
            for j in range(8, 24):
                if j == 8:
                    sp.wait_ge(wv_lo, 2)
                elif j == 10:
                    for a in range(2):
                        sp.wait_ge(h_lo_done[a], KD // 2)
                elif j >= 12:
                    sp.wait_ge(slab_used, j - 3)
                load_slab(j)
            for s in range(2):
                sp.wait_ge(mod_ready, s + 2)
                sp.dma_start(modd[s], mod_rows[s + 1]).then_inc(mod_stored, 16)
            sp.wait_ge(zeros_ready, 1)
            sp.dma_start(O["keep_b"], A["state_b"][:, 1:2, :]).then_inc(stored, 16)
            sp.dma_start(O["keep_p"], A["state_p"][:, 1:PC, :]).then_inc(stored, 16)
            sp.dma_start(O["keep_d"], A["state_d"][:, 1:CD - 1, :]).then_inc(stored, 16)

            pair, gpair = 0, 0
            for name in ("D", "A", "gA", "B", "gB", "C", "gC", "gD"):
                n = MIX_PAIRS.get(name, KD)
                src, at = (A["w_mix"], pair) if name in MIX_PAIRS else (A["w_gate"], gpair)
                q0 = Q0[name]
                width = src.shape[2]
                with sp.Fori(1 if name == "D" else 0, n) as i:
                    sp.wait_ge(hi_done, q0 + 2 * i)
                    sp.wait_ge(lo_done, q0 + 2 * i)
                    sp.dma_start(rawf[:, 0:width], src[bass.ds(at + i, 1)].rearrange("o p n -> (o p) n")
                                 ).then_inc(raw_in, 16)
                    if name not in MIX_PAIRS:
                        for a in range(2):
                            sp.dma_start(yd[bass.ds((i + (MIN_BLOCKS + gpair)) * P, P), a * 512:(a + 1) * 512],
                                         zeros[:, :]).then_inc(y_zero, 16)
                if name in MIX_PAIRS:
                    pair += n
                else:
                    gpair += n
                if name == "D":
                    sp.wait_ge(v_done, TILES)
                    sp.dma_start(O["v_s"], e("vs")[0:NS, :]).then_inc(stored, 16)
                if name == "gA":
                    sp.wait_ge(evac[1], evacuated(9))
                    sp.dma_start(O["tail_d"], gl[:, :, LP:LP + CD - 1 + NS]).then_inc(stored, 16)
            sp.wait_ge(tails_b, 1)
            sp.dma_start(O["tail_b"], tail_b).then_inc(stored, 16)
            sp.wait_ge(tails_p, 1)
            sp.dma_start(O["tail_p"], tail_p).then_inc(stored, 16)

            def load_wo(k):
                if k >= 3:
                    for a in range(2):
                        sp.wait_ge(wo_lo_done[a], (k - 1 - a) // 2)
                sp.dma_start(wo_raw[k % 3], A["w_out"][:, k, :]).then_inc(wo_in[k % 3], 16)

            def load_x(t):
                at, n = tile_rows(t)
                sp.dma_start(xt[0:n, t % 2, :], A["x_tok"][at:at + n, :]).then_inc(xt_in[t % 2], 16)

            sp.wait_ge(hi_done, N_GROUPS)
            sp.wait_ge(lo_done, N_GROUPS)
            for k in range(3):
                load_wo(k)
            sp.wait_ge(grp, N_GROUPS)
            sp.wait_ge(mod_stored, 32)
            vectors = (0, 2, 1)
            load_x(0)
            for k in range(3, KD):
                if k < 6:
                    load_rows(sp, rows[:, k - 3, :], None, vectors[k - 3], rows_in)
                load_wo(k)
            load_x(1)
            sp.dma_start(r3[:, :], A["routing"]).then_inc(r3_in, 16)
            sp.wait_ge(wo_lo_done[0], KD // 2)
            sp.wait_ge(wo_lo_done[1], KD // 2)
            sp.wait_ge(m_lo_done, KD)
            for j, vec in enumerate(vectors):
                load_rows(sp, None, rows_s[0:NS, j, :], vec, rows_s_in)
            for t in range(TILES):
                at, n = tile_rows(t)
                sp.wait_ge(x1_done, t + 1)
                sp.dma_start(x1d[at:at + n, :], xt[0:n, t % 2, :]).then_inc(x1_out[t % 2], 16)
                sp.wait_ge(h2_done, t + 1)
                sp.dma_start(h2d[at:at + n, :], h2[0:n, t % 2, :]).then_inc(h2_out[t % 2], 16)
                if t + 2 < TILES:
                    sp.wait_ge(x1_out[t % 2], 16 * (t // 2 + 1))
                    n2 = tile_rows(t + 2)[1]
                    sp.dma_start(xt[0:n2, t % 2, :], A["x_tok"][(t + 2) * P:(t + 2) * P + n2, :]
                                 ).then_inc(xt_in[t % 2], 16)

            sp.wait_ge(blocks_done, 1)
            sp.wait_ge(rank_prod, 1)
            sp.wait_ge(x1_out[0], 16 * 5)
            sp.wait_ge(x1_out[1], 16 * 4)
            sp.wait_ge(h2_out[0], 16 * 5)
            sp.wait_ge(h2_out[1], 16 * 4)

            def load_experts(b, place, wait):
                ex = sp.value_load(block_e[0:1, bass.ds(b, 1)], min_val=0, max_val=NE - 1)
                if wait:
                    sp.wait_ge(gu_prod, b - 3)
                sp.dma_start(we[:, place, 0:GUW], A["w_exp"][bass.ds(ex, 1), :, 0:GUW].rearrange("o p n -> (o p) n")
                             ).then_inc(we_in[place], 16)
                if wait:
                    sp.wait_ge(y_prod, b - 3)
                sp.dma_start(we[:, place, GUW:], A["w_exp"][bass.ds(ex, 1), :, GUW:].rearrange("o p n -> (o p) n")
                             ).then_inc(wd_in[place], 16)

            for b in range(WB):
                if b == 2:
                    sp.wait_ge(gathers, 2)
                    sp.wait_ge(blocks_done, 2)
                load_experts(b, b, False)
            rest = sp.value_load(block_e[0:1, BLOCKS:BLOCKS + 1], min_val=0, max_val=NPAIR - 1)
            with sp.Fori(0, NPAIR // 2 - 1) as j:
                for pair in range(2):
                    with sp.If(2 * j + pair + 2 < rest + 1):
                        for s in range(2):
                            load_experts(4 * j + 4 + 2 * pair + s, 2 * pair + s, True)
            sp.wait_ge(y_zero, 16 * 2 * (BLOCKS - MIN_BLOCKS))
            load_rows(sp, g2r[:, 0, :], g2r[0:NS, 1, :], 3, g2_in)
            sp.dma_start(fg[:, :], A["final_g"]).then_inc(fg_in, 16)
            for t in range(YB):
                load_x1(sp, t)
            for t in range(TILES):
                send(sp, t)
                if t >= 1 and t + YB - 1 < TILES:
                    sp.wait_ge(out_st[t - 1], 16)
                    load_x1(sp, t + YB - 1)
            for j in range(YB):
                sp.wait_ge(out_st[j], 16 * (2 if j + YB < TILES else 1))
            sp.wait_ge(stored, 16 * 7)

        @block.tensor
        def _(pe):
            pe.wait_ge(small_in, 16)
            def mod_slab(j):
                pe.wait_ge(slab_in[j if j < 8 else j % 4], 16 if j < 8 else 16 * (j // 4))
                k = j % KD
                for q in range(4):
                    mmi = pe.matmul(ps[32 * q:32 * q + 32, 7 if j // KD == 2 else 6, :], cT[:, k, :],
                                    slab[j][:, q * 512:(q + 1) * 512], start=(k == 0), stop=(k == KD - 1))
                mmi.then_inc(slab_used, 1)

            for j in range(8):
                mod_slab(j)
                if j == 2:
                    pe.wait_ge(sq_added, KD - 1)
                    for t in range(TILES):
                        at, n = tile_rows(t)
                        mmi = pe.matmul(ps[0:n, 0, t:t + 1], sbf(2, at, n), ones[:, 0:1], start=True, stop=True)
                    mmi.then_inc(sq_prod, 1)
                if j == 3:
                    pe.wait_ge(rstd_ready, 1)
                    for t in range(TILES):
                        at, n = tile_rows(t)
                        mmi = pe.matmul(ps[:, 3 + t // 4, (t % 4) * P:(t % 4) * P + n], st[0:n, t:t + 1].to_broadcast([n, P]),
                                        ident[0:n, 0:n], start=True, stop=True)
                    mmi.then_inc(rstd_row, 1)
            pe.wait_ge(mod_ready, 1)
            for n in range(4):
                mmi = pe.transpose(ps[:, 7, n * P:(n + 1) * P], mod_rows[0][:, n * P:(n + 1) * P], ident)
            mmi.then_inc(mod_turned, 1)
            for t in range(TILES):
                at, n = tile_rows(t)
                if t == 0:
                    pe.wait_ge(evac[0], 1)
                elif t > 1:
                    pe.wait_ge(evac[t % 2], (1 if t % 2 == 0 else 0) + t // 2)
                for k in range(KD):
                    if t == 0:
                        pe.wait_ge(wv_lo, 1 + k // 4)
                        pe.wait_ge(h_lo_done[k % 2], k // 2 + 1)
                    for x, (l, w) in enumerate(((h_hi, wvh), (h_hi, wvl), (h_lo, wvh))):
                        mmi = pe.matmul(ps[0:n, 3 * (t % 2), :], l[:, k, at:at + n], w[:, k, :],
                                        start=(k == 0 and x == 0), stop=(k == KD - 1 and x == 2))
                mmi.then_inc(v_prod, 1)
                if t < 8:
                    mod_slab(8 + 2 * t)
                    mod_slab(9 + 2 * t)

            def group(q, s, before, rh, rl, nk):
                pe.wait_ge(hi_done, q + 1)
                pe.wait_ge(lo_done, q + 1)
                pe.wait_ge(evac[s], before)
                for k in range(nk):
                    for x, (w, rr) in enumerate(((w_hi, rh), (w_hi, rl), (w_lo, rh))):
                        for a in range(NT):
                            mmi = pe.matmul(ps[:, 3 * s + a, 0:TT], w[:, s, k, :], rr[:, k, a, :],
                                            start=(k == 0 and x == 0), stop=(k == nk - 1 and x == 2))
                mmi.then_inc(grp, 1)

            def pairs_of(name, first=0):
                q0 = Q0[name]
                gates = name[0] == "g"
                with pe.Fori(first, MIX_PAIRS.get(name, KD)) as i:
                    group(q0 + 2 * i, 0, evacuated(q0) + i, h3h, h3l, KD)
                    if gates:
                        pe.wait_ge(y_done, KW * (1 + "ABCD".index(name[1])))
                        group(q0 + 2 * i + 1, 1, evacuated(q0 + 1) + i, yh3, yl3, KW)
                    else:
                        group(q0 + 2 * i + 1, 1, evacuated(q0 + 1) + i, h3h, h3l, KD)

            pairs_of("D")
            pe.wait_ge(masked, 1)
            pe.wait_ge(v_done, TILES)
            pe.wait_ge(mod_ready, 3)
            for g in range(KW):
                q, s = Q0["A"] + g, g % 2
                if g:
                    pe.wait_ge(gate_read, g)
                for n in range(8):
                    pe.matmul(ps[:, 6 + n // 4, (n % 4) * P:(n % 4 + 1) * P], vn[:, n, g * P:(g + 1) * P],
                              aws[:, g, :], start=True, stop=True)
                pe.wait_ge(evac[s], evacuated(q))
                pe.matmul(ps[:, 3 * s, 400:400 + NS], e("vs")[0:NS, g * P:(g + 1) * P], ident[0:NS, 0:NS],
                          start=True, stop=True).then_inc(gate_prod, 1)
                group(q, s, evacuated(q), h3h, h3l, KD)
            pairs_of("gA")
            pairs_of("B")
            pairs_of("gB")

            def pool_mix(ch):
                s = ch % 2
                pe.wait_ge(pooled, ch + 1)
                for a in range(NT):
                    mmi = pe.matmul(ps[:, 3 * s + a, 0:TT], poolw[:, ch, :],
                                    sbf(pooled_in(ch), PC + a * TT, TT), start=True, stop=True)
                mmi.then_inc(pool_prod, 1)

            def ln_sums(which):
                pe.wait_ge(evac[1], evacuated(Q0["C"] + 1 + 2 * which) - 1)
                for ch in range(KW):
                    if which == 1:
                        pe.wait_ge(ln_sq, ch + 1)
                    elif ch == 0:
                        pe.wait_ge(ln_in, 1)
                    for a in range(NT):
                        rhs = dc[:, ch, a * TT:(a + 1) * TT] if which == 0 else ln_row(ch + 1)[:, a * TT:(a + 1) * TT]
                        mmi = pe.matmul(ps[:, 3 + a, 0:TT], ones, rhs, start=(ch == 0), stop=(ch == KW - 1))
                    mmi.then_inc(ln_prod, 1)

            for ch in range(KW):
                q = Q0["C"] + ch
                if ch == 1:
                    ln_sums(0)
                if ch == 2:
                    pool_mix(0)
                if ch == 3:
                    pool_mix(1)
                    ln_sums(1)
                group(q, ch % 2, evacuated(q), h3h, h3l, KD)
            pool_mix(2)
            group(Q0["gC"], 0, evacuated(Q0["gC"]), h3h, h3l, KD)
            pool_mix(3)
            pe.wait_ge(y_done, 3 * KW)
            group(Q0["gC"] + 1, 1, evacuated(Q0["gC"] + 1), yh3, yl3, KW)
            pairs_of("gC", 1)
            pairs_of("gD")


            def project(t):
                at, n = tile_rows(t)
                b = 2 * (t % 2)
                if t < 2:
                    pe.wait_ge(evac[t], evacuated(N_GROUPS - 2 + t) + 1)
                else:
                    pe.wait_ge(o_read, t - 1)
                for k in range(KD):
                    if t == 0:
                        pe.wait_ge(wo_lo_done[k % 2], k // 2 + 1)
                        pe.wait_ge(m_lo_done, k + 1)
                    for x, (l, w) in enumerate(((m_hi, wo_hi), (m_hi, wo_lo), (m_lo, wo_hi))):
                        for a in range(2):
                            mmi = pe.matmul(ps[0:n, b + a, :], l[:, k, at:at + n], w[:, k, a * 512:(a + 1) * 512],
                                            start=(k == 0 and x == 0), stop=(k == KD - 1 and x == 2))
                mmi.then_inc(o_prod, 1)

            def turn_h2(t):
                at, n = tile_rows(t)
                pe.wait_ge(h2_done, t + 1)
                if t:
                    pe.wait_ge(h2T_done, t)
                for k in range(KD):
                    mmi = pe.transpose(ps[:, 4 + k // 4, (k % 4) * P:(k % 4) * P + n],
                                       h2[0:n, t % 2, k * P:(k + 1) * P], ident[0:n, 0:n])
                mmi.then_inc(h2_turned, 1)

            def logits(t):
                at, n = tile_rows(t)
                pe.wait_ge(h2T_done, t + 1)
                if t:
                    pe.wait_ge(logit_read, t)
                else:
                    pe.wait_ge(r3_in, 16)
                for k in range(KD):
                    mmi = pe.matmul(ps[0:n, 6, 0:36], h2T[:, k, 0:n], r("wr").rearrange("p (k n) -> p k n", k=KD)[:, k, :],
                                    start=(k == 0), stop=(k == KD - 1))
                mmi.then_inc(logit_prod, 1)

            MS = MK[:, 2, :].rearrange("p (t e) -> p t e", t=TILES)

            def ranks(t):
                pe.wait_ge(mask_done, min(t + 1, TILES))
                for u in range(min(t + 1, TILES)):
                    mmi = pe.matmul(ps[:, 7, t * NE:(t + 1) * NE], r("tri") if u == t else ones, MS[:, u, :],
                                    start=(u == 0), stop=(u == min(t, TILES - 1)))
                return mmi

            for t in range(TILES + 2):
                if t < TILES:
                    project(t)
                if t > 1:
                    logits(t - 2)
                if 0 < t <= TILES:
                    turn_h2(t - 1)
                if t > 2:
                    ranks(t - 3)
            ranks(TILES - 1)
            ranks(TILES).then_inc(rank_prod, 1)
            pe.wait_ge(expert_in, 1)
            pe.matmul(ps[:, 5, 0:BLOCKS], rt[:, BE:BE + 1].to_broadcast([P, P]), ident[:, 0:BLOCKS], start=True, stop=True
                      ).then_inc(expert_prod, 1)
            pe.wait_ge(hot_done, 1)
            for j in range(2 * TILES):
                mmi = pe.matmul(ps[:, 6, 0:BLOCKS], in_place[:, j, :], in_block[:, j, :],
                                start=(j == 0), stop=(j == 2 * TILES - 1))
            mmi.then_inc(table_prod, 1)

            pe.wait_ge(table_done, 1)
            pe.wait_ge(blocks_done, 2)
            rest = pe.value_load(block_e[0:1, BLOCKS:BLOCKS + 1], min_val=0, max_val=NPAIR - 1)

            odd = pe.value_load(block_e[0:1, BLOCKS + 1:BLOCKS + 2], min_val=0, max_val=1)

            def turn(i, s, first=False):
                b = 2 * i + s
                pe.wait_ge(xg_in[s], 16 * (i + 1))
                if not first:
                    pe.wait_ge(xgT_done, b)
                for k in range(KD):
                    mmi = pe.transpose(ps[:, k // 4, (k % 4) * P:(k % 4 + 1) * P], xg[:, s, k * P:(k + 1) * P], ident)
                mmi.then_inc(turned, 1)

            def turn_hidden(b):
                pe.wait_ge(hm_done, b + 1)
                for f in range(2):
                    mmi = pe.transpose(ps[:, 4, f * P:(f + 1) * P], hm[:, f * P:(f + 1) * P], ident)
                mmi.then_inc(hm_turned, 1)

            def gate_up(b, s, place, loads):
                pe.wait_ge(we_in[place], 16 * loads)
                pe.wait_ge(xgT_done, b + 1)
                wv = we[:, place, 0:KD * 2 * FE].rearrange("p (k n) -> p k n", k=KD)
                for k in range(KD):
                    mmi = pe.matmul(ps[:, 2 + s, :], xgT[:, s, k, :], wv[:, k, :], start=(k == 0), stop=(k == KD - 1))
                mmi.then_inc(gu_prod, 1)

            def down(b, place, loaded, first=False):
                pe.wait_ge(wd_in[place], loaded)
                pe.wait_ge(hmT_done, b + 1)
                if not first:
                    pe.wait_ge(y_copied, b)
                wv = we[:, place, KD * 2 * FE:].rearrange("p (f n) -> p f n", f=2)
                for a in range(2):
                    for f in range(2):
                        mmi = pe.matmul(ps[:, 5 + a, :], hmT[:, f, :], wv[:, f, a * 512:(a + 1) * 512],
                                        start=(f == 0), stop=(f == 1))
                mmi.then_inc(y_prod, 1)

            turn(0, 0, first=True)
            turn(0, 1)
            gate_up(0, 0, 0, 1)
            turn(1, 0)
            turn_hidden(0)
            gate_up(1, 1, 1, 1)
            down(0, 0, 16, first=True)
            with pe.Fori(0, NPAIR // 2) as j:
                for p in range(2):
                    i = 2 * j + 1 + p
                    with pe.If(i < rest + 1):
                        for s in range(2):
                            b, place = 4 * j + 2 + 2 * p + s, (2 + 2 * p + s) % WB
                            turn(i + s, 1 - s)
                            turn_hidden(b - 1)
                            gate_up(b, s, place, j + 1 + p)
                            down(b - 1, (place - 1) % WB, 16 * j + 16 + 16 * (p if s else 0))
            turn_hidden(2 * rest + 1)
            with pe.If(odd > 0):
                down(2 * rest + 1, 1, 8 * rest + 16)
            with pe.If(odd < 1):
                down(2 * rest + 1, 3, 8 * rest + 8)

        @block.scalar
        def _(act):
            act.wait_ge(x_in, 16)
            act.wait_ge(small_in, 16)
            for k in range(KD):
                if k >= 2:
                    act.wait_ge(sq_added, max(1, k - 2))
                act.activation(sbf(k % 2), xT[:, k, :], ACT.Square).then_inc(sq_ready, 1)
            act.wait_ge(rstd_in, 1)
            act.activation(st[:, 0:TILES], st[:, 0:TILES], ACT.Sqrt).then_inc(rstd_ready, 1)
            act.wait_ge(wv_in, 16)
            for a in range(2):
                half = slice(a * KD * W // 2, (a + 1) * KD * W // 2)
                act.activation(y_hi[:, half], e("wv")[:, half], ACT.Copy).then_inc(wv_hi, 1)
            act.wait_ge(h_f32, 1)
            act.activation(h_hi[:, :, LP:T], h_f[:, :, LP:T], ACT.Copy).then_inc(h_hi_done, 1)
            for k in range(KD):
                act.activation(h_hi[:, k, 0:LP], xT[:, k, 0:LP], ACT.Identity, bias=modT[:, k, 0:1],
                               scale=modT[:, 8 + k, 0:1]).then_inc(h_hi_done, 1)
            def split_hi(pr, s, wait=True):
                act.wait_ge(raw_in, 16 * (pr + 1))
                if wait:
                    act.wait_ge(grp, 2 * pr + s - 1)
                act.activation(w_hi[:, s, :, :].rearrange("p k n -> p (k n)"), raw[:, s, :], ACT.Copy
                               ).then_inc(hi_done, 1)

            for t in range(TILES):
                n, s = tile_rows(t)[1], t % 2
                act.wait_ge(v_prod, t + 1)
                if t >= 2:
                    act.wait_ge(v_done, t - 1)
                if t == 2:
                    split_hi(0, 0, False)
                    split_hi(0, 1, False)
                act.activation(sbf(s, 0, W)[0:n], ps[0:n, 3 * s, :], ACT.Gelu_apprx_tanh,
                               accum_out=st[0:n, 4 * s:4 * s + 1]).then_inc(evac[s], 1)
                act.wait_ge(v_dve, 2 * t + 1)
                act.activation(sbf(2, 0, W)[0:n], sbf(s, 0, W)[0:n], ACT.Square,
                               accum_out=st[0:n, 4 * s + 1:4 * s + 2]).then_inc(v_act, 1)
                act.wait_ge(v_dve, 2 * t + 2)
                act.activation(st[0:n, 4 * s + 2:4 * s + 3], st[0:n, 4 * s + 2:4 * s + 3], ACT.Sqrt).then_inc(v_act, 1)

            act.wait_ge(v_done, TILES)

            with act.Fori(0, 4) as i:
                act.wait_ge(grp, 2 * i + 1)
                act.wait_ge(evac[1], evacuated(1) + i)
                act.activation(three(sbf(0)), pset(0), ACT.Sigmoid).then_inc(evac[0], 1)
                split_hi(i + 1, 0)
                split_hi(i + 1, 1)
            for g in range(KW):
                q, s = Q0["A"] + g, g % 2
                act.wait_ge(grp, q + 1)
                if g < 2:
                    act.wait_ge(evac[1], evacuated(7) + 1)
                    act.wait_ge(mod_stored, 32)
                else:
                    act.wait_ge(y_done, g - 1)
                act.activation(smp[:, s, :], ps[:, 3 * s, 400:400 + NS], ACT.Identity, bias=c("bs00")[:, g:g + 1],
                               scale=c("ws00")[:, g:g + 1])
                act.activation(three(sbf(s)), pset(s), ACT.Gelu_apprx_tanh).then_inc(evac[s], 1)
                split_hi(q // 2 + 1, s)

            def merged_hi(j):
                act.wait_ge(m_ready, j + 1)
                act.activation(m_hi[:, bass.ds(j, 1), :].rearrange("p o t -> p (o t)"),
                               mm[:, bass.ds(j, 1), :].rearrange("p o t -> p (o t)"), ACT.Copy).then_inc(m_hi_done, 1)

            def gates(name, between=None):
                q0 = Q0[name]

                def pair(i, more=True):
                    act.wait_ge(grp, q0 + 2 * i + 1)
                    act.wait_ge(evac[1], evacuated(q0 + 1) + i)
                    act.activation(three(sbf(0)), pset(0), ACT.Sigmoid).then_inc(evac[0], 1)
                    if more:
                        split_hi(q0 // 2 + i + 1, 0)
                        act.wait_ge(grp, q0 + 2 * i + 2)
                        split_hi(q0 // 2 + i + 1, 1)

                act.wait_ge(y_done, KW * (1 + "ABCD".index(name[1])))
                if between:
                    pair(0)
                    between()
                if name != "gD":
                    with act.Fori(1 if between else 0, KD) as i:
                        pair(i)
                    return
                pair(0)
                with act.Fori(1, KD - 1) as i:
                    pair(i)
                    merged_hi(i - 1)
                pair(KD - 1, False)
                merged_hi(KD - 2)

            gates("gA")
            for j in range(3 * KW):
                q, s = Q0["B"] + j, j % 2
                act.wait_ge(grp, q + 1)
                if j % 3 == 0:
                    act.wait_ge(evac[(q - 2) % 2] if j else evac[1], evacuated(q - 2) + 1 if j else evacuated(q - 1) + 1)
                    act.activation(three(sbf(0)), pset(s), ACT.Copy).then_inc(evac[s], 1)
                split_hi(q // 2 + 1, s)
            gates("gB")
            for ch in range(KW):
                q, s = Q0["C"] + ch, ch % 2
                act.wait_ge(grp, q + 1)
                if ch:
                    act.wait_ge(pooled, ch)
                else:
                    act.wait_ge(gap_zero, 1)
                act.activation(three(sbf(0, PC)), pset(s), ACT.Copy).then_inc(evac[s], 1)
                split_hi(q // 2 + 1, s)
                if ch == 1:
                    for j in range(KW):
                        act.wait_ge(ln_mean, j + 1)
                        act.activation(ln_row(j + 1), dc[:, j, :], ACT.Square).then_inc(ln_sq, 1)
            act.wait_ge(ln_rstd, 1)
            act.activation(ln_row(1), ln_row(1), ACT.Sqrt).then_inc(ln_rstd, 1)

            def silus():
                for ch in range(KW):
                    act.wait_ge(ln_norm, ch + 1)
                    act.activation(dc[:, ch, :], dc[:, ch, :], ACT.Silu, bias=c("dlb")[:, ch:ch + 1],
                                   scale=c("dlg")[:, ch:ch + 1]).then_inc(ln_y, 1)

            gates("gC", silus)
            act.wait_ge(ln_y, KW)
            act.wait_ge(grp, Q0["gD"])
            for ch in range(KW):
                act.activation(yh[:, ch, :], dc[:, ch, :], ACT.Copy).then_inc(ln_y, 1)
            gates("gD")
            act.wait_ge(grp, N_GROUPS - 1)
            for k in range(KD):
                if k == 2:
                    merged_hi(KD - 1)
                act.wait_ge(wo_in[k % 3], 16 * (k // 3 + 1))
                act.activation(wo_hi[:, k, :], wo_raw[k % 3], ACT.Copy).then_inc(wo_hi_done, 1)

            def normalise(t):
                n, s = tile_rows(t)[1], t % 2
                act.wait_ge(x1_done, t + 1)
                act.activation(sq[0:n, :], xt[0:n, s, :], ACT.Square, accum_out=rt[0:n, 140:141]).then_inc(x1_sq, 1)
                act.wait_ge(x1_var, t + 1)
                act.activation(rt[0:n, 141:142], rt[0:n, 141:142], ACT.Sqrt).then_inc(x1_rstd, 1)

            def h2_columns(t):
                n = tile_rows(t)[1]
                act.wait_ge(h2_turned, t + 1)
                if t:
                    act.wait_ge(logit_prod, t)
                act.activation(h2T[:, :, 0:n].rearrange("p (a k) n -> p a k n", a=2),
                               ps[:, 4:6, :].rearrange("p a (k n) -> p a k n", k=4)[:, :, :, 0:n], ACT.Copy
                               ).then_inc(h2T_done, 1)

            def exponentials(t):
                n = tile_rows(t)[1]
                act.wait_ge(gexp_in, t + 1)
                act.activation(rt[0:n, 60:64], rt[0:n, 0:4], ACT.Exp, bias=rt[0:n, 142:143],
                               accum_out=rt[0:n, 143:144]).then_inc(gexp_done, 1)
                act.wait_ge(eexp_in, t + 1)
                act.activation(rt[0:n, 145:146], rt[0:n, 144:145], ACT.Exp).then_inc(eexp_done, 1)

            for t in range(TILES + 2):
                if t < TILES:
                    normalise(t)
                if 0 < t <= TILES:
                    h2_columns(t - 1)
                if t > 1:
                    exponentials(t - 2)

            act.wait_ge(table_done, 1)
            act.wait_ge(blocks_done, 2)
            act.wait_ge(y_zero, 16 * 2 * (BLOCKS - MIN_BLOCKS))
            rest = act.value_load(block_e[0:1, BLOCKS:BLOCKS + 1], min_val=0, max_val=NPAIR - 1)

            def columns_out(b, s, used=True):
                act.wait_ge(turned, b + 1)
                if used:
                    act.wait_ge(gu_prod, b - 1)
                act.activation(xgT[:, s, :, :].rearrange("p (a k) n -> p a (k n)", a=2), ps[:, 0:2, :], ACT.Copy
                               ).then_inc(xgT_done, 1)

            def silu(b, s, used=True):
                act.wait_ge(gu_prod, b + 1)
                if used:
                    act.wait_ge(hm_done, b)
                act.activation(sg[:, :], ps[:, 2 + s, 0:FE], ACT.Silu).then_inc(silu_done, 1)

            def store(b, s):
                act.wait_ge(y_copied, b + 1)
                act.dma_start(yd[bass.ds(b * P, P), :], yb[:, s, :]).then_inc(y_out[s], 16)

            columns_out(0, 0, False)
            columns_out(1, 1, False)
            silu(0, 0, False)
            columns_out(2, 0)
            silu(1, 1)
            store(0, 0)
            with act.Fori(1, NPAIR) as i:
                with act.If(i < rest + 1):
                    for s in range(2):
                        columns_out(2 * i + s + 1, 1 - s)
                        silu(2 * i + s, s)
                        store(2 * i + s - 1, 1 - s)
            store(2 * rest + 1, 1)
            act.wait_ge(y_out[0], 16 * rest + 16)
            act.wait_ge(y_out[1], 16 * rest + 16)
            def scale_y1(t):
                n = tile_rows(t)[1]
                act.wait_ge(y12_in[t], 32)
                act.activation(y12[0:n, t, 0, :], y12[0:n, t, 0, :], ACT.Copy, scale=wts[0:n, 0, t:t + 1]
                               ).then_inc(y1_scaled, 1)

            scale_y1(0)
            for t in range(TILES + 1):
                if t + 1 < TILES:
                    scale_y1(t + 1)
                if t < TILES:
                    n, j = tile_rows(t)[1], t % YB
                    act.wait_ge(c_sq_in, t + 1)
                    act.activation(y12[0:n, t, 0, :], x1[0:n, j, :], ACT.Square, accum_out=cs[0:n, 2 * (t % 2):2 * (t % 2) + 1]
                                   ).then_inc(c_sq, 1)
                if t:
                    n, v = tile_rows(t - 1)[1], 2 * ((t - 1) % 2) + 1
                    act.wait_ge(c_var, t)
                    act.activation(cs[0:n, v:v + 1], cs[0:n, v:v + 1], ACT.Sqrt).then_inc(c_rstd, 1)
                    act.wait_ge(c_rstd, t)
                    x = x1[0:n, (t - 1) % YB, :]
                    act.activation(x, x, ACT.Copy, scale=cs[0:n, v:v + 1]).then_inc(c_normed, 1)

        @block.gpsimd
        def _(pool):
            pool.memset(zeros[:, :], 0.0).then_inc(zeros_ready, 1)
            for a in range(2):
                half = slice(a * KD * W // 2, (a + 1) * KD * W // 2)
                pool.wait_ge(wv_hi, a + 1)
                pool.tensor_tensor(y_lo[:, half], e("wv")[:, half], y_hi[:, half].bitcast(F32), ALU.subtract
                                   ).then_inc(wv_lo, 1)
            for k in range(1, KD, 2):
                pool.wait_ge(h_f32, k + 2)
                pool.wait_ge(h_hi_done, k + 2)
                pool.tensor_tensor(h_lo[:, k, :], h_f[:, k, :], h_hi[:, k, :].bitcast(F32), ALU.subtract
                                   ).then_inc(h_lo_done[1], 1)
            pool.wait_ge(early_in, 16)
            pool.affine_select(out=aws, in_=aws, compare_op=ALU.is_ge, fill=0.0, base=0,
                               pattern=[[0, KW], [1, P]], channel_multiplier=-1).then_inc(masked, 1)

            def split_lo(pr, s, wait=True):
                pool.wait_ge(raw_in, 16 * (pr + 1))
                pool.wait_ge(hi_done, 2 * pr + s + 1)
                if wait:
                    pool.wait_ge(grp, 2 * pr + s - 1)
                pool.tensor_tensor(w_lo[:, s, :, :].rearrange("p k n -> p (k n)"), raw[:, s, :],
                                   w_hi[:, s, :, :].rearrange("p k n -> p (k n)").bitcast(F32), ALU.subtract
                                   ).then_inc(lo_done, 1)

            pool.wait_ge(mod_ready, 3)
            split_lo(0, 0, False)
            split_lo(0, 1, False)
            with pool.Fori(1, N_GROUPS // 2) as i:
                for s in range(2):
                    split_lo(i, s)

            for k in range(0, KD, 2):
                pool.wait_ge(wo_hi_done, k + 1)
                pool.tensor_tensor(wo_lo[:, k, :], wo_raw[k % 3], wo_hi[:, k, :].bitcast(F32), ALU.subtract
                                   ).then_inc(wo_lo_done[0], 1)

            pool.wait_ge(table_done, 1)
            pool.wait_ge(h2_out[0], 16 * 5)
            pool.wait_ge(h2_out[1], 16 * 4)

            def gather(i, s, used=True):
                b = 2 * i + s
                if used:
                    pool.wait_ge(turned, b - 1)
                pool.tensor_copy(idx[:, s:s + 1], table[:, bass.ds(b, 1)]).then_inc(idx_done, 1)
                pool.wait_ge(idx_done, b + 1)
                pool.sem_inc(gathers, 1)
                pool.indirect_dma_start(
                    xg[:, s, :], None, h2d, bass.IndirectOffsetOnAxis(ap=idx[:, s:s + 1].bitcast(U32), axis=0)
                ).then_inc(xg_in[s], 16)

            gather(0, 0, False)
            gather(0, 1, False)
            gather(1, 0)
            pool.wait_ge(blocks_done, 2)
            rest = pool.value_load(block_e[0:1, BLOCKS:BLOCKS + 1], min_val=0, max_val=NPAIR - 1)
            with pool.Fori(1, NPAIR) as i:
                with pool.If(i < rest + 1):
                    gather(i, 1)
                    gather(i + 1, 0)
            pool.wait_ge(y_out[0], 16 * rest + 16)
            pool.wait_ge(y_out[1], 16 * rest + 16)
            pool.sem_inc(gathers, 1)

            for t in range(TILES):
                n = tile_rows(t)[1]
                for ch in range(2):
                    j = ch * TILES + t
                    pool.indirect_dma_start(
                        y12[0:n, t, ch, :], None, yd,
                        bass.IndirectOffsetOnAxis(ap=slots[0:n, j:j + 1].bitcast(U32), axis=0)
                    ).then_inc(y12_in[t], 16)
            pool.wait_ge(fg_in, 16)
            for t in range(TILES):
                n, x = tile_rows(t)[1], x1[0:tile_rows(t)[1], t % YB, :]
                pool.wait_ge(c_normed, t + 1)
                pool.tensor_tensor(x, x, fg[0:n, :], ALU.mult).then_inc(c_done, 1)

        @block.vector
        def _(dve):
            steps = Steps(dve, dve_step)
            link = steps.link
            SUB, ADD, MUL = ALU.subtract, ALU.add, ALU.mult
            tt, ts, stt, cp = dve.tensor_tensor, dve.tensor_scalar, dve.scalar_tensor_tensor, dve.tensor_copy
            for k in range(1, KD):
                dve.wait_ge(sq_ready, k + 1)
                if k > 1:
                    dve.wait_ge(sq_added, k - 1)
                tt(sbf(2), sbf(0 if k == 1 else 2), sbf(k % 2), ADD).then_inc(sq_added, 1)
            dve.wait_ge(sq_prod, 1)
            link(dve.memset(st[:, 0:TILES], 1.0))
            link(ts(st[:, 0:TILES - 1], ps[:, 0, 0:TILES - 1], 1.0 / D, EPS, MUL, ADD))
            ts(st[0:NS, TILES - 1:TILES], ps[0:NS, 0, TILES - 1:TILES], 1.0 / D, EPS, MUL, ADD).then_inc(evac[0], 1)
            dve.wait_ge(evac[0], 1)
            dve.reciprocal(st[:, 0:TILES], st[:, 0:TILES]).then_inc(rstd_in, 1)
            dve.wait_ge(rstd_row, 1)
            tt(xT[:, :, LP:T], xT[:, :, LP:T], ps[:, 5, 0:NS].unsqueeze(1).to_broadcast([P, KD, NS]), MUL).then_inc(scaled, 1)
            for k in range(KD):
                tt(xT[:, k, 0:LP].rearrange("p (a n) -> p a n", a=2), xT[:, k, 0:LP].rearrange("p (a n) -> p a n", a=2),
                   ps[:, 3:5, :], MUL).then_inc(scaled, 1)

            def modulation(s, scale):
                R, at = mod_rows[s], slice(scale, scale + 64)
                link(tt(R, ps[:, 7 if s == 2 else 6, :], mod_const[:, s, :], ADD))
                if scale >= 0:
                    link(stt(R[at], R[at], 1.0, mod_const[at, 3, :], ADD, MUL))
                dve.engine_nop().then_inc(mod_ready, 1)

            dve.wait_ge(slab_used, 8)
            dve.wait_ge(small_in, 16)
            dve.wait_ge(const_in, 16)
            modulation(0, 64)
            dve.wait_ge(mod_turned, 1)
            link(cp(modT.rearrange("p (j n) v -> p n j v", j=4),
                    ps[:, 7, :].rearrange("p (n j v) -> p n j v", n=4, v=32)[:, :, :, 0:NV]))
            dve.wait_ge(scaled, KD + 1)
            hs = h_f[:, :, LP:T]
            link(tt(hs, xT[:, :, LP:T], modT[:, 8:16, 1:NV], MUL))
            tt(hs, hs, modT[:, 0:8, 1:NV], ADD).then_inc(h_f32, 1)
            for k in range(KD):
                hk = h_f[:, k, :]
                ts(hk[:, 0:LP], xT[:, k, 0:LP], modT[:, 8 + k, 0:1], modT[:, k, 0:1], MUL, ADD).then_inc(h_f32, 1)
                if k % 2:
                    dve.wait_ge(h_f32, k + 1)
                    dve.wait_ge(h_hi_done, k + 1)
                    tt(h_lo[:, k - 1, :], h_f[:, k - 1, :], h_hi[:, k - 1, :].bitcast(F32), SUB
                       ).then_inc(h_lo_done[0], 1)
            dve.wait_ge(early_in, 16)
            for t in range(TILES):
                n, s = tile_rows(t)[1], t % 2
                v, w = sbf(s, 0, W)[0:n], st[0:n, 4 * s:4 * s + 4]
                dve.wait_ge(evac[s], (2 if s == 0 else 1) + t // 2)
                link(ts(w[:, 3:4], w[:, 0:1], -1.0 / W, None, MUL))
                ts(v, v, w[:, 3:4], None, ADD).then_inc(v_dve, 1)
                dve.wait_ge(v_act, 2 * t + 1)
                link(ts(w[:, 2:3], w[:, 1:2], 1.0 / W, EPS, MUL, ADD))
                dve.reciprocal(w[:, 2:3], w[:, 2:3]).then_inc(v_dve, 1)
                dve.wait_ge(v_act, 2 * t + 2)
                link(stt(v, v, w[:, 2:3], e("alg")[0:n], MUL, MUL))
                out = vn[:, t, :] if t < TILES - 1 else e("vs")[0:NS, :]
                tt(out, v, e("alb")[0:n], ADD).then_inc(v_done, 1)
                if t in (4, 7):
                    s = (t - 1) // 3
                    dve.wait_ge(slab_used, 8 * s + 8)
                    modulation(s, 0 if s == 2 else -1)
            dve.wait_ge(v_done, TILES)
            for ch in range(KW):
                scr = sbf(2, 0, NS * (CD - 1)).rearrange("p (b l) -> p b l", b=NS)
                link(tt(scr, st_d[:, ch], cdw[:, ch, 0:CD - 1].unsqueeze(1).to_broadcast([P, NS, CD - 1]), MUL))
                link(dve.tensor_reduce(dsums[:, ch, :], scr, AXX, ADD))
                link(dve.tensor_reduce(psums[:, ch, :], st_p[:, ch, :, PC + 1 - 2 ** (ch + 1):PC], AXX, ADD))
            link(dve.memset(gl[:, :, 0:CD - 1], 0.0))
            with dve.Fori(0, 4) as i:
                dve.wait_ge(evac[0], evacuated(0) + 1 + i)
                dve.wait_ge(grp, 2 * i + 2)
                tt(three(gl[:, bass.ds(i, 1), CD - 1:].rearrange("p o t -> p (o t)")), pset(1), three(sbf(0)), MUL
                   ).then_inc(evac[1], 1)
            dve.wait_ge(evac[1], evacuated(9))

            def split_y(ch, src):
                link(cp(yh[:, ch, :], src))
                tt(yl[:, ch, :], src, yh[:, ch, :].bitcast(F32), SUB).then_inc(y_done, 1)

            for g in range(KW):
                q, s = Q0["A"] + g, g % 2
                dve.wait_ge(gate_prod, g + 1)
                if g == 0:
                    dve.wait_ge(mod_stored, 32)
                if g:
                    dve.wait_ge(y_done, g)
                tt(sbf(2, 0, LP).rearrange("p (a n t) -> p a n t", a=2, n=4), ps[:, 6:8, :].rearrange("p a (n t) -> p a n t", n=4),
                   abs_[:, g, :].unsqueeze(1).unsqueeze(1).to_broadcast([P, 2, 4, P]), ADD).then_inc(gate_read, 1)
                dve.wait_ge(gate_read, g + 1)
                dve.wait_ge(evac[s], evacuated(q) + 1)
                link(tt(sbf(2, 0, LP), sbf(2, 0, LP), sbf(s, 0, LP), MUL))
                link(tt(sbf(2, LP, NS), smp[:, s, :], sbf(s, LP, NS), MUL))
                split_y(g, sbf(2))
            dve.wait_ge(y_done, KW)

            def tap(ch, l):
                link(stt(dc[:, ch, 0:LP], gl[:, ch, bass.ds(l, LP)], cdw[:, ch, bass.ds(l, 1)], dc[:, ch, 0:LP],
                         MUL, ADD))

            def first_tap(ch):
                link(ts(dc[:, ch, 0:LP], gl[:, ch, 0:LP], cdw[:, ch, 0:1], c("cdb")[:, ch:ch + 1], MUL, ADD))
                link(stt(dc[:, ch, LP:T], gl[:, ch, GLW - NS:GLW], cdw[:, ch, CD - 1:CD], dsums[:, ch, :], MUL, ADD))
                link(ts(dc[:, ch, LP:T], dc[:, ch, LP:T], c("cdb")[:, ch:ch + 1], None, ADD))

            def merge(name, i, j):
                q0 = Q0[name]
                dve.wait_ge(grp, q0 + 2 * i + 2)
                dve.wait_ge(evac[0], evacuated(q0) + i + 1)
                mj = mm[:, bass.ds(j, 1), :].rearrange("p o t -> p (o t)")
                if name == "gA":
                    tt(three(mj), pset(1), three(sbf(0)), MUL).then_inc(evac[1], 1)
                else:
                    tt(three(sbf(1)), pset(1), three(sbf(0)), MUL).then_inc(evac[1], 1)
                    dve.wait_ge(evac[1], evacuated(q0 + 1) + i + 1)
                    if name == "gD":
                        tt(mj, mj, sbf(1), ADD).then_inc(m_ready, 1)
                        dve.wait_ge(m_ready, j + 1)
                    else:
                        link(tt(mj, mj, sbf(1), ADD))

            def merged_lo(j):
                dve.wait_ge(m_hi_done, j + 1)
                one = lambda ap: ap[:, bass.ds(j, 1), :].rearrange("p o t -> p (o t)")
                tt(one(m_lo), one(mm), one(m_hi).bitcast(F32), SUB).then_inc(m_lo_done, 1)

            def gates(name, chunks=(), between=None):
                for ch in chunks:
                    first_tap(ch)
                if name == "gD":
                    merge(name, 0, 0)
                    with dve.Fori(1, KD) as i:
                        merge(name, i, i)
                        merged_lo(i - 1)
                    merged_lo(KD - 1)
                    return
                adds, first = 0 if name == "gA" else 1, 0
                if between:
                    merge(name, 0, 0)
                    between()
                    first = 1
                with dve.Fori(first, KD - 1) as i:
                    steps.loop(i, first, adds + 4 * len(chunks))
                    merge(name, i, i)
                    for k in range(4):
                        for ch in chunks:
                            tap(ch, 1 + 4 * i + k)
                steps.done(KD - 1 - first)
                merge(name, KD - 1, KD - 1)
                for l in (CD - 2, CD - 1):
                    for ch in chunks:
                        tap(ch, l)

            gates("gA", (0, 1))
            link(dve.memset(sbf(1, 0, 2), 0.0))
            for ch in range(KW):
                q = Q0["B"] + 3 * ch
                cx, o = sbf(1, 0, T + 2), sbf(2)
                dve.wait_ge(grp, q + 2)
                dve.wait_ge(evac[q % 2], evacuated(q) + 1)
                s = (q + 1) % 2
                tt(three(cx[:, 2:]), pset(s), three(sbf(0)), MUL).then_inc(evac[s], 1)
                dve.wait_ge(evac[s], evacuated(q + 1) + 1)
                if ch:
                    dve.wait_ge(y_done, KW + ch)
                link(ts(o[:, 0:LP], cx[:, 0:LP], cbw[:, 0, ch:ch + 1], None, MUL))
                link(ts(o[:, LP:T], st_b[:, ch, :, 0], cbw[:, 0, ch:ch + 1], None, MUL))
                link(stt(o[:, 0:LP], cx[:, 1:LP + 1], cbw[:, 1, ch:ch + 1], o[:, 0:LP], MUL, ADD))
                link(stt(o[:, LP:T], st_b[:, ch, :, 1], cbw[:, 1, ch:ch + 1], o[:, LP:T], MUL, ADD))
                link(stt(o, cx[:, 2:], cbw[:, 2, ch:ch + 1], o, MUL, ADD))
                link(cp(tail_b[:, ch, :], cx[:, LP:LP + 10]))
                s = (q + 2) % 2
                dve.wait_ge(grp, q + 3)
                tt(three(o), pset(s), three(o), MUL).then_inc(evac[s], 1)
                dve.wait_ge(evac[s], evacuated(q + 2) + 1)
                split_y(ch, o)
            dve.wait_ge(y_done, 2 * KW)
            dve.engine_nop().then_inc(tails_b, 1)
            gates("gB", (2, 3))
            dve.wait_ge(stored, 16 * 5)
            dve.engine_nop().then_inc(ln_in, 1)
            dve.memset(sbf(0, 0, PC), 0.0).then_inc(gap_zero, 1)
            dve.wait_ge(ln_prod, KW)
            ts(three(ln_row(0)), pset(1), 1.0 / W, None, MUL).then_inc(evac[1], 1)
            X = PC + LP
            for ch in range(KW):
                q, s = Q0["C"] + ch, ch % 2
                x0 = sbf(0, 0, PC + T)
                dve.wait_ge(evac[s], evacuated(q) + 1)
                if ch:
                    dve.wait_ge(y_done, 2 * KW + ch)
                src, width = x0, 1
                for d in range(ch + 1):
                    dst = sbf(1 + d % 2, 0, PC + T)
                    lo = 2 * width - 1
                    link(tt(dst[:, lo:X], src[:, lo:X], src[:, lo - width:X - width], ADD))
                    src, width = dst, 2 * width
                p = sbf(pooled_in(ch), 0, PC + T)
                link(stt(p[:, PC:X], src[:, PC:X], 1.0 / width, x0[:, PC:X], MUL, SUB))
                link(tt(p[:, PC:2 * PC], src[:, PC:2 * PC], inv[:, ch, :], MUL))
                link(tt(p[:, PC:2 * PC], p[:, PC:2 * PC], x0[:, PC:2 * PC], SUB))
                link(tt(p[:, X:X + NS], psums[:, ch, :], x0[:, X:X + NS], ADD))
                link(cp(tail_p[:, ch, :], x0[:, LP:LP + PC + NS]))
                stt(p[:, X:X + NS], p[:, X:X + NS], 1.0 / width, x0[:, X:X + NS], MUL, SUB).then_inc(pooled, 1)
                if ch == 0:
                    dve.wait_ge(evac[1], evacuated(Q0["C"] + 1))
                    for j in range(KW):
                        tt(dc[:, j, :], dc[:, j, :], ln_row(0), SUB).then_inc(ln_mean, 1)
                dve.wait_ge(pool_prod, ch + 1)
                o = sbf(3 - pooled_in(ch))
                ts(three(o), pset(s), c("pscale")[:, ch:ch + 1], None, MUL).then_inc(evac[s], 1)
                dve.wait_ge(evac[s], evacuated(q + 2) - (1 if ch == 1 else 0))
                split_y(ch, o)
                if ch == 1:
                    dve.wait_ge(ln_prod, 2 * KW)
                    ts(three(ln_row(1)), pset(1), 1.0 / W, EPS, MUL, ADD).then_inc(evac[1], 1)
                    dve.wait_ge(evac[1], evacuated(q + 2))
                    dve.reciprocal(ln_row(1), ln_row(1)).then_inc(ln_rstd, 1)
            dve.wait_ge(y_done, 3 * KW)
            dve.engine_nop().then_inc(tails_p, 1)

            def normalise():
                dve.wait_ge(ln_mean, KW)
                dve.wait_ge(ln_rstd, 2)
                for ch in range(KW):
                    tt(dc[:, ch, :], dc[:, ch, :], ln_row(1), MUL).then_inc(ln_norm, 1)

            gates("gC", between=normalise)
            for ch in range(KW):
                dve.wait_ge(ln_y, KW + ch + 1)
                tt(yl[:, ch, :], dc[:, ch, :], yh[:, ch, :].bitcast(F32), SUB).then_inc(y_done, 1)
            gates("gD")
            for k in range(1, KD, 2):
                dve.wait_ge(wo_hi_done, k + 1)
                tt(wo_lo[:, k, :], wo_raw[k % 3], wo_hi[:, k, :].bitcast(F32), SUB).then_inc(wo_lo_done[1], 1)

            dve.wait_ge(rows_in, 16 * 3)
            dve.wait_ge(r3_in, 16)
            M1, M2, MS = (MK[:, j, :].rearrange("p (t e) -> p t e", t=TILES) for j in range(3))
            link(dve.memset(MK[:, :, (TILES - 1) * NE:], 0.0))
            link(dve.memset(slots[:, :], 0))
            link(dve.memset(rt[:, 40:48], -3.0e38))
            two = lambda ap: ap.rearrange("p (a n) -> p a n", a=2)

            def residual(t):
                n, s = tile_rows(t)[1], t % 2
                R = rows if t < TILES - 1 else rows_s
                if t == TILES - 1:
                    dve.wait_ge(rows_s_in, 16 * 3)
                z = rt[0:n, :]
                dve.wait_ge(o_prod, t + 1)
                if t >= 2:
                    dve.wait_ge(h2_out[s], 16 * (t // 2))
                    dve.wait_ge(h2_turned, t - 1)
                tt(two(h2[0:n, s, :]), ps[0:n, 2 * s:2 * s + 2, :], two(R[0:n, 0, :]), MUL).then_inc(o_read, 1)
                dve.wait_ge(o_read, t + 1)
                dve.wait_ge(xt_in[s], 16 * (t // 2 + 1))
                tt(xt[0:n, s, :], h2[0:n, s, :], xt[0:n, s, :], ADD).then_inc(x1_done, 1)
                dve.wait_ge(x1_sq, t + 1)
                dve.wait_ge(x1_done, t + 1)
                link(ts(z[:, 141:142], z[:, 140:141], 1.0 / D, EPS, MUL, ADD))
                dve.reciprocal(z[:, 141:142], z[:, 141:142]).then_inc(x1_var, 1)
                dve.wait_ge(x1_rstd, t + 1)
                link(stt(h2[0:n, s, :], xt[0:n, s, :], z[:, 141:142], R[0:n, 1, :], MUL, MUL))
                tt(h2[0:n, s, :], h2[0:n, s, :], R[0:n, 2, :], ADD).then_inc(h2_done, 1)

            def route(t):
                n = tile_rows(t)[1]
                z = rt[0:n, :]
                zi = ri[0:n, :]
                dve.wait_ge(logit_prod, t + 1)
                tt(z[:, 0:36], ps[0:n, 6, 0:36], r("br")[0:n], ADD).then_inc(logit_read, 1)
                dve.wait_ge(logit_read, t + 1)
                link(cp(z[:, 40:44], z[:, 0:4]))
                link(dve.max(z[:, 48:56], z[:, 40:48]))
                link(dve.max_index(zi[:, 0:8], z[:, 48:56], z[:, 40:48]))
                link(cp(z[:, 56:57], zi[:, 0:1]))
                ts(z[:, 142:143], z[:, 48:49], -1.0, None, MUL).then_inc(gexp_in, 1)
                link(ts(z[:, 116:120], r("iota")[0:n, 0:NG], z[:, 56:57], None, ALU.is_equal))
                link(tt(z[:, 64:96].rearrange("p (g e) -> p g e", g=NG), z[:, 4:36].rearrange("p (g e) -> p g e", g=NG),
                        z[:, 116:120].unsqueeze(2).to_broadcast([n, NG, 8]), MUL))
                link(dve.tensor_reduce(z[:, 96:104], z[:, 64:96].rearrange("p (g e) -> p e g", g=NG), AXX, ADD))
                link(dve.max(z[:, 104:112], z[:, 96:104]))
                link(dve.max_index(zi[:, 8:16], z[:, 104:112], z[:, 96:104]))
                tt(z[:, 144:145], z[:, 105:106], z[:, 104:105], SUB).then_inc(eexp_in, 1)
                link(cp(z[:, 112:114], zi[:, 8:10]))
                link(stt(z[:, 114:116], z[:, 56:57].to_broadcast([n, 2]), 8.0, z[:, 112:114], MUL, ADD))
                link(ts(M1[0:n, t, :], r("iota")[0:n], z[:, 114:115], None, ALU.is_equal))
                link(ts(M2[0:n, t, :], r("iota")[0:n], z[:, 115:116], None, ALU.is_equal))
                tt(MS[0:n, t, :], M1[0:n, t, :], M2[0:n, t, :], ADD).then_inc(mask_done, 1)
                dve.wait_ge(gexp_done, t + 1)
                dve.wait_ge(eexp_done, t + 1)
                link(ts(z[:, 146:147], z[:, 145:146], 1.0, z[:, 143:144], ADD, MUL))
                link(dve.reciprocal(wts[0:n, 0, t:t + 1], z[:, 146:147]))
                link(tt(wts[0:n, 1, t:t + 1], wts[0:n, 0, t:t + 1], z[:, 145:146], MUL))

            for t in range(TILES + 2):
                if t < TILES:
                    residual(t)
                if t > 1:
                    route(t - 2)
            dve.wait_ge(rank_prod, 1)
            nb, end, base, expert = rt[:, 32:64], rt[:, 64:96], rt[:, 96:128], rt[:, BE:BE + 1]
            big = cmp_[:, 0:NE * TILES].rearrange("p (e j) -> p e j", e=NE)
            link(tt(big, ps[:, 7, TILES * NE:(TILES + 1) * NE].unsqueeze(2).to_broadcast([P, NE, TILES]),
                    r("thr").unsqueeze(1).to_broadcast([P, NE, TILES]), ALU.is_gt))
            link(dve.tensor_reduce(nb, big, AXX, ADD))
            link(dve.tensor_tensor_scan(end, ones[:, 0:NE], nb, 0.0, MUL, ADD))
            link(ts(cmp_[:, 0:NE], end, r("tokens")[:, 0:1], None, ALU.is_le))
            link(dve.tensor_reduce(expert, cmp_[:, 0:NE], AXX, ADD))
            ts(expert, expert, float(NE - 1), None, ALU.min).then_inc(expert_in, 1)
            link(tt(base, end, nb, SUB))
            rank = cmp_[:, 0:TILES * NE].rearrange("p (t e) -> p t e", t=TILES)
            link(stt(rank, ps[:, 7, 0:TILES * NE].rearrange("p (t e) -> p t e", t=TILES), 1.0 / P,
                     base.unsqueeze(1).to_broadcast([P, TILES, NE]), MUL, ADD))
            dve.wait_ge(expert_prod, 1)
            cp(block_e[:, 0:BLOCKS], ps[:, 5, 0:BLOCKS]).then_inc(blocks_done, 1)
            M12 = MK[:, 0:2, :].rearrange("p c (t e) -> p c t e", t=TILES)
            link(tt(M12, M12, rank.unsqueeze(1).to_broadcast([P, 2, TILES, NE]), MUL))
            slot, place, block = (rt[:, at:at + 2 * TILES] for at in (128, 0, 32))
            link(dve.tensor_reduce(slot, MK[:, 0:2, :].rearrange("p c (t e) -> p (c t) e", t=TILES), AXX, ADD))
            hot = [P, 2 * TILES, BLOCKS]
            link(tt(in_block[:, :, :], slot.unsqueeze(2).to_broadcast(hot), r("blocks").unsqueeze(1).to_broadcast(hot),
                    ALU.is_ge))
            link(dve.tensor_reduce(block, in_block[:, :, :].bitcast(F32), AXX, ADD))
            link(tt(place, slot, block, SUB))
            link(tt(in_block[:, :, :], block.unsqueeze(2).to_broadcast(hot), r("after").unsqueeze(1).to_broadcast(hot),
                    ALU.is_equal))
            tok = r("tokens").unsqueeze(1).unsqueeze(3).to_broadcast([P, 2, TILES, BLOCKS])
            by_choice = in_block[:, :, :].rearrange("p (c t) b -> p c t b", c=2)
            link(tt(by_choice, by_choice.bitcast(F32), tok, MUL))
            tt(in_place[:, :, :], place.unsqueeze(2).to_broadcast([P, 2 * TILES, P]),
               r("places").unsqueeze(1).to_broadcast([P, 2 * TILES, P]), ALU.is_equal).then_inc(hot_done, 1)
            dve.wait_ge(table_prod, 1)
            cp(table[:, :], ps[:, 6, 0:BLOCKS]).then_inc(table_done, 1)
            link(ts(cmp_[:, 0:NPAIR], r("pair"), end[:, NE - 1:NE], None, ALU.is_lt))
            link(dve.tensor_reduce(rt[:, BE + 1:BE + 2], cmp_[:, 0:NPAIR], AXX, ADD))
            link(ts(block_e[:, BLOCKS:BLOCKS + 1], rt[:, BE + 1:BE + 2], -1.0, None, ADD))
            link(tt(cmp_[:, 0:NPAIR], cmp_[:, 0:NPAIR], r("sign"), MUL))
            link(dve.tensor_reduce(rt[:, BE + 2:BE + 3], cmp_[:, 0:NPAIR], AXX, ADD))
            link(cp(block_e[:, BLOCKS + 1:BLOCKS + 2], rt[:, BE + 2:BE + 3]))
            ts(slots[:, :], slot, float(P), None, MUL).then_inc(blocks_done, 1)

            dve.wait_ge(table_done, 1)
            dve.wait_ge(blocks_done, 2)
            rest = dve.value_load(block_e[0:1, BLOCKS:BLOCKS + 1], min_val=0, max_val=NPAIR - 1)

            def hidden(b, s):
                dve.wait_ge(silu_done, b + 1)
                tt(hm[:, :], ps[:, 2 + s, FE:2 * FE], sg[:, :], MUL).then_inc(hm_done, 1)

            def hidden_columns(b):
                dve.wait_ge(hm_turned, b + 1)
                cp(hmT[:, :, :].rearrange("p f n -> p (f n)"), ps[:, 4, 0:2 * P]).then_inc(hmT_done, 1)

            def copy_y(b, i, s, used=True):
                dve.wait_ge(y_prod, b + 1)
                if used:
                    dve.wait_ge(y_out[s], 16 * i)
                cp(two(yb[:, s, :]), ps[:, 5:7, :]).then_inc(y_copied, 1)

            hidden(0, 0)
            hidden_columns(0)
            hidden(1, 1)
            copy_y(0, 0, 0, False)
            hidden_columns(1)
            hidden(2, 0)
            copy_y(1, 0, 1, False)
            hidden_columns(2)
            hidden(3, 1)
            copy_y(2, 1, 0)
            with dve.Fori(2, NPAIR) as i:
                with dve.If(i < rest + 1):
                    hidden_columns(2 * i - 1)
                    hidden(2 * i, 0)
                    copy_y(2 * i - 1, i - 1, 1)
                    hidden_columns(2 * i)
                    hidden(2 * i + 1, 1)
                    copy_y(2 * i, i, 0)
            hidden_columns(2 * rest + 1)
            copy_y(2 * rest + 1, rest, 1)
            dve.wait_ge(g2_in, 32)

            def combine(t):
                n, j = tile_rows(t)[1], t % YB
                a, b_, x = y12[0:n, t, 0, :], y12[0:n, t, 1, :], x1[0:n, j, :]
                dve.wait_ge(y1_scaled, t + 1)
                dve.wait_ge(y12_in[t], 32)
                link(stt(b_, b_, wts[0:n, 1, t:t + 1], a, MUL, ADD))
                link(tt(b_, b_, g2r[0:n, 0 if t < TILES - 1 else 1, :], MUL))
                dve.wait_ge(x1_in[j], 16 * (t // YB + 1))
                tt(x, x, b_, ADD).then_inc(c_sq_in, 1)

            def last_norm(t):
                n = tile_rows(t)[1]
                total, rstd = (cs[0:n, 2 * (t % 2) + a:2 * (t % 2) + a + 1] for a in range(2))
                dve.wait_ge(c_sq_in, t + 1)
                dve.wait_ge(c_sq, t + 1)
                link(ts(rstd, total, 1.0 / D, EPS, MUL, ADD))
                dve.reciprocal(rstd, rstd).then_inc(c_var, 1)

            for t in range(TILES + 1):
                if t < TILES:
                    combine(t)
                if t:
                    last_norm(t - 1)


def kernel(**inputs):
    import concourse.bacc as bacc
    from concourse.bass_utils import run_bass_kernel_spmd

    a = {k: np.asarray(v) for k, v in inputs.items()}
    f = np.float32

    def chan(x, n):
        x = np.moveaxis(x, -1, 0)
        return np.moveaxis(x.reshape((n, P) + x.shape[1:]), 0, 1)

    def kmaj(w):
        return w.reshape(-1, P, w.shape[1]).transpose(1, 0, 2)

    def rep(x):
        return np.broadcast_to(x.reshape(1, -1), (P, x.size))

    def fill(where, width, parts):
        out = np.zeros((P, width), f)
        for name, x in parts.items():
            lo, hi = where[name]
            out[:, lo:hi] = np.asarray(x).reshape(P, hi - lo)
        return out

    x = np.concatenate([a["x_prompt"][0], a["x_sample"][:, 0]], axis=0)
    cc = np.concatenate([a["c_prompt"], a["c_sample"]], axis=0)
    eye = np.eye(P, dtype=f)
    inv = np.stack([1.0 / np.minimum(np.arange(PC) + 1, 2 ** (g + 1)) for g in range(KW)]).astype(f)
    ws = a["a_ws"][0]
    cT = np.zeros((P, KD, 32), f)
    cT[:, :, 0:NV] = chan(cc, KD)
    mod_const = np.zeros((4, 32, 4, 512), f)
    for s in range(3):
        mod_const[:, 0:NV, s] = a["b_mod"][0].reshape(3, 4, 1, 512)[s]
    mod_const[:, 0:NV, 3] = np.concatenate([a["norm2_g"][0], a["norm1_g"][0]]).reshape(4, 1, 512)
    small = fill(COLS, LOADED, dict(
        ident=eye, ones=np.ones((P, P), f), cT=cT, cbw=np.moveaxis(chan(a["conv_b_w"][0], KW), 2, 1), cdw=chan(a["conv_d_w"][0], KW),
        cdb=chan(a["conv_d_b"][0], KW), dlg=chan(a["d_ln_g"][0], KW), dlb=chan(a["d_ln_b"][0], KW),
        pscale=chan(a["pool_scale"][0], KW), ws00=rep(ws[:, 0, 0]), bs00=rep(a["a_bs"][0, :, 0]),
        st_b=chan(a["state_conv_b"][0], KW), poolw=a["pool_w"][0].transpose(1, 0, 2), inv=rep(inv)))
    early = fill(ECOLS, EARLY_LOADED, dict(
        wv=kmaj(a["w_in"][0][:, W:2 * W]), st_d=chan(a["state_conv_d"][0], KW), st_p=chan(a["state_pool"][0], KW),
        alg=rep(a["a_ln_g"][0]), alb=rep(a["a_ln_b"][0]), aws=ws.transpose(2, 0, 1), abs=rep(a["a_bs"][0])))
    w_in = kmaj(a["w_in"][0])

    def cols(first, n=P):
        return w_in[:, :, first:first + n].reshape(P, -1)

    u, gb, gc, xin, pin, ga, gg = (x_ * W for x_ in (0, 2, 3, 4, 5, 6, 7))
    order = []
    for ch in range(KW):
        order += [gg + ch * P, ga + ch * P]
    order += [u + ch * P for ch in range(KW)]
    for ch in range(KW):
        order += [gc + ch * P, xin + ch * P, gb + ch * P]
    order += [pin + ch * P for ch in range(KW)]
    w_mix = np.stack([cols(o) for o in order]).reshape(-1, 2, P, KD * P).transpose(0, 2, 1, 3).reshape(-1, P, 2 * KD * P)
    w_gate = np.stack([np.concatenate([cols(8 * W + br * D + j * P), kmaj(a["w_branch"][0, br][:, j * P:(j + 1) * P]
                                                                     ).reshape(P, -1)], axis=1)
                       for br in range(4) for j in range(KD)])
    gu = np.concatenate([a["w_eg"][0], a["w_eu"][0]], axis=2).reshape(NE, KD, P, 2 * FE).transpose(0, 2, 1, 3)
    dn = a["w_ed"][0].reshape(NE, 2, P, D).transpose(0, 2, 1, 3)
    routing = np.zeros((P, R3W), f)
    routing[:, slice(*R3["tri"])] = np.triu(np.ones((P, P), f), 1)
    routing[:, slice(*R3["iota"])] = np.arange(NE)
    routing[:, slice(*R3["thr"])] = P * np.arange(9)
    routing[:, slice(*R3["blocks"])] = np.arange(BLOCKS)
    routing[:, slice(*R3["after"])] = np.arange(BLOCKS) + 1
    routing[:, slice(*R3["places"])] = np.arange(P) / P - 1
    tokens = np.arange(P)[:, None] + P * np.arange(TILES)[None, :]
    routing[:, slice(*R3["tokens"])] = np.where(tokens < T, tokens, 0)
    routing[:, slice(*R3["pair"])] = 2 * np.arange(NPAIR)
    routing[:, slice(*R3["sign"])] = (-1.0) ** np.arange(NPAIR)
    routing[:, slice(*R3["br"])] = np.concatenate([a["b_rg"][0], a["b_re"][0]])
    routing[:, slice(*R3["wr"])] = kmaj(np.concatenate([a["w_rg"][0], a["w_re"][0]], axis=1)).reshape(P, -1)
    arrays = dict(
        small=small, xT=chan(x, KD), early=early,
        w_mod=kmaj(a["w_mod"][0]).reshape(P, KD, 3, SLAB).transpose(2, 1, 0, 3).reshape(24, P, SLAB),
        mod_const=mod_const.reshape(P, -1), w_mix=w_mix, w_gate=w_gate,
        w_out=kmaj(a["w_out"][0]), x_tok=x, routing=routing,
        w_exp=np.concatenate([gu.reshape(NE, P, -1), dn.reshape(NE, P, -1)], axis=2), final_g=rep(a["final_g"]),
        state_b=a["state_conv_b"][0], state_p=a["state_pool"][0], state_d=a["state_conv_d"][0])
    arrays = {k: np.ascontiguousarray(v) for k, v in arrays.items()}
    shapes = dict(y=(T, D), v_s=(NS, W), keep_b=(NS, 1, W), keep_p=(NS, PC - 1, W), keep_d=(NS, CD - 2, W),
                  tail_b=(P, KW, 10), tail_p=(P, KW, 23), tail_d=(P, KW, 38))
    nc = bacc.Bacc("TRN2", target_bir_lowering=False, num_devices=1)
    A = {k: nc.dram_tensor(k, v.shape, mybir.dt.from_np(v.dtype), kind="ExternalInput").ap() for k, v in arrays.items()}
    O = {k: nc.dram_tensor("out_" + k, v, F32, kind="ExternalOutput").ap() for k, v in shapes.items()}
    build(nc, A, O)
    r = run_bass_kernel_spmd(nc, [arrays], core_ids=[0]).results[0]
    o = {k: np.asarray(r["out_" + k]) for k in shapes}

    def rows_of(tail):
        return tail.transpose(2, 1, 0).reshape(tail.shape[2], W)

    tb, tp, td = (rows_of(o[k]) for k in ("tail_b", "tail_p", "tail_d"))

    def state(keep, tail):
        return np.concatenate([keep, tail[-NS:, None, :]], axis=1)[None]

    return (o["y"][None, :LP], o["y"][LP:, None], tb[None, None, :2], tp[None, None, :PC], td[None, None, :CD - 1],
            state(o["keep_b"], tb), state(o["keep_p"], tp), state(o["keep_d"], td), o["v_s"][None, :, None])
```
